# Optimizing a Trainium2 kernel written in Bass

```python
import jax, jax.numpy as jnp
from jax import lax
import numpy as np

D_MODEL = 1024
BATCH = 1
SEQ = 512
DEPTH = 1

GRID_W = 64
WIN_H_MAX = 8
WIN_W = 16
ATTN_HEADS = 8
ATTN_HEAD_DIM = 64
ATTN_WIDTH = ATTN_HEADS * ATTN_HEAD_DIM
DN_HEADS = 4
DN_HEAD_DIM = 128
DN_WIDTH = DN_HEADS * DN_HEAD_DIM
DN_CONV = 5
DN_CHUNK = 64
D_MIX = ATTN_WIDTH + DN_WIDTH
IN_COLS = 3 * ATTN_WIDTH + 4 * DN_WIDTH + 4 * DN_HEADS
N_GROUPS = 8
EXPERTS_PER_GROUP = 8
N_EXPERTS = N_GROUPS * EXPERTS_PER_GROUP
TOP_K_IN_GROUP = 2
D_EXPERT = D_MODEL // 4
MOE_BLOCK = 256
EPS = 1e-6


def rms_norm(x, g):
    xf = x.astype(jnp.float32)
    y = xf * lax.rsqrt(jnp.mean(xf * xf, axis=-1, keepdims=True) + EPS)
    return (y * g.astype(jnp.float32)).astype(x.dtype)

def l2_norm(x):
    xf = x.astype(jnp.float32)
    return xf * lax.rsqrt(jnp.sum(xf * xf, axis=-1, keepdims=True) + EPS)

def neighbourhood_attention(q, k, v, rpb):
    b_, s_, h_, dh = q.shape
    rows = s_ // GRID_W
    kh = min(WIN_H_MAX, rows)
    to_grid = lambda t: t.reshape(b_, rows, GRID_W, h_, dh).transpose(1, 0, 3, 2, 4)
    qg, kg, vg = to_grid(q), to_grid(k), to_grid(v)
    cols = jnp.arange(GRID_W)
    col_start = jnp.clip(cols - WIN_W // 2, 0, GRID_W - WIN_W)
    col_idx = col_start[:, None] + jnp.arange(WIN_W)[None, :]
    col_off = col_idx - cols[:, None] + (WIN_W - 1)
    scale = dh ** -0.5

    def row_block(args):
        r, q_row = args
        r0 = jnp.clip(r - kh // 2, 0, rows - kh)
        k_band = lax.dynamic_slice_in_dim(kg, r0, kh, axis=0)
        v_band = lax.dynamic_slice_in_dim(vg, r0, kh, axis=0)
        k_win = k_band[:, :, :, col_idx]
        v_win = v_band[:, :, :, col_idx]
        row_off = r0 + jnp.arange(kh) - r + (WIN_H_MAX - 1)
        bias = rpb[:, row_off[None, :, None], col_off[:, None, :]]
        logits = jnp.einsum('bhqd,rbhqcd->bhqrc', q_row, k_win).astype(jnp.float32) * scale
        logits = logits + bias.astype(jnp.float32)[None]
        p = jax.nn.softmax(logits.reshape(b_, h_, GRID_W, kh * WIN_W), axis=-1)
        p = p.reshape(b_, h_, GRID_W, kh, WIN_W).astype(v.dtype)
        return jnp.einsum('bhqrc,rbhqce->bqhe', p, v_win)

    out = lax.map(row_block, (jnp.arange(rows), qg))
    return out.transpose(1, 0, 2, 3, 4).reshape(b_, s_, h_ * dh)

def gated_delta_rule(q, k, v, g, beta):
    f32 = jnp.float32
    bn, hn, t_, dk = q.shape
    dv = v.shape[-1]
    c = DN_CHUNK
    nc = t_ // c
    q = q.astype(f32).reshape(bn, hn, nc, c, dk)
    k = k.astype(f32).reshape(bn, hn, nc, c, dk)
    v = v.astype(f32).reshape(bn, hn, nc, c, dv)
    beta = beta.astype(f32).reshape(bn, hn, nc, c)
    gc = jnp.cumsum(g.astype(f32).reshape(bn, hn, nc, c), axis=-1)
    incl = jnp.tril(jnp.ones((c, c), bool))
    strict = jnp.tril(jnp.ones((c, c), bool), -1)
    diff = gc[..., :, None] - gc[..., None, :]
    decay = jnp.where(incl, jnp.exp(jnp.where(incl, diff, 0.0)), 0.0)
    kb = k * beta[..., None]
    lower = jnp.where(strict, jnp.einsum('bhnid,bhnjd->bhnij', kb, k) * decay, 0.0)
    a_mat = jnp.eye(c, dtype=f32) + lower
    rhs = jnp.concatenate([v * beta[..., None], kb * jnp.exp(gc)[..., None]], axis=-1)
    sol = lax.linalg.triangular_solve(a_mat, rhs, left_side=True, lower=True, unit_diagonal=True)
    u, w = sol[..., :dv], sol[..., dv:]
    qk = jnp.einsum('bhnid,bhnjd->bhnij', q, k) * decay

    def step(state, inp):
        q_c, k_c, u_c, w_c, g_c, qk_c = inp
        v_new = u_c - jnp.einsum('bhck,bhkv->bhcv', w_c, state)
        o_c = (jnp.einsum('bhck,bhkv->bhcv', q_c * jnp.exp(g_c)[..., None], state)
               + jnp.einsum('bhij,bhjv->bhiv', qk_c, v_new))
        g_last = g_c[..., -1:]
        state = (state * jnp.exp(g_last)[..., None]
                 + jnp.einsum('bhck,bhcv->bhkv', k_c * jnp.exp(g_last - g_c)[..., None], v_new))
        return state, o_c

    xs = tuple(jnp.moveaxis(t, 2, 0) for t in (q, k, u, w, gc, qk))
    state0 = jnp.zeros((bn, hn, dk, dv), f32)
    _, o = lax.scan(step, state0, xs)
    return jnp.moveaxis(o, 0, 2).reshape(bn, hn, t_, dv)

def bidirectional_gated_deltanet(qkv_raw, z, a, b, conv_w, a_log, dt_bias, out_norm_g):
    b_, s_, _ = qkv_raw.shape
    qkv = lax.conv_general_dilated(qkv_raw, conv_w[:, None, :].astype(qkv_raw.dtype),
                                   window_strides=(1,), padding=[(DN_CONV // 2, DN_CONV // 2)],
                                   dimension_numbers=('NWC', 'WIO', 'NWC'),
                                   feature_group_count=3 * DN_WIDTH)
    qkv = jax.nn.silu(qkv)
    q, k, v = jnp.split(qkv.reshape(b_, s_, 3, DN_HEADS, DN_HEAD_DIM), 3, axis=2)
    q = l2_norm(q[:, :, 0]) * (DN_HEAD_DIM ** -0.5)
    k = l2_norm(k[:, :, 0])
    v = v[:, :, 0].astype(jnp.float32)
    g = -jnp.exp(a_log.astype(jnp.float32)) * jax.nn.softplus(a.astype(jnp.float32) + dt_bias.astype(jnp.float32))
    beta = jax.nn.sigmoid(b.astype(jnp.float32))
    bht = lambda t: t.transpose(0, 2, 1, 3)
    both = lambda t: jnp.concatenate([t, jnp.flip(t, axis=2)], axis=1)
    q2, k2, v2 = both(bht(q)), both(bht(k)), both(bht(v))
    g2 = jnp.concatenate([g[:, :, 0].transpose(0, 2, 1), jnp.flip(g[:, :, 1].transpose(0, 2, 1), axis=-1)], axis=1)
    beta2 = jnp.concatenate([beta[:, :, 0].transpose(0, 2, 1), jnp.flip(beta[:, :, 1].transpose(0, 2, 1), axis=-1)], axis=1)
    o2 = gated_delta_rule(q2, k2, v2, g2, beta2)
    o = o2[:, :DN_HEADS] + jnp.flip(o2[:, DN_HEADS:], axis=2)
    o = o.transpose(0, 2, 1, 3)
    zf = z.reshape(b_, s_, DN_HEADS, DN_HEAD_DIM).astype(jnp.float32)
    o = rms_norm(o, out_norm_g) * jax.nn.silu(zf)
    return o.reshape(b_, s_, DN_WIDTH).astype(qkv_raw.dtype)

def hierarchical_moe(h, wg_r, bg_r, we_r, be_r, w_gate, w_up, w_down):
    b_, s_, d_ = h.shape
    n = b_ * s_
    hf = h.reshape(n, d_)
    group_logits = (hf @ wg_r + bg_r).astype(jnp.float32)
    group_prob = jax.nn.softmax(group_logits, axis=-1)
    gsel = jnp.argmax(group_logits, axis=-1)
    gp = jnp.take_along_axis(group_prob, gsel[:, None], axis=-1)
    exp_logits = (hf @ we_r + be_r).astype(jnp.float32).reshape(n, N_GROUPS, EXPERTS_PER_GROUP)
    in_group = jnp.take_along_axis(exp_logits, gsel[:, None, None], axis=1)[:, 0]
    top_val, top_idx = lax.top_k(in_group, TOP_K_IN_GROUP)
    gates = gp * jax.nn.softmax(top_val, axis=-1)
    eid = (gsel[:, None] * EXPERTS_PER_GROUP + top_idx).reshape(-1).astype(jnp.int32)
    gate_flat = gates.reshape(-1)
    tok_flat = jnp.repeat(jnp.arange(n, dtype=jnp.int32), TOP_K_IN_GROUP)
    nk = n * TOP_K_IN_GROUP
    p_rows = -(-nk // MOE_BLOCK) * MOE_BLOCK + N_EXPERTS * MOE_BLOCK
    nb = p_rows // MOE_BLOCK
    order = jnp.argsort(eid)
    e_sorted = eid[order]
    counts = jnp.bincount(eid, length=N_EXPERTS)
    starts = jnp.cumsum(counts) - counts
    padded = -(-counts // MOE_BLOCK) * MOE_BLOCK
    pends = jnp.cumsum(padded)
    pstarts = pends - padded
    dest = pstarts[e_sorted] + (jnp.arange(nk) - starts[e_sorted])
    buf_tok = jnp.full((p_rows,), n, jnp.int32).at[dest].set(tok_flat[order])
    buf_gate = jnp.zeros((p_rows,), jnp.float32).at[dest].set(gate_flat[order])
    block_expert = jnp.clip(jnp.searchsorted(pends, jnp.arange(nb) * MOE_BLOCK, side='right'),
                            0, N_EXPERTS - 1).astype(jnp.int32)
    h_pad = jnp.concatenate([hf, jnp.zeros((1, d_), hf.dtype)], axis=0)

    def expert_block(args):
        tok, e = args
        xb = h_pad[tok]
        hid = jax.nn.silu(xb @ w_gate[e]) * (xb @ w_up[e])
        return hid @ w_down[e]

    out = lax.map(expert_block, (buf_tok.reshape(nb, MOE_BLOCK), block_expert))
    out = (out.reshape(p_rows, d_).astype(jnp.float32) * buf_gate[:, None]).astype(h.dtype)
    y = jnp.zeros((n + 1, d_), h.dtype).at[buf_tok].add(out)[:n]
    return y.reshape(b_, s_, d_)

def hybrid_layer(x, ln1_g, w_in, q_norm_g, k_norm_g, rpb, attn_out_g, conv_w, a_log, dt_bias,
                 dn_out_g, w_out, ln2_g, wg_r, bg_r, we_r, be_r, w_gate, w_up, w_down):
    b_, s_, _ = x.shape
    h = rms_norm(x, ln1_g)
    proj = h @ w_in
    a3 = 3 * ATTN_WIDTH
    aq, ak, av, dqkv, dz, dab = jnp.split(
        proj, [ATTN_WIDTH, 2 * ATTN_WIDTH, a3, a3 + 3 * DN_WIDTH, a3 + 4 * DN_WIDTH], axis=-1)
    hs = lambda t: t.reshape(b_, s_, ATTN_HEADS, ATTN_HEAD_DIM)
    aq = rms_norm(hs(aq), q_norm_g)
    ak = rms_norm(hs(ak), k_norm_g)
    attn = rms_norm(neighbourhood_attention(aq, ak, hs(av), rpb), attn_out_g)
    dab = dab.reshape(b_, s_, 2, 2, DN_HEADS)
    dn = bidirectional_gated_deltanet(dqkv, dz, dab[:, :, 0], dab[:, :, 1], conv_w, a_log,
                                      dt_bias, dn_out_g)
    x = x + jnp.concatenate([attn, dn], axis=-1) @ w_out
    x = x + hierarchical_moe(rms_norm(x, ln2_g), wg_r, bg_r, we_r, be_r, w_gate, w_up, w_down)
    return x

def first_inputs(seed: int = 0) -> dict:
    key = jax.random.key(seed)
    ks = jax.random.split(key, 24)
    f32 = jnp.float32
    nrm = lambda k, shape, s: jax.random.normal(k, shape, f32) * s
    gain = lambda k, shape: 1.0 + 0.01 * jax.random.normal(k, shape, f32)
    L = DEPTH
    dt = jnp.exp(jax.random.uniform(ks[9], (L, 2, DN_HEADS), f32, np.log(1e-3), np.log(1e-1)))
    return {
        'x': nrm(ks[0], (BATCH, SEQ, D_MODEL), 1.0),
        'ln1_g': gain(ks[1], (L, D_MODEL)),
        'w_in': nrm(ks[2], (L, D_MODEL, IN_COLS), D_MODEL ** -0.5),
        'attn_q_norm_g': gain(ks[3], (L, ATTN_HEAD_DIM)),
        'attn_k_norm_g': gain(ks[4], (L, ATTN_HEAD_DIM)),
        'attn_rpb': nrm(ks[5], (L, ATTN_HEADS, 2 * WIN_H_MAX - 1, 2 * WIN_W - 1), 0.1),
        'attn_out_norm_g': gain(ks[6], (L, ATTN_WIDTH)),
        'dn_conv_w': nrm(ks[7], (L, DN_CONV, 3 * DN_WIDTH), DN_CONV ** -0.5),
        'dn_a_log': jnp.log(jax.random.uniform(ks[8], (L, 2, DN_HEADS), f32, 1.0, 16.0)),
        'dn_dt_bias': dt + jnp.log(-jnp.expm1(-dt)),
        'dn_out_norm_g': gain(ks[10], (L, DN_HEAD_DIM)),
        'w_out': nrm(ks[11], (L, D_MIX, D_MODEL), D_MIX ** -0.5),
        'ln2_g': gain(ks[12], (L, D_MODEL)),
        'router_group_w': nrm(ks[13], (L, D_MODEL, N_GROUPS), D_MODEL ** -0.5),
        'router_group_b': nrm(ks[14], (L, N_GROUPS), 0.01),
        'router_expert_w': nrm(ks[15], (L, D_MODEL, N_EXPERTS), D_MODEL ** -0.5),
        'router_expert_b': nrm(ks[16], (L, N_EXPERTS), 0.01),
        'expert_w_gate': nrm(ks[17], (L, N_EXPERTS, D_MODEL, D_EXPERT), D_MODEL ** -0.5),
        'expert_w_up': nrm(ks[18], (L, N_EXPERTS, D_MODEL, D_EXPERT), D_MODEL ** -0.5),
        'expert_w_down': nrm(ks[19], (L, N_EXPERTS, D_EXPERT, D_MODEL), D_EXPERT ** -0.5),
    }

def first_block(x, ln1_g, w_in, attn_q_norm_g, attn_k_norm_g, attn_rpb, attn_out_norm_g, dn_conv_w,
              dn_a_log, dn_dt_bias, dn_out_norm_g, w_out, ln2_g, router_group_w, router_group_b,
              router_expert_w, router_expert_b, expert_w_gate, expert_w_up, expert_w_down):
    for l in range(DEPTH):
        x = hybrid_layer(x, ln1_g[l], w_in[l], attn_q_norm_g[l], attn_k_norm_g[l], attn_rpb[l],
                         attn_out_norm_g[l], dn_conv_w[l], dn_a_log[l], dn_dt_bias[l],
                         dn_out_norm_g[l], w_out[l], ln2_g[l], router_group_w[l], router_group_b[l],
                         router_expert_w[l], router_expert_b[l], expert_w_gate[l], expert_w_up[l],
                         expert_w_down[l])
    return x


ML_HEADS = 4
ML_HEAD_DIM = 256
ML_W = ML_HEADS * ML_HEAD_DIM
ML_CHUNK = 64
SC_W = D_MODEL
CONV_K = 3
SB_HEADS = 16
SB_HEAD_DIM = 64
SB_W = SB_HEADS * SB_HEAD_DIM
SB_BLOCK = 128
N_BRANCH = 3
D_FF = 4 * D_MODEL
SPLIT_SIZES = (ML_W, ML_W, ML_W, ML_W, ML_HEADS, ML_HEADS,
               SC_W, SC_W, SC_W,
               SB_W, SB_W, SB_W,
               D_MODEL, D_MODEL, D_MODEL)
N_IN = sum(SPLIT_SIZES)


def rmsnorm(x, g):
    xf = x.astype(jnp.float32)
    y = xf * lax.rsqrt(jnp.mean(xf * xf, axis=-1, keepdims=True) + EPS)
    return (y * g.astype(jnp.float32)).astype(x.dtype)

def _to_chunks(a, nc, L):
    a = a.reshape((a.shape[0], nc, L) + a.shape[2:])
    return jnp.swapaxes(jnp.moveaxis(a, 1, 0), 2, 3)

def mlstm(q, k, v, i_pre, f_pre):
    B_, S_, H, dh = q.shape
    L = ML_CHUNK
    nc = S_ // L
    f32 = jnp.float32
    qc = _to_chunks(q.astype(f32), nc, L)
    kc = _to_chunks(k.astype(f32) * (dh ** -0.5), nc, L)
    vc = _to_chunks(v.astype(f32), nc, L)
    ic = _to_chunks(i_pre.astype(f32), nc, L)
    lfc = _to_chunks(jax.nn.log_sigmoid(f_pre.astype(f32)), nc, L)
    causal = jnp.tril(jnp.ones((L, L), dtype=bool))

    def step(carry, xs):
        C, n, m = carry
        qb, kb, vb, ib, lfb = xs
        b = jnp.cumsum(lfb, axis=-1)
        dmat = b[..., :, None] - b[..., None, :] + ib[..., None, :]
        dmat = jnp.where(causal, dmat, -jnp.inf)
        inter = b + m[..., None]
        m_t = jnp.maximum(inter, jnp.max(dmat, axis=-1))
        w_intra = jnp.exp(dmat - m_t[..., None])
        a_inter = jnp.exp(inter - m_t)
        s = jnp.einsum('bhtd,bhsd->bhts', qb, kb) * w_intra
        num = (jnp.einsum('bhts,bhsd->bhtd', s, vb)
               + a_inter[..., None] * jnp.einsum('bhvk,bhtk->bhtv', C, qb))
        den = jnp.sum(s, axis=-1) + a_inter * jnp.einsum('bhk,bhtk->bht', n, qb)
        h = num / jnp.maximum(jnp.abs(den), jnp.exp(-m_t))[..., None]
        b_last = b[..., -1]
        g = b_last[..., None] - b + ib
        m_new = jnp.maximum(b_last + m, jnp.max(g, axis=-1))
        decay = jnp.exp(b_last + m - m_new)
        w_state = jnp.exp(g - m_new[..., None])
        C_new = decay[..., None, None] * C + jnp.einsum('bhs,bhsv,bhsk->bhvk', w_state, vb, kb)
        n_new = decay[..., None] * n + jnp.einsum('bhs,bhsk->bhk', w_state, kb)
        return (C_new, n_new, m_new), h

    init = (jnp.zeros((B_, H, dh, dh), f32), jnp.zeros((B_, H, dh), f32), jnp.zeros((B_, H), f32))
    _, hs = lax.scan(step, init, (qc, kc, vc, ic, lfc))
    hs = jnp.moveaxis(jnp.swapaxes(hs, 2, 3), 0, 1)
    return hs.reshape(B_, S_, H, dh)

def short_conv(gate_b, gate_c, u, w):
    z = gate_c * u
    y = lax.conv_general_dilated(
        z, w[:, None, :].astype(z.dtype), window_strides=(1,),
        padding=[(CONV_K - 1, 0)], dimension_numbers=('NWC', 'WIO', 'NWC'),
        feature_group_count=z.shape[-1])
    return gate_b * y

def stick_breaking(q, k, v):
    B_, S_, H, d = q.shape
    nb = S_ // SB_BLOCK
    f32 = jnp.float32
    qf = q.astype(f32) * (d ** -0.5)
    kf = k.astype(f32)
    vf = v.astype(f32)
    q_blocks = jnp.transpose(qf.reshape(B_, nb, SB_BLOCK, H, d), (1, 0, 3, 2, 4))
    starts = jnp.arange(nb, dtype=jnp.int32) * SB_BLOCK
    key_pos = jnp.arange(S_, dtype=jnp.int32)

    def block(args):
        qblk, start = args
        q_pos = start + jnp.arange(SB_BLOCK, dtype=jnp.int32)
        mask = key_pos[None, :] < q_pos[:, None]
        z = jnp.einsum('bhqd,bshd->bhqs', qblk, kf)
        log_beta = jax.nn.log_sigmoid(z)
        log_1m = jnp.where(mask, log_beta - z, 0.0)
        cum = jnp.cumsum(log_1m, axis=-1)
        log_a = log_beta + cum[..., -1:] - cum
        a = jnp.where(mask, jnp.exp(log_a), 0.0)
        return jnp.einsum('bhqs,bshd->bqhd', a, vf)

    out = lax.map(block, (q_blocks, starts))
    return jnp.moveaxis(out, 0, 1).reshape(B_, S_, H * d)

def head_rmsnorm(h, g, n_heads):
    B_, S_, W = h.shape
    hh = h.reshape(B_, S_, n_heads, W // n_heads)
    hh = hh * lax.rsqrt(jnp.mean(hh * hh, axis=-1, keepdims=True) + EPS)
    return hh.reshape(B_, S_, W) * g.astype(jnp.float32)

def second_inputs(seed: int = 0) -> dict:
    key = jax.random.key(seed)
    ks = jax.random.split(key, 16)
    nrm = jax.random.normal
    x = nrm(ks[0], (BATCH, SEQ, D_MODEL), jnp.float32)
    norm_mix_g = 1.0 + 0.02 * nrm(ks[1], (DEPTH, D_MODEL), jnp.float32)
    w_in = nrm(ks[2], (DEPTH, D_MODEL, N_IN), jnp.float32) * D_MODEL ** -0.5
    b_if = jnp.concatenate([
        0.1 * nrm(ks[3], (DEPTH, ML_HEADS), jnp.float32),
        jnp.linspace(3.0, 6.0, ML_HEADS, dtype=jnp.float32)[None, :]
        + 0.1 * nrm(ks[4], (DEPTH, ML_HEADS), jnp.float32)], axis=-1)
    ml_norm_g = 1.0 + 0.02 * nrm(ks[5], (DEPTH, ML_W), jnp.float32)
    conv_w = nrm(ks[6], (DEPTH, CONV_K, SC_W), jnp.float32) * CONV_K ** -0.5
    w_ml_proj = nrm(ks[7], (DEPTH, ML_W, D_MODEL), jnp.float32) * ML_W ** -0.5
    w_sc_proj = nrm(ks[8], (DEPTH, SC_W, D_MODEL), jnp.float32) * SC_W ** -0.5
    w_sb_proj = nrm(ks[9], (DEPTH, SB_W, D_MODEL), jnp.float32) * SB_W ** -0.5
    w_out = nrm(ks[10], (DEPTH, D_MODEL, D_MODEL), jnp.float32) * D_MODEL ** -0.5
    norm_mlp_g = 1.0 + 0.02 * nrm(ks[11], (DEPTH, D_MODEL), jnp.float32)
    w_up = nrm(ks[12], (DEPTH, D_MODEL, D_FF), jnp.float32) * D_MODEL ** -0.5
    w_down = nrm(ks[13], (DEPTH, D_FF, D_MODEL), jnp.float32) * D_FF ** -0.5
    norm_final_g = 1.0 + 0.02 * nrm(ks[14], (D_MODEL,), jnp.float32)
    return {"x": x, "norm_mix_g": norm_mix_g, "w_in": w_in, "b_if": b_if,
            "ml_norm_g": ml_norm_g, "conv_w": conv_w, "w_ml_proj": w_ml_proj,
            "w_sc_proj": w_sc_proj, "w_sb_proj": w_sb_proj, "w_out": w_out,
            "norm_mlp_g": norm_mlp_g, "w_up": w_up, "w_down": w_down,
            "norm_final_g": norm_final_g}

def second_block(x, norm_mix_g, w_in, b_if, ml_norm_g, conv_w, w_ml_proj, w_sc_proj,
              w_sb_proj, w_out, norm_mlp_g, w_up, w_down, norm_final_g):
    B_, S_, _ = x.shape
    offsets = []
    acc = 0
    for sz in SPLIT_SIZES[:-1]:
        acc += sz
        offsets.append(acc)
    for l in range(DEPTH):
        h = rmsnorm(x, norm_mix_g[l])
        proj = h @ w_in[l]
        (ml_q, ml_k, ml_v, ml_o, ml_i, ml_f,
         sc_b, sc_c, sc_u,
         sb_q, sb_k, sb_v,
         g_ml, g_sc, g_sb) = jnp.split(proj, offsets, axis=-1)
        i_pre = ml_i + b_if[l, :ML_HEADS]
        f_pre = ml_f + b_if[l, ML_HEADS:]
        h_tilde = mlstm(ml_q.reshape(B_, S_, ML_HEADS, ML_HEAD_DIM),
                        ml_k.reshape(B_, S_, ML_HEADS, ML_HEAD_DIM),
                        ml_v.reshape(B_, S_, ML_HEADS, ML_HEAD_DIM),
                        i_pre, f_pre).reshape(B_, S_, ML_W)
        y_ml = head_rmsnorm(jax.nn.sigmoid(ml_o.astype(jnp.float32)) * h_tilde,
                            ml_norm_g[l], ML_HEADS).astype(x.dtype)
        y_sc = short_conv(sc_b, sc_c, sc_u, conv_w[l])
        y_sb = stick_breaking(sb_q.reshape(B_, S_, SB_HEADS, SB_HEAD_DIM),
                              sb_k.reshape(B_, S_, SB_HEADS, SB_HEAD_DIM),
                              sb_v.reshape(B_, S_, SB_HEADS, SB_HEAD_DIM)).astype(x.dtype)
        merged = (jax.nn.sigmoid(g_ml) * (y_ml @ w_ml_proj[l])
                  + jax.nn.sigmoid(g_sc) * (y_sc @ w_sc_proj[l])
                  + jax.nn.sigmoid(g_sb) * (y_sb @ w_sb_proj[l]))
        x = x + merged @ w_out[l]
        h2 = rmsnorm(x, norm_mlp_g[l])
        x = x + jnp.square(jax.nn.relu(h2 @ w_up[l])) @ w_down[l]
    return rmsnorm(x, norm_final_g)


def setup_inputs(seed=0):
    out = dict(first_inputs(seed))
    for name, value in second_inputs(seed + 1).items():
        if name != "x":
            out[name + "_2"] = value
    return out


def reference(
    x, ln1_g, w_in, attn_q_norm_g, attn_k_norm_g, attn_rpb, attn_out_norm_g, dn_conv_w,
    dn_a_log, dn_dt_bias, dn_out_norm_g, w_out, ln2_g, router_group_w, router_group_b,
    router_expert_w, router_expert_b, expert_w_gate, expert_w_up, expert_w_down, norm_mix_g_2,
    w_in_2, b_if_2, ml_norm_g_2, conv_w_2, w_ml_proj_2, w_sc_proj_2, w_sb_proj_2, w_out_2,
    norm_mlp_g_2, w_up_2, w_down_2, norm_final_g_2,
):
    x = first_block(
        x, ln1_g, w_in, attn_q_norm_g, attn_k_norm_g, attn_rpb, attn_out_norm_g, dn_conv_w,
        dn_a_log, dn_dt_bias, dn_out_norm_g, w_out, ln2_g, router_group_w, router_group_b,
        router_expert_w, router_expert_b, expert_w_gate, expert_w_up, expert_w_down,
    )
    return second_block(
        x, norm_mix_g_2, w_in_2, b_if_2, ml_norm_g_2, conv_w_2, w_ml_proj_2, w_sc_proj_2,
        w_sb_proj_2, w_out_2, norm_mlp_g_2, w_up_2, w_down_2, norm_final_g_2,
    )


_drawn_inputs = setup_inputs


def setup_inputs(seed=0):
    import zlib

    import numpy as np

    out = dict(_drawn_inputs(seed))
    spreads = {}
    factors = {'ln1_g': 2.751,
     'attn_q_norm_g': 3.846,
     'attn_k_norm_g': 4.367,
     'attn_out_norm_g': 11.996,
     'dn_out_norm_g': 5.118,
     'ln2_g': 3.954,
     'router_group_b': 6.877,
     'router_expert_b': 4.398,
     'ml_norm_g_2': 149.328,
     'norm_mlp_g_2': 10.296,
     'norm_final_g_2': 23.435,
     'conv_w_2': 2.881,
     'w_sc_proj_2': 2.892,
     'w_sb_proj_2': 4.328}
    for name, (base, spread) in spreads.items():
        noise = np.random.default_rng([zlib.crc32(name.encode()), seed]).standard_normal(out[name].shape)
        drawn = base * np.exp(spread * noise) if base else spread * noise
        out[name] = __import__('jax').numpy.asarray(drawn.astype(out[name].dtype))
    for name, factor in factors.items():
        out[name] = (out[name] * factor).astype(out[name].dtype)
    return out
```

```python
from contextlib import ExitStack

import numpy as np

import concourse.bass as bass
from concourse import mybir

F32 = mybir.dt.float32
F32R = mybir.dt.float32r
I32 = mybir.dt.int32
U32 = mybir.dt.uint32
ALU = mybir.AluOpType
ACT = mybir.ActivationFunctionType
X_AXIS = mybir.AxisListType.X

P = 128
T = 512
TT = T // P
D = 1024
KT = D // P
EPS = 1e-6
HA, DA = 8, 64
GW, GH = 64, T // 64
WIN = 16
KROWS = 2 * GH - 2
HD, DD = 4, 128
CONV = 5
NG, EG = 8, 8
NE = NG * EG
DE = 256
SLOTS = 2 * T
BLK = 64
HM, DM = 4, 256
HS, DS = 16, 64
DFF = 4 * D
UNIT = 2048
UC = UNIT // KT
RAW = 4
SPLIT = 2
BIG = 1e30

COLS = {}
_n = 0
for _name, _w in (("ln1", KT), ("qg", 1), ("kg", 1), ("attn_out", 4), ("dn_out", 1), ("ln2", KT), ("ln2_i", KT),
                  ("mix2", KT), ("ml", KT), ("mlp2", KT), ("conv", 12 * CONV), ("conv2", KT * 3)):
    COLS[_name] = _n
    _n += _w
NCOLS = _n
ROWS = {}
_n = 0
for _name, _w in (("a_log", 8), ("dt_bias", 8), ("rb", NG + NE), ("b_if", 8)):
    ROWS[_name] = _n
    _n += _w
NROWS = _n
CONSTS = ("ident", "le", "ge", "lt", "gt", "diag16", "ones", "neg_ge", "neg_ones", "neg_mask")


def constant_matrices():
    p, f = np.arange(P)[:, None], np.arange(P)[None, :]
    m = {"ident": p == f, "le": p <= f, "ge": p >= f, "lt": p < f, "gt": p > f, "diag16": p // 16 == f // 16,
         "ones": p >= 0 * f, "neg_ge": -1.0 * (p >= f), "neg_ones": -1.0 * (p >= 0 * f), "neg_mask": -1e5 * (p >= f)}
    return np.stack([m[k].astype(np.float32) for k in CONSTS], axis=1)


def build(nc, x_in, cols_in, rows_in, consts_in, bias_in, w_in, w_ab, w_out, w_router, w_gate, w_up, w_down,
          w_in2, w_gates2, w_ml, w_sc, w_sb, w_out2, w_up2, w_down2, gfin_in, out, upto=None, blk=BLK):
    stages = []
    BANK = 14
    holders = {}
    for i in range(3 * BANK):
        h = nc.alloc_semaphore(f"local{i}")
        holders[h.num] = h
    first_sem = min(holders)
    banks = [list(range(first_sem + b * BANK, first_sem + (b + 1) * BANK)) for b in range(3)]
    used = {}

    def local(name):
        k = len(stages)
        i = used.get(k, 0)
        used[k] = i + 1
        num = banks[k % 3][i]
        if num in holders:
            nc.release_semaphore(holders[num])
        holders[num] = nc.alloc_semaphore(name, num=num)
        return holders[num]

    def sem(name):
        return nc.alloc_semaphore(name)

    base = 16512
    o_raw = base
    o_hi = o_raw + RAW * UNIT * 4
    o_lo = o_hi + SPLIT * UNIT * 4
    o_x = o_lo + SPLIT * UNIT * 4
    o_a = o_x + TT * D * 4
    o_b = o_a + 2 * KT * T * 4
    o_m = o_b + 2 * KT * T * 4
    o_p = o_m + KT * T * 4
    o_w = o_p + 6144
    end = 229344
    KB = 1024

    def at(name, offset, shape, dt=F32):
        size = int(np.prod(shape[1:])) * 4
        assert offset % 32 == 0 and offset + size <= end, (name, offset, size, end)
        return nc.alloc_sbuf_tensor_at(name, shape, dt, offset=offset)

    raw = at("raw", o_raw, [P, RAW, UNIT])
    whi = at("whi", o_hi, [P, SPLIT, UNIT], F32R)
    wlo = at("wlo", o_lo, [P, SPLIT, UNIT], F32R)
    x = at("x", o_x, [P, TT, D])
    consts = at("consts", o_p, [P, len(CONSTS), P])
    cols = at("cols", o_p + 5120, [P, NCOLS])
    rows = at("rows", o_p + 5120 + 4 * ((NCOLS + 7) // 8 * 8), [P, NROWS])
    assert 5120 + 4 * ((NCOLS + 7) // 8 * 8) + 4 * NROWS <= 6144
    act_hi = at("act_hi", o_a, [P, KT, T], F32R)
    act_lo = at("act_lo", o_a + 16 * KB, [P, KT, T], F32R)
    PS = nc.alloc_psum_tensor("PS", [P, 8, 512], F32)
    const = {n: consts[:, i, :] for i, n in enumerate(CONSTS)}
    ident, ones = const["ident"], const["ones"]

    def col(name, j=0):
        return cols[:, COLS[name] + j:COLS[name] + j + 1]

    def row(name, n):
        return rows[:, ROWS[name]:ROWS[name] + n]

    def middle(ap, n):
        return ap.rearrange("p (a f) -> p a f", a=1).broadcast_to([P, n, ap.shape[-1]])

    raw_full = [sem(f"raw_full{i}") for i in range(RAW)]
    hi_ready, lo_ready = sem("hi_ready"), sem("lo_ready")
    pe_unit = sem("pe_unit")
    evac = sem("evac")
    done = {n: sem(f"{n}_stage") for n in ("pe", "act", "dve", "pool")}
    steps = {n: sem(f"{n}_steps") for n in ("act", "dve", "pool")}
    passed = {n: sem(f"{n}_passed") for n in ("sp", "pe", "pool")}

    def pass_wait(eng, name):
        eng.sem_inc(passed[name], 1)

    s_load = sem("s_load")
    s_small = sem("s_small")
    small_uses = []
    s_out = sem("s_out")

    class Steps:

        def __init__(self, eng, name):
            self.eng, self.sem, self.n = eng, steps[name], 0

        def __call__(self, ins):
            ins.then_inc(self.sem, 1)
            self.n += 1
            return self.n

        def wait(self, n=None):
            self.eng.wait_ge(self.sem, self.n if n is None else n)

        def then(self, ins):
            self(ins)
            self.wait()

    class Stream:
        n = 0
        dense = 0

    def raw_slot(u):
        return u % RAW

    def load_unit(sp, u, u_reg, view, src):
        if isinstance(u_reg, int):
            if u_reg >= RAW:
                sp.wait_ge(lo_ready, u_reg - RAW + 1)
        else:
            sp.wait_ge(lo_ready, u_reg - (RAW - 1))
            pass_wait(sp, "sp")
        dst = raw[:, raw_slot(u), :]
        if view:
            dst = dst.rearrange(view[0], **view[1])
        sp.dma_start(dst, src).then_inc(raw_full[raw_slot(u)], 16)

    TOTAL = {}

    def split_hi(act, u, u_reg, uses):
        if isinstance(u_reg, int):
            if u_reg >= TOTAL["n"]:
                return
            if u_reg >= SPLIT:
                act.wait_ge(pe_unit, u_reg - SPLIT + 1)
        else:
            act.wait_ge(pe_unit, u_reg - (SPLIT - 1))
        act.wait_ge(raw_full[raw_slot(u)], uses * 16)
        nc.scalar.activation(whi[:, u % SPLIT, :], raw[:, raw_slot(u), :], ACT.Copy).then_inc(hi_ready, 1)

    def split_lo(dve, u, u_reg):
        if isinstance(u_reg, int) and u_reg >= TOTAL["n"]:
            return
        dve.wait_ge(hi_ready, u_reg + 1)
        nc.vector.tensor_tensor(wlo[:, u % SPLIT, :], raw[:, raw_slot(u), :], whi[:, u % SPLIT, :].bitcast(F32),
                                ALU.subtract).then_inc(lo_ready, 1)

    def add_stage(**parts):
        stages.append(parts)

    def dense(tag, sources, mode, out_fn, by, acc_hi=act_hi, acc_lo=act_lo, loaded=0):
        u0, e0, n = Stream.n, Stream.dense, len(sources)
        modes = mode if isinstance(mode, list) else [mode] * n
        Stream.n += n
        Stream.dense += n

        def bank(j):
            return 2 * (j % 2)

        def psum_of(j):
            b = PS[:, bank(j):bank(j) + 2, :]
            if modes[j] == "token":
                return b.rearrange("p b (t c) -> p (b t) c", c=UC)
            return b

        def sp_part(sp):
            for j, src in enumerate(sources):
                if j < loaded:
                    continue
                load_unit(sp, u0 + j, u0 + j, ("p (c n) -> p c n", dict(c=KT)), src.rearrange("(c p) n -> p c n", p=P))

        def pe_part(pe):
            for j in range(n):
                u = u0 + j
                pe.wait_ge(lo_ready, u + 1)
                if j >= 2:
                    pe.wait_ge(evac, e0 + j - 1)
                h = whi[:, u % SPLIT, :].rearrange("p (c n) -> p c n", c=KT)
                l = wlo[:, u % SPLIT, :].rearrange("p (c n) -> p c n", c=KT)
                ps = psum_of(j)
                for m in range(2 if modes[j] == "feature" else TT):
                    for c in range(KT):
                        if modes[j] == "feature":
                            s = slice(m * P, m * P + P)
                            three = ((h[:, c, s], acc_hi[:, c, :]), (h[:, c, s], acc_lo[:, c, :]), (l[:, c, s], acc_hi[:, c, :]))
                        else:
                            s = slice(m * P, m * P + P)
                            three = ((acc_hi[:, c, s], h[:, c, :]), (acc_hi[:, c, s], l[:, c, :]), (acc_lo[:, c, s], h[:, c, :]))
                        for k, (a, b) in enumerate(three):
                            last = nc.tensor.matmul(ps[:, m, :], a, b, start=(c == 0 and k == 0), stop=(c == KT - 1 and k == 2))
                last.then_inc(pe_unit, 1)

        def taker(eng, st, j):
            eng.wait_ge(pe_unit, u0 + j + 1)
            out_fn(eng, st, j, psum_of(j)).then_inc(evac, 1)

        def act_part(act, st):
            for j in range(n):
                u = u0 + j
                if by == "act":
                    taker(act, st, j)
                split_hi(act, u + 2, u + 2, (u + 2) // RAW + 1)

        def dve_part(dve, st):
            for j in range(n):
                u = u0 + j
                if by == "dve":
                    taker(dve, st, j)
                split_lo(dve, u + 2, u + 2)

        add_stage(sp=sp_part, pe=pe_part, act=act_part, dve=dve_part)

    def slabs(w, c0, n):
        return [w[:, c0 + UC * j:c0 + UC * (j + 1)] for j in range(n)]

    def transposes(tag, src_tile, gain, n_c=KT, dst_hi=act_hi, dst_lo=act_lo, dst_f32=None, src_step=1):
        s_t = local(f"{tag}_t")

        def pe_part(pe):
            for c in range(n_c):
                for tt in range(TT):
                    last = nc.tensor.transpose(PS[:, c % 8, tt * P:(tt + 1) * P], src_tile(tt, c), ident)
                last.then_inc(s_t, 1)

        s_h = local(f"{tag}_h")

        def act_part(act, st):
            for c in range(n_c):
                act.wait_ge(s_t, c + 1)
                dst = dst_f32[:, c, :] if dst_f32 is not None else dst_hi[:, c, :]
                g = gain(c) if gain else 1.0
                nc.scalar.activation(dst, PS[:, c % 8, :], ACT.Copy, scale=g).then_inc(s_h, 1)

        def dve_part(dve, st):
            if dst_f32 is not None:
                return
            for c in range(n_c):
                dve.wait_ge(s_h, c + 1)
                g = gain(c) if gain else 1.0
                nc.vector.scalar_tensor_tensor(dst_lo[:, c, :], PS[:, c % 8, :], g, dst_hi[:, c, :].bitcast(F32),
                                               ALU.mult, ALU.subtract)
        add_stage(pe=pe_part, act=act_part, dve=dve_part)

    def normalise(tag, src, dst, ss, inv, width, scratch, eps_scale=None, extra=1.0):
        groups = src.shape[1]
        eps_scale = width if eps_scale is None else eps_scale
        s_sq, s_var, s_std = local(f"{tag}_sq"), local(f"{tag}_var"), local(f"{tag}_std")
        few = groups == TT and width == D
        chunks = 4
        gc = groups // chunks
        sc = scratch.rearrange("p (g w) -> p g w", w=width)

        def act_part(act, st):
            for i in range(chunks):
                if few:
                    if i < 2:
                        nc.scalar.activation(sc[:, i, :], src[:, i, :], ACT.Square, accum_out=ss[:, i:i + 1]).then_inc(s_sq, 1)
                else:
                    nc.scalar.activation(sc[:, i * gc:(i + 1) * gc, :], src[:, i * gc:(i + 1) * gc, :], ACT.Square).then_inc(s_sq, 1)
            act.wait_ge(s_var, 1)
            nc.scalar.activation(inv, ss, ACT.Sqrt).then_inc(s_std, 1)

        def dve_part(dve, st):
            if few:
                for i in (2, 3):
                    st(nc.vector.tensor_tensor_reduce(out=sc[:, i, :], in0=src[:, i, :], in1=src[:, i, :], scale=1.0, scalar=0.0,
                                                      op0=ALU.mult, op1=ALU.add, accum_out=ss[:, i:i + 1]))
                dve.wait_ge(s_sq, 2)
            else:
                for i in range(chunks):
                    dve.wait_ge(s_sq, i + 1)
                    st(nc.vector.tensor_reduce(ss[:, i * gc:(i + 1) * gc], sc[:, i * gc:(i + 1) * gc, :], X_AXIS, ALU.add))
            st.wait()
            nc.vector.tensor_scalar(ss, ss, 1.0 / eps_scale, EPS, ALU.mult, ALU.add).then_inc(s_var, 1)
            dve.wait_ge(s_std, 1)
            st.then(nc.vector.reciprocal(inv, inv))
            if extra != 1.0:
                st.then(nc.vector.tensor_scalar(inv, inv, extra, None, ALU.mult))
            if few:
                for i in range(groups):
                    nc.vector.tensor_scalar(dst[:, i, :], src[:, i, :], inv[:, i:i + 1], None, ALU.mult)
            else:
                nc.vector.tensor_tensor(dst, src, inv.rearrange("p (g w) -> p g w", w=1).broadcast_to([P, groups, width]), ALU.mult)
        add_stage(act=act_part, dve=dve_part)

    xv = x_in.rearrange("o (t p) d -> p (o t) d", p=P)
    o_w2 = o_w
    attn_bias = at("attn_bias", o_w + 8 * KB, [P, HA, KROWS, GW])
    xn = at("xn", o_b, [P, TT, D])
    sq_b = at("sq_b", o_m, [P, TT * D])
    stat_a = at("stat_a", o_w, [P, 32])
    stat_b = at("stat_b", o_w + 128, [P, 32])

    def first_sp(sp):
        for tt in range(TT):
            sp.dma_start(x[:, tt, :], xv[:, tt, :]).then_inc(s_load, 16)
        sp.dma_start(consts[:, :, :], consts_in).then_inc(s_load, 16)
        sp.dma_start(cols[:, :], cols_in).then_inc(s_load, 16)
        sp.dma_start(rows[:, :], rows_in).then_inc(s_load, 16)

    s_bias = sem("s_bias")

    def first_pool(pool, st):
        pool.dma_start(attn_bias[:, :, :, :], bias_in).then_inc(s_bias, 16)
        pool.wait_ge(s_load, 7 * 16)

    def first_act(act, st):
        act.wait_ge(s_load, 7 * 16)
        for u in range(SPLIT):
            split_hi(act, u, u, 1)

    def first_dve(dve, st):
        dve.wait_ge(s_load, 7 * 16)
        for u in range(SPLIT):
            split_lo(dve, u, u)

    add_stage(sp=first_sp, act=first_act, dve=first_dve, pe=lambda pe: pe.wait_ge(s_load, 7 * 16), pool=first_pool)
    normalise("n1", x[:, :, :], xn[:, :, :], stat_a[:, 0:TT], stat_b[:, 0:TT], D, sq_b[:, :])
    transposes("t1", lambda tt, c: xn[:, tt, c * P:(c + 1) * P], lambda c: col("ln1", c))

    q_tok = at("q_tok", o_b, [P, TT, 512])
    k_tok = at("k_tok", o_b + 8 * KB, [P, TT, 512])
    v_tok = at("v_tok", o_b + 16 * KB, [P, TT, 512])
    qT = at("qT", o_b + 24 * KB, [P, 4, T])
    kT = at("kT", o_w, [P, 4, T])
    mix = at("mix", o_m, [P, KT, T])
    sq_a = at("sq_a", o_m, [P, 2, TT * 512])
    stat_q = at("stat_q", o_w + 36 * KB, [P, 4, 32])
    qkv = [q_tok, k_tok, v_tok]

    def qkv_out(eng, st, j, ps):
        return nc.scalar.activation(qkv[j // 2][:, :, (j % 2) * UC:(j % 2 + 1) * UC], ps, ACT.Copy)
    dense("qkv", slabs(w_in, 0, 6), "token", qkv_out, "act")

    def heads64(t):
        return t[:, :, :].rearrange("p t (h e) -> p (t h) e", e=DA)
    normalise("nq", heads64(q_tok), heads64(q_tok), stat_q[:, 0, :], stat_q[:, 1, :], DA, sq_a[:, 0, :], extra=DA ** -0.5)
    normalise("nk", heads64(k_tok), heads64(k_tok), stat_q[:, 2, :], stat_q[:, 3, :], DA, sq_a[:, 1, :])
    transposes("tq", lambda tt, c: q_tok[:, tt, c * P:(c + 1) * P], lambda c: col("qg"), n_c=4, dst_f32=qT)
    transposes("tk", lambda tt, c: k_tok[:, tt, c * P:(c + 1) * P], lambda c: col("kg"), n_c=4, dst_f32=kT)

    def attention():
        logit = at("logit", o_w + 36 * KB, [P, 2, 512])
        prob = at("prob", o_b + 8 * KB, [P, 2, 512])
        probT = at("probT", o_b + 12 * KB, [P, 2, TT, P])
        o_tok = at("o_tok", o_b, [P, TT, 512])
        mx = at("mx", o_w + 40 * KB, [P, 32])
        nmx = at("nmx", o_w + 40 * KB + 128, [P, 32])
        rsum = at("rsum", o_w + 40 * KB + 256, [P, 32])
        rinv = at("rinv", o_w + 40 * KB + 384, [P, 32])
        s_logit, s_max, s_exp = local("a_logit"), local("a_max"), local("a_exp")
        s_pt, s_pts, s_av, s_o = local("a_pt"), local("a_pts"), local("a_av"), local("a_o")
        N = HA * TT

        def pe_part(pe):
            def logits(u):
                h, i = divmod(u, TT)
                if u >= 2:
                    pe.wait_ge(s_max, u - 1)
                r = slice((h % 2) * DA, (h % 2) * DA + DA)
                nc.tensor.matmul(PS[:, u % 2, :], qT[r, h // 2, i * P:(i + 1) * P], kT[r, h // 2, :],
                                 start=True, stop=True).then_inc(s_logit, 1)

            def turn(u):
                pe.wait_ge(s_exp, u + 1)
                if u >= 2:
                    pe.wait_ge(s_pts, u - 1)
                for kt in range(TT):
                    last = nc.tensor.transpose(PS[:, 2 + u % 2, kt * P:(kt + 1) * P], prob[:, u % 2, kt * P:(kt + 1) * P], ident)
                last.then_inc(s_pt, 1)

            def values(u):
                h, i = divmod(u, TT)
                pe.wait_ge(s_pts, u + 1)
                if i == 0 and h >= 2:
                    pe.wait_ge(s_o, h - 1)
                for kt in range(TT):
                    last = nc.tensor.matmul(PS[:, 4 + h % 2, i * DA:(i + 1) * DA], probT[:, u % 2, kt, :],
                                            v_tok[:, kt, h * DA:(h + 1) * DA], start=(kt == 0), stop=(kt == TT - 1))
                last.then_inc(s_av, 1)
            logits(0)
            for u in range(N):
                if u + 1 < N:
                    logits(u + 1)
                turn(u)
                if u:
                    values(u - 1)
            values(N - 1)

        def act_part(act, st):
            def copy(u):
                act.wait_ge(s_pt, u + 1)
                if u >= 2:
                    act.wait_ge(s_av, u - 1)
                nc.scalar.activation(probT[:, u % 2, :, :].rearrange("p a b -> p (a b)"), PS[:, 2 + u % 2, :], ACT.Copy).then_inc(s_pts, 1)
            for u in range(N):
                act.wait_ge(s_max, u + 1)
                if u >= 2:
                    act.wait_ge(s_pt, u - 1)
                nc.scalar.activation(prob[:, u % 2, :], logit[:, u % 2, :], ACT.Exp, bias=nmx[:, u:u + 1],
                                     accum_out=rsum[:, u:u + 1]).then_inc(s_exp, 1)
                if u:
                    copy(u - 1)
            copy(N - 1)

        def dve_part(dve, st):
            def head_out(h):
                dve.wait_ge(s_exp, TT * (h + 1))
                st.then(nc.vector.reciprocal(rinv[:, TT * h:TT * (h + 1)], rsum[:, TT * h:TT * (h + 1)]))
                dve.wait_ge(s_av, TT * (h + 1))
                nc.vector.tensor_tensor(o_tok[:, :, h * DA:(h + 1) * DA],
                                        PS[:, 4 + h % 2, 0:TT * DA].rearrange("p (t e) -> p t e", e=DA),
                                        rinv[:, TT * h:TT * (h + 1)].rearrange("p (t e) -> p t e", e=1).broadcast_to([P, TT, DA]),
                                        ALU.mult).then_inc(s_o, 1)
            dve.wait_ge(s_bias, 16)
            for u in range(N):
                h, i = divmod(u, TT)
                dve.wait_ge(s_logit, u + 1)
                if u >= 2:
                    dve.wait_ge(s_exp, u - 1)
                k0 = KROWS // 2 - 1 - 2 * i
                st.then(nc.vector.tensor_tensor_reduce(
                    out=logit[:, u % 2, :], in0=PS[:, u % 2, :],
                    in1=attn_bias[:, h, k0:k0 + GH, :].rearrange("p r c -> p (r c)"),
                    scale=1.0, scalar=-3e38, op0=ALU.add, op1=ALU.max, accum_out=mx[:, u:u + 1]))
                nc.vector.tensor_scalar(nmx[:, u:u + 1], mx[:, u:u + 1], -1.0, None, ALU.mult).then_inc(s_max, 1)
                if u % TT == 2 and u >= 6:
                    head_out((u - 6) // TT)
            head_out(HA - 1)
        add_stage(pe=pe_part, act=act_part, dve=dve_part)
        return o_tok

    o_tok = attention()
    attn_n = at("attn_n", o_b + 8 * KB, [P, TT, 512])
    sq_o = at("sq_o", o_b + 16 * KB, [P, TT * 512])
    normalise("nao", o_tok[:, :, :], attn_n[:, :, :], stat_q[:, 0, 0:TT], stat_q[:, 1, 0:TT], 512, sq_o[:, :])
    transposes("tao", lambda tt, c: attn_n[:, tt, c * P:(c + 1) * P], lambda c: col("attn_out", c), n_c=4, dst_f32=mix)

    conv_in = at("conv_in", o_b, [P, 12, T + CONV - 1])
    z_tok = at("z_tok", o_w, [P, TT, 512])
    ab_w = at("ab_w", o_b + 25 * KB, [P, KT, 16])
    ab_wh = at("ab_wh", o_b + 25 * KB + 512, [P, KT, 16], F32R)
    ab_wl = at("ab_wl", o_b + 26 * KB, [P, KT, 16], F32R)
    o_s = o_w + 36 * KB
    ab = at("ab", o_s, [P, TT, 16])

    def small_product(tag, w_dram, w_f32, w_hi, w_lo, n, dst, bank=6):
        small_uses.append(tag)
        landed = len(small_uses) * 16
        s_wh, s_wl, s_p = local(f"{tag}_wh"), local(f"{tag}_wl"), local(f"{tag}_p")

        def pool_part(pool, st):
            pool.dma_start(w_f32[:, :, :], w_dram.rearrange("(c p) n -> p c n", p=P)).then_inc(s_small, 16)

        def act_part(act, st):
            act.wait_ge(s_small, landed)
            nc.scalar.activation(w_hi[:, :, :], w_f32[:, :, :], ACT.Copy).then_inc(s_wh, 1)

        def dve_part(dve, st):
            dve.wait_ge(s_wh, 1)
            nc.vector.tensor_tensor(w_lo[:, :, :], w_f32[:, :, :], w_hi[:, :, :].bitcast(F32), ALU.subtract).then_inc(s_wl, 1)
            dve.wait_ge(s_p, 1)
            nc.vector.tensor_copy(dst, PS[:, bank, 0:TT * n].rearrange("p (t n) -> p t n", n=n))

        def pe_part(pe):
            pe.wait_ge(s_wl, 1)
            for tt in range(TT):
                s = slice(tt * P, tt * P + P)
                for c in range(KT):
                    for k, (a, b) in enumerate(((act_hi, w_hi), (act_hi, w_lo), (act_lo, w_hi))):
                        last = nc.tensor.matmul(PS[:, bank, tt * n:(tt + 1) * n], a[:, c, s], b[:, c, :],
                                                start=(c == 0 and k == 0), stop=(c == KT - 1 and k == 2))
            last.then_inc(s_p, 1)
        add_stage(pool=pool_part, act=act_part, dve=dve_part, pe=pe_part)

    small_product("ab", w_ab, ab_w, ab_wh, ab_wl, 16, ab[:, :, :])

    def dn_out_fn(eng, st, j, ps):
        if j < 6:
            return nc.scalar.activation(conv_in[:, 2 * j:2 * j + 2, 2:2 + T], ps, ACT.Copy)
        return nc.scalar.activation(z_tok[:, :, (j - 6) * UC:(j - 5) * UC], ps, ACT.Copy)
    dense("dn", slabs(w_in, 3 * HA * DA, 8), ["feature"] * 6 + ["token"] * 2, dn_out_fn, "act")

    g = at("g", o_s + 256, [P, TT, 8])
    beta = at("beta", o_s + 384, [P, TT, 8])
    gc = at("gc", o_s + 512, [P, TT, 8])
    bexp = at("bexp", o_s + 640, [P, TT, 8])
    t_a = at("t_a", o_s + 768, [P, TT, 8])
    t_b = at("t_b", o_s + 896, [P, TT, 8])
    t_c = at("t_c", o_s + 1024, [P, TT, 8])
    glast = at("glast", o_s + 1152, [P, 8, TT])
    eglast = at("eglast", o_s + 1280, [P, 8, TT])
    kdsc = at("kdsc", o_s + 1408, [P, 8, TT])
    stat_d = at("stat_d", o_s + 1536, [P, 4, 16])
    rates = at("rates", o_s + 1792, [P, 8])
    conv_t = at("conv_t", o_w + 32 * KB, [P, 2, T])
    conv_o = at("conv_o", o_w + 8 * KB, [P, 12, T])
    s_pads = local("pads")

    def conv_stage():
        s_c, s_silu, s_g0, s_g1 = local("cv_c"), local("cv_silu"), local("cv_g0"), local("cv_g1")

        def pool_part(pool, st):
            nc.gpsimd.memset(conv_in[:, :, 0:2], 0.0)
            nc.gpsimd.memset(conv_in[:, :, T + 2:T + 4], 0.0).then_inc(s_pads, 1)

        def dve_part(dve, st):
            st.then(nc.vector.tensor_tensor(t_a[:, :, :], ab[:, :, 0:8], middle(row("dt_bias", 8), TT), ALU.add))
            nc.vector.scalar_tensor_tensor(t_b[:, :, :], t_a[:, :, :], -1.0, t_a[:, :, :], ALU.mult, ALU.max).then_inc(s_g0, 1)
            dve.wait_ge(s_pads, 1)
            for j in range(12):
                t = conv_t[:, j % 2, :]
                if j >= 2:
                    dve.wait_ge(s_silu, j - 1)
                st.then(nc.vector.tensor_scalar(t, conv_in[:, j, 0:T], col("conv", j * CONV), None, ALU.mult))
                for w in range(1, CONV):
                    i = nc.vector.scalar_tensor_tensor(t, conv_in[:, j, w:w + T], col("conv", j * CONV + w), t, ALU.mult, ALU.add)
                    if w < CONV - 1:
                        st.then(i)
                i.then_inc(s_c, 1)
            dve.wait_ge(s_g1, 4)
            st.then(nc.vector.scalar_tensor_tensor(t_c[:, :, :], t_a[:, :, :], 0.0, t_c[:, :, :], ALU.max, ALU.add))
            nc.vector.scalar_tensor_tensor(g[:, :, :], t_c[:, :, :], -1.0, middle(rates[:, :], TT), ALU.mult, ALU.mult)

        def act_part(act, st):
            act.wait_ge(s_g0, 1)
            nc.scalar.activation(rates[:, :], row("a_log", 8), ACT.Exp).then_inc(s_g1, 1)
            nc.scalar.activation(t_c[:, :, :], t_b[:, :, :], ACT.Exp, scale=-1.0).then_inc(s_g1, 1)
            act.wait_ge(s_g1, 2)
            nc.scalar.activation(t_c[:, :, :], t_c[:, :, :], ACT.Ln, bias=1.0).then_inc(s_g1, 1)
            nc.scalar.activation(beta[:, :, :], ab[:, :, 8:16], ACT.Sigmoid).then_inc(s_g1, 1)
            for j in range(12):
                act.wait_ge(s_c, j + 1)
                nc.scalar.activation(conv_o[:, j, :], conv_t[:, j % 2, :], ACT.Silu).then_inc(s_silu, 1)
        add_stage(pool=pool_part, dve=dve_part, act=act_part)

    conv_stage()

    dq_tok = at("dq_tok", o_a, [P, TT, 512])
    dk_tok = at("dk_tok", o_a + 8 * KB, [P, TT, 512])
    dv_tok = at("dv_tok", o_a + 16 * KB, [P, TT, 512])

    def to_tokens():
        s_t, s_c = local("dt_t"), local("dt_c")

        def pe_part(pe):
            for kind in range(3):
                for tt in range(TT):
                    u = kind * TT + tt
                    if u >= 8:
                        pe.wait_ge(s_c, u - 7)
                    for h in range(HD):
                        last = nc.tensor.transpose(PS[:, u % 8, h * DD:(h + 1) * DD], conv_o[:, kind * HD + h, tt * P:(tt + 1) * P], ident)
                    last.then_inc(s_t, 1)

        def act_part(act, st):
            for u in range(3 * TT):
                act.wait_ge(s_t, u + 1)
                dst = (dq_tok, dk_tok, dv_tok)[u // TT]
                nc.scalar.activation(dst[:, u % TT, :], PS[:, u % 8, :], ACT.Copy).then_inc(s_c, 1)
        add_stage(pe=pe_part, act=act_part)
    to_tokens()

    def heads128(t):
        return t[:, :, :].rearrange("p t (h e) -> p (t h) e", e=DD)
    sq_d = at("sq_d", o_w + 8 * KB, [P, TT * 512])
    sq_e = at("sq_e", o_w + 16 * KB, [P, TT * 512])
    normalise("ndq", heads128(dq_tok), heads128(dq_tok), stat_d[:, 0, :], stat_d[:, 1, :], DD, sq_d[:, :], eps_scale=1.0, extra=DD ** -0.5)
    normalise("ndk", heads128(dk_tok), heads128(dk_tok), stat_d[:, 2, :], stat_d[:, 3, :], DD, sq_e[:, :], eps_scale=1.0)
    dqT = at("dqT", o_b, [P, HD, T])
    dkT = at("dkT", o_b + 8 * KB, [P, HD, T])
    transposes("tdq", lambda tt, c: dq_tok[:, tt, c * P:(c + 1) * P], None, n_c=4, dst_f32=dqT)
    transposes("tdk", lambda tt, c: dk_tok[:, tt, c * P:(c + 1) * P], None, n_c=4, dst_f32=dkT)
    KK = at("KK", o_w + 8 * KB, [P, HD, T])
    KQ = at("KQ", o_w + 16 * KB, [P, HD, T])
    dn_o = at("dn_o", o_a, [P, TT, 512])

    def grams():
        s_g, s_gc = local("gr_g"), local("gr_gc")

        def pe_part(pe):
            for b, (rhs) in enumerate((dkT, dqT)):
                for h in range(HD):
                    for tt in range(TT):
                        s = slice(tt * P, (tt + 1) * P)
                        if b == 1 and h >= 2 and tt == 0:
                            pe.wait_ge(s_gc, 4 * b + h - 5)
                        bank = (4 * b + h) % 6
                        last = nc.tensor.matmul(PS[:, bank, s], dkT[:, h, s], rhs[:, h, s], start=True, stop=True)
                    last.then_inc(s_g, 1)
            for tt in range(TT):
                nc.tensor.matmul(PS[:, 6, tt * 8:tt * 8 + 4], const["le"], g[:, tt, 0:4], start=True, stop=True)
                last = nc.tensor.matmul(PS[:, 6, tt * 8 + 4:tt * 8 + 8], const["ge"], g[:, tt, 4:8], start=True, stop=True)
            last.then_inc(s_g, 1)

        def act_part(act, st):
            for b in range(8):
                act.wait_ge(s_g, b + 1)
                dst = (KK, KQ)[b // 4]
                nc.scalar.activation(dst[:, b % 4, :], PS[:, b % 6, :], ACT.Copy).then_inc(s_gc, 1)

        def dve_part(dve, st):
            dve.wait_ge(s_g, 9)
            nc.vector.tensor_copy(gc[:, :, :], PS[:, 6, 0:TT * 8].rearrange("p (t n) -> p t n", n=8))
        add_stage(pe=pe_part, act=act_part, dve=dve_part)
    grams()

    def batch_array(name, offset):
        return at(name, offset, [P, 2, TT, P])
    pw = batch_array("pw", o_a + 24 * KB)
    pwT = batch_array("pwT", o_a + 28 * KB)
    yT = batch_array("yT", o_b + 16 * KB)
    lo_m = batch_array("lo_m", o_b + 20 * KB)
    vT = batch_array("vT", o_b + 24 * KB)
    dec = batch_array("dec", o_b + 28 * KB)
    bv = batch_array("bv", o_w + 24 * KB)
    kbe = batch_array("kbe", o_w + 28 * KB)
    kd = batch_array("kd", o_w + 32 * KB)
    qeT = batch_array("qeT", o_m + 8 * KB)
    qkT = batch_array("qkT", o_m + 12 * KB)
    tinvT, y_m, u_m, wT_m = lo_m, dec, pw, pwT
    state = at("state", o_s + 2048, [P, 2, DD])
    vnew = at("vnew", o_s + 3072, [P, 2, DD])

    def flat(t, h):
        return t[:, h, :, :].rearrange("p a b -> p (a b)")

    def bc(ap, n=TT):
        return ap.rearrange("p (a b) -> p a b", b=1).broadcast_to([P, n, P])

    def delta_batch(d, pair):
        tag = f"d{d}{pair}_"
        heads = (2 * pair, 2 * pair + 1)
        incl, strict = (("le", "gt"), ("ge", "lt"))[d]
        s_tg, s_gr, s_raw, s_exp, s_prep, s_pool = (local(tag + n) for n in ("tg", "gr", "raw", "exp", "prep", "pool"))
        s_mm, s_ea, s_ev = local(tag + "mm"), local(tag + "ea"), local(tag + "ev")
        s_vn, s_pv, s_po, s_st, s_oo = (local(tag + n) for n in ("vn", "pv", "po", "st", "oo"))
        last_col = P - 1 if d == 0 else 0
        dh = [4 * d + h for h in heads]
        order = list(range(TT)) if d == 0 else list(range(TT))[::-1]
        I = None
        STEPS = [
            ([("t", pw)], [("dve", yT, "eye-"), ("dve", pwT, "copy")], [0, 0]),
            ([(pwT, pw), (pw, pwT)], [("act", pw, "copy"), ("dve", pwT, "copy")], [0, 1]),
            ([(pw, yT), (pwT, pw), (pw, pwT)], [("dve", yT, "add"), ("act", pw, "copy"), ("dve", pwT, "copy")], [0, 1, 2]),
            ([(pw, yT), (pwT, pw)], [("dve", yT, "add"), ("act", pw, "copy")], [0, 1]),
            ([(pw, yT)], [("dve", yT, "add")], [0]),
            ([(yT, lo_m), (lo_m, yT), ("t", yT)],
             [("act", pw, "copy"), ("dve", pwT, "copy"), ("dve", vT, "eye-"), ("act", y_m, "copy")], [0, 1, 1, 2]),
            ([(pwT, pw), (pw, pwT)], [("act", pw, "copy"), ("dve", pwT, "copy")], [0, 1]),
            ([(pw, vT), (pwT, pw)], [("dve", vT, "add"), ("act", pw, "copy")], [0, 1]),
            ([(pw, vT)], [("dve", vT, "add")], [0]),
            ([(y_m, vT)], [("act", tinvT, "copy")], [0]),
            ([(tinvT, bv), (kbe, tinvT)], [("act", u_m, "copy"), ("dve", wT_m, "copy")], [0, 1]),
        ]
        n_act = [sum(k[0] == "act" for k in s[1]) for s in STEPS]
        n_dve = [sum(k[0] == "dve" for k in s[1]) for s in STEPS]

        def before(counts, s, hb):
            return 2 * sum(counts[:s]) + (hb + 1) * counts[s]

        def pe_part(pe):
            for hb in range(2):
                pe.wait_ge(s_tg, hb + 1)
                nc.tensor.matmul(PS[:, 6 + hb, :], ones, flat(vT, hb), start=True, stop=True).then_inc(s_gr, 1)
            for s, (products, _, _) in enumerate(STEPS):
                for hb in range(2):
                    if s == 0:
                        pe.wait_ge(s_prep, hb + 1)
                    else:
                        pe.wait_ge(s_ea, before(n_act, s - 1, hb)) if before(n_act, s - 1, hb) else None
                        pe.wait_ge(s_ev, before(n_dve, s - 1, hb)) if before(n_dve, s - 1, hb) else None
                    if s == 10:
                        pe.wait_ge(s_pool, 1 + hb)
                    for b, (lhsT, rhs) in enumerate(products):
                        for tt in order:
                            o = PS[:, 3 * hb + b, tt * P:(tt + 1) * P]
                            if isinstance(lhsT, str):
                                last = nc.tensor.transpose(o, rhs[:, hb, tt, :], ident)
                            else:
                                last = nc.tensor.matmul(o, lhsT[:, hb, tt, :], rhs[:, hb, tt, :], start=True, stop=True)
                    last.then_inc(s_mm, 1)
            n_s = len(STEPS) - 1
            for n, tt in enumerate(order):
                for hb in range(2):
                    pe.wait_ge(s_ea, before(n_act, n_s, hb))
                    pe.wait_ge(s_ev, before(n_dve, n_s, hb))
                    if n:
                        pe.wait_ge(s_st, 2 * (n - 1) + hb + 1)
                        nc.tensor.matmul(PS[:, 3 * hb, 0:P], wT_m[:, hb, tt, :], state[:, hb, :], start=True, stop=True).then_inc(s_pv, 1)
                    if n >= 1:
                        pe.wait_ge(s_oo, 2 * (n - 1) + hb + 1)
                if n == 0:
                    pe.wait_ge(s_pool, 4)
                for hb in range(2):
                    pe.wait_ge(s_vn, 2 * n + hb + 1)
                    o = PS[:, 3 * hb + 1, 0:P]
                    if n:
                        nc.tensor.matmul(o, qeT[:, hb, tt, :], state[:, hb, :], start=True, stop=False)
                    nc.tensor.matmul(o, qkT[:, hb, tt, :], vnew[:, hb, :], start=(n == 0), stop=True)
                    nc.tensor.matmul(PS[:, 3 * hb + 2, 0:P], kd[:, hb, tt, :], vnew[:, hb, :], start=True, stop=True).then_inc(s_po, 1)

        def take(eng, st, who, s, hb):
            products, takers, banks = STEPS[s]
            eng.wait_ge(s_mm, 2 * s + hb + 1)
            for (by, dst, how), b in zip(takers, banks):
                if by != who:
                    continue
                ps = PS[:, 3 * hb + b, :]
                out = flat(dst, hb)
                if by == "act":
                    nc.scalar.activation(out, ps, ACT.Copy).then_inc(s_ea, 1)
                elif how == "copy":
                    nc.vector.tensor_copy(out, ps).then_inc(s_ev, 1)
                elif how == "add":
                    nc.vector.tensor_tensor(out, out, ps, ALU.add).then_inc(s_ev, 1)
                else:
                    nc.vector.scalar_tensor_tensor(dst[:, hb, :, :], ps.rearrange("p (a b) -> p a b", b=P), -1.0,
                                                   middle(ident, TT), ALU.mult, ALU.add).then_inc(s_ev, 1)

        def pool_part(pool, st):
            pool.wait_ge(s_exp, 2 * 3 + 2)
            for hb, h in enumerate(heads):
                s = slice(h * DD, (h + 1) * DD)
                nc.gpsimd.tensor_tensor(bv[:, hb, :, :], dv_tok[:, :, s], bc(beta[:, :, dh[hb]]), ALU.mult)
                nc.gpsimd.tensor_tensor(kbe[:, hb, :, :], dk_tok[:, :, s], bc(bexp[:, :, dh[hb]]), ALU.mult).then_inc(s_pool, 1)
            for hb, h in enumerate(heads):
                s = slice(h * DD, (h + 1) * DD)
                nc.gpsimd.tensor_tensor(kd[:, hb, :, :], dk_tok[:, :, s], bc(kdsc[:, dh[hb], :]), ALU.mult).then_inc(s_pool, 1)

        def act_part(act, st):
            for hb in range(2):
                act.wait_ge(s_raw, 2 * hb + 1)
                nc.scalar.activation(flat(dec, hb), flat(dec, hb), ACT.Exp, scale=-1.0).then_inc(s_exp, 1)
                nc.scalar.activation(flat(qkT, hb), flat(qkT, hb), ACT.Exp).then_inc(s_exp, 1)
                nc.scalar.activation(flat(qeT, hb), PS[:, 6 + hb, :], ACT.Exp).then_inc(s_exp, 1)
                if hb == 1:
                    act.wait_ge(s_raw, 4)
                    nc.scalar.activation(eglast[:, dh[0]:dh[1] + 1, :], glast[:, dh[0]:dh[1] + 1, :], ACT.Exp).then_inc(s_exp, 1)
                    nc.scalar.activation(kdsc[:, dh[0]:dh[1] + 1, :], kdsc[:, dh[0]:dh[1] + 1, :], ACT.Exp).then_inc(s_exp, 1)
            for s in range(len(STEPS)):
                for hb in range(2):
                    if n_act[s]:
                        take(act, st, "act", s, hb)

        def dve_part(dve, st):
            nc_v = nc.vector
            for hb in range(2):
                nc_v.tensor_tensor(vT[:, hb, :, :], middle(const[incl], TT), bc(g[:, :, dh[hb]]), ALU.mult).then_inc(s_tg, 1)
            for hb in range(2):
                h = heads[hb]
                dve.wait_ge(s_gr, hb + 1)
                st(nc_v.tensor_copy(glast[:, dh[hb], :], PS[:, 6 + hb, last_col:last_col + (TT - 1) * P + 1:P]))
                for tt in range(TT):
                    ps = PS[:, 6 + hb, tt * P:(tt + 1) * P]
                    nc_v.tensor_scalar(dec[:, hb, tt, :], ps, gc[:, tt, dh[hb]:dh[hb] + 1], 0.0, ALU.subtract, ALU.max)
                    last = nc_v.tensor_scalar(qkT[:, hb, tt, :], ps, gc[:, tt, dh[hb]:dh[hb] + 1], 0.0, ALU.subtract, ALU.min)
                last.then_inc(s_raw, 1)
                st.wait()
                nc_v.tensor_tensor(kdsc[:, dh[hb], :], glast[:, dh[hb], :], gc[:, :, dh[hb]], ALU.subtract).then_inc(s_raw, 1)
            for hb in range(2):
                h = heads[hb]
                dve.wait_ge(s_exp, 3 * hb + 3)
                st.then(nc_v.tensor_tensor(dec[:, hb, :, :], dec[:, hb, :, :], middle(const[strict], TT), ALU.mult))
                for tt in range(TT):
                    st(nc_v.scalar_tensor_tensor(lo_m[:, hb, tt, :], KK[:, h, tt * P:(tt + 1) * P], beta[:, tt, dh[hb]:dh[hb] + 1],
                                                 dec[:, hb, tt, :], ALU.mult, ALU.mult))
                st(nc_v.tensor_tensor(qkT[:, hb, :, :], qkT[:, hb, :, :], middle(const[incl], TT), ALU.mult))
                st(nc_v.tensor_tensor(flat(qeT, hb), flat(qeT, hb), dqT[:, h, :], ALU.mult))
                st.wait()
                st.then(nc_v.tensor_tensor(pw[:, hb, :, :], lo_m[:, hb, :, :], middle(const["diag16"], TT), ALU.mult))
                st(nc_v.tensor_tensor(flat(qkT, hb), flat(qkT, hb), KQ[:, h, :], ALU.mult))
                nc_v.tensor_tensor(flat(lo_m, hb), flat(lo_m, hb), flat(pw, hb), ALU.subtract).then_inc(s_prep, 1)
            for s in range(len(STEPS)):
                for hb in range(2):
                    if n_dve[s]:
                        take(dve, st, "dve", s, hb)
            dve.wait_ge(s_ea, before(n_act, len(STEPS) - 1, 1))
            for n, tt in enumerate(order):
                for hb in range(2):
                    if n:
                        dve.wait_ge(s_pv, 2 * (n - 1) + hb + 1)
                        nc_v.tensor_tensor(vnew[:, hb, :], u_m[:, hb, tt, :], PS[:, 3 * hb, 0:P], ALU.subtract).then_inc(s_vn, 1)
                    else:
                        nc_v.tensor_copy(vnew[:, hb, :], u_m[:, hb, tt, :]).then_inc(s_vn, 1)
                for hb in range(2):
                    h = heads[hb]
                    dve.wait_ge(s_po, 2 * n + hb + 1)
                    if n:
                        nc_v.scalar_tensor_tensor(state[:, hb, :], state[:, hb, :], eglast[:, dh[hb], tt:tt + 1],
                                                  PS[:, 3 * hb + 2, 0:P], ALU.mult, ALU.add).then_inc(s_st, 1)
                    else:
                        nc_v.tensor_copy(state[:, hb, :], PS[:, 3 * hb + 2, 0:P]).then_inc(s_st, 1)
                    dst = dn_o[:, tt, h * DD:(h + 1) * DD]
                    if d == 0:
                        nc_v.tensor_copy(dst, PS[:, 3 * hb + 1, 0:P]).then_inc(s_oo, 1)
                    else:
                        nc_v.tensor_tensor(dst, dst, PS[:, 3 * hb + 1, 0:P], ALU.add).then_inc(s_oo, 1)
        add_stage(pool=pool_part, pe=pe_part, act=act_part, dve=dve_part)

    def beta_exp():
        s_e = local("be_e")

        def act_part(act, st):
            nc.scalar.activation(t_a[:, :, :], gc[:, :, :], ACT.Exp).then_inc(s_e, 1)

        def dve_part(dve, st):
            dve.wait_ge(s_e, 1)
            nc.vector.tensor_tensor(bexp[:, :, :], t_a[:, :, :], beta[:, :, :], ALU.mult)
        add_stage(act=act_part, dve=dve_part)
    beta_exp()
    for d in range(2):
        for pair in range(2):
            delta_batch(d, pair)

    dn_sq = at("dn_sq", o_b, [P, TT * 512])
    dn_z = at("dn_z", o_b + 8 * KB, [P, TT, 512])
    dn_n = at("dn_n", o_b + 16 * KB, [P, TT, 512])
    normalise("ndo", heads128(dn_o), heads128(dn_n), stat_d[:, 0, :], stat_d[:, 1, :], DD, dn_sq[:, :])

    def gate_z():
        s_z = local("gz")

        def act_part(act, st):
            nc.scalar.activation(dn_z[:, :, :], z_tok[:, :, :], ACT.Silu).then_inc(s_z, 1)

        def dve_part(dve, st):
            dve.wait_ge(s_z, 1)
            nc.vector.tensor_tensor(dn_n[:, :, :], dn_n[:, :, :], dn_z[:, :, :], ALU.mult)
        add_stage(act=act_part, dve=dve_part)
    gate_z()
    mix_d = mix[:, 4:8, :]
    transposes("tdn", lambda tt, c: dn_n[:, tt, c * P:(c + 1) * P], lambda c: col("dn_out"), n_c=4, dst_f32=mix_d)

    def split_into(tag, src, hi, lo):
        s_h = local(f"{tag}_h")

        def act_part(act, st):
            for c in range(0, KT, 2):
                nc.scalar.activation(hi[:, c:c + 2, :], src[:, c:c + 2, :], ACT.Copy).then_inc(s_h, 1)

        def dve_part(dve, st):
            for c in range(0, KT, 2):
                dve.wait_ge(s_h, c // 2 + 1)
                nc.vector.tensor_tensor(lo[:, c:c + 2, :], src[:, c:c + 2, :], hi[:, c:c + 2, :].bitcast(F32), ALU.subtract)
        add_stage(act=act_part, dve=dve_part)
    split_into("smix", mix, act_hi, act_lo)

    def residual_out(eng, st, j, ps):
        s = slice((j % 4) * UC, (j % 4 + 1) * UC)
        return nc.vector.tensor_tensor(x[:, :, s], x[:, :, s], ps, ALU.add)
    dense("wout", slabs(w_out, 0, 4), "token", residual_out, "dve")

    xn2 = at("xn2", o_w, [P, TT, D])
    sq_m = at("sq_m", o_b, [P, TT * D])
    o_r = o_w + 36 * KB
    stat_m = at("stat_m", o_r, [P, 2, TT])
    normalise("n2", x[:, :, :], xn2[:, :, :], stat_m[:, 0, :], stat_m[:, 1, :], D, sq_m[:, :])
    transposes("t2", lambda tt, c: xn2[:, tt, c * P:(c + 1) * P], lambda c: col("ln2", c))
    NR = NG + NE
    r_w = at("r_w", o_b, [P, KT, NR])
    r_wh = at("r_wh", o_b + 3 * KB, [P, KT, NR], F32R)
    r_wl = at("r_wl", o_b + 6 * KB, [P, KT, NR], F32R)
    lg = at("lg", o_b + 9 * KB, [P, TT, NR])
    small_product("router", w_router, r_w, r_wh, r_wl, NR, lg[:, :, :])

    KOV = SLOTS // blk
    iota = at("iota", o_w + 32 * KB, [P, SLOTS])
    onehot = at("onehot", o_b + 11 * KB, [P, 2, TT, NE])
    both = at("both", o_b + 13 * KB, [P, TT, NE])
    tmp64 = at("tmp64", o_b + 14 * KB, [P, TT, NE])
    table = at("table", o_b + 15 * KB, [P, KOV, NE])
    pos = at("pos", o_b + 31 * KB, [P, TT, NE])
    r8 = at("r8", o_m, [P, 10, TT, 8])
    r1 = at("r1", o_m + 2 * KB, [P, 12, TT])
    ev = at("ev", o_m + 3 * KB, [P, 8, NE])
    kv = at("kv", o_m + 5 * KB, [P, 4, KOV])
    gates = at("gates", o_r + 64, [P, 2, TT])
    dest = at("dest", o_r + 128, [P, 2, TT])
    dest_u = at("dest_u", o_r + 192, [P, 2, TT], U32)
    start_i = at("start_i", o_r + 256, [P, NE], I32)
    over_i = at("over_i", o_r + 512, [P, 2, KOV], I32)
    n_over = at("n_over", o_r + 1024, [P, 1], I32)

    def route():
        s_i, s_e0, s_e1, s_c, s_p = local("rt_i"), local("rt_e0"), local("rt_e1"), local("rt_c"), local("rt_p")
        lgs, tmp8, cand, oh_g, ing, oh1, oh2, rest, eg = (r8[:, i, :, :] for i in range(9))
        gmax, gsel, gsum, v1, v2, i1, i2, e21, den, gp = (r1[:, i, :] for i in range(10))
        cnt, incl, start, nov, oc, ocx, base_e = (ev[:, i, :] for i in range(7))
        iota8 = iota[:, 0:8]

        def bc8(ap):
            return ap.rearrange("p (t e) -> p t e", e=1).broadcast_to([P, TT, 8])

        def pool_part(pool, st):
            nc.gpsimd.iota(iota[:, :], pattern=[[1, SLOTS]], base=0, channel_multiplier=0,
                           allow_small_or_imprecise_dtypes=True).then_inc(s_i, 1)

        def act_part(act, st):
            act.wait_ge(s_e0, 1)
            nc.scalar.activation(eg, tmp8, ACT.Exp).then_inc(s_e1, 1)
            act.wait_ge(s_e0, 2)
            nc.scalar.activation(e21, den, ACT.Exp).then_inc(s_e1, 1)

        def dve_part(dve, st):
            V = nc.vector

            def first_of(values, top, oh, idx):
                st.then(V.tensor_tensor(cand, values, bc8(top), ALU.is_equal))
                st.then(V.scalar_tensor_tensor(cand, cand, -99.0, middle(iota8, TT), ALU.mult, ALU.add))
                st.then(V.tensor_reduce(idx, cand, X_AXIS, ALU.min))
                st.then(V.tensor_scalar(idx, idx, 99.0, None, ALU.add))
                st.then(V.tensor_tensor(oh, middle(iota8, TT), bc8(idx), ALU.is_equal))

            dve.wait_ge(s_i, 1)
            st.then(V.tensor_tensor(lg[:, :, :], lg[:, :, :], middle(row("rb", NR), TT), ALU.add))
            G = lg[:, :, 0:NG]
            st.then(V.tensor_reduce(gmax, G, X_AXIS, ALU.max))
            V.tensor_tensor(tmp8, G, bc8(gmax), ALU.subtract).then_inc(s_e0, 1)
            first_of(G, gmax, oh_g, gsel)
            t4 = tmp64[:, :, :].rearrange("p t (g e) -> p t g e", e=EG)
            st.then(V.tensor_tensor(t4, lg[:, :, NG:NR].rearrange("p t (g e) -> p t g e", e=EG),
                                    oh_g.rearrange("p t (g e) -> p t g e", e=1).broadcast_to([P, TT, NG, EG]), ALU.mult))
            st.then(V.tensor_reduce(ing, t4.rearrange("p t g e -> p t e g"), X_AXIS, ALU.add))
            st.then(V.tensor_reduce(v1, ing, X_AXIS, ALU.max))
            first_of(ing, v1, oh1, i1)
            st.then(V.scalar_tensor_tensor(rest, oh1, -BIG, ing, ALU.mult, ALU.add))
            st.then(V.tensor_reduce(v2, rest, X_AXIS, ALU.max))
            first_of(rest, v2, oh2, i2)
            V.tensor_tensor(den, v2, v1, ALU.subtract).then_inc(s_e0, 1)
            dve.wait_ge(s_e1, 2)
            st.then(V.tensor_reduce(gsum, eg, X_AXIS, ALU.add))
            st.then(V.scalar_tensor_tensor(den, e21, 1.0, gsum, ALU.add, ALU.mult))
            st.then(V.reciprocal(gates[:, 0, :], den))
            st.then(V.tensor_tensor(gates[:, 1, :], gates[:, 0, :], e21, ALU.mult))
            for k, oh in enumerate((oh1, oh2)):
                st(V.tensor_tensor(onehot[:, k, :, :].rearrange("p t (g e) -> p t g e", e=EG),
                                   oh_g.rearrange("p t (g e) -> p t g e", e=1).broadcast_to([P, TT, NG, EG]),
                                   oh.rearrange("p t (g e) -> p t g e", g=1).broadcast_to([P, TT, NG, EG]), ALU.mult))
            st.wait()
            V.tensor_tensor(both[:, :, :], onehot[:, 0, :, :], onehot[:, 1, :, :], ALU.add).then_inc(s_c, 1)
            dve.wait_ge(s_p, 1)
            st.then(V.tensor_copy(cnt, PS[:, 6, 0:NE]))
            st.then(V.memset(base_e, 0.0))
            st.then(V.tensor_tensor_scan(incl, cnt, base_e, 0.0, ALU.add, ALU.add))
            st.then(V.tensor_tensor(start, incl, cnt, ALU.subtract))
            st(V.tensor_copy(start_i[:, :], start))
            st.then(V.tensor_tensor(pos[:, :, :], PS[:, 7, 0:TT * NE].rearrange("p (t e) -> p t e", e=NE), middle(start, TT), ALU.add))
            for k in range(2):
                st.then(V.tensor_tensor(tmp64[:, :, :], pos[:, :, :], onehot[:, k, :, :], ALU.mult))
                st.then(V.tensor_reduce(dest[:, k, :], tmp64[:, :, :], X_AXIS, ALU.add))
            st(V.tensor_copy(dest_u[:, :, :], dest[:, :, :]))
            st.then(V.tensor_scalar(nov, cnt, float(blk), None, ALU.is_gt))
            for m in range(2, T // blk):
                st.then(V.scalar_tensor_tensor(nov, cnt, float(m * blk), nov, ALU.is_gt, ALU.add))
            st.then(V.tensor_tensor_scan(oc, nov, base_e, 0.0, ALU.add, ALU.add))
            st(V.tensor_copy(n_over[:, :], oc[:, NE - 1:NE]))
            st.then(V.tensor_tensor(ocx, oc, nov, ALU.subtract))
            st.then(V.scalar_tensor_tensor(base_e, ocx, float(blk), incl, ALU.mult, ALU.add))
            kk = iota[:, 0:KOV].rearrange("p (k e) -> p k e", e=1).broadcast_to([P, KOV, NE])
            st.then(V.tensor_tensor(table[:, :, :], middle(oc, KOV), kk, ALU.is_le))
            st.then(V.tensor_reduce(kv[:, 0, :], table[:, :, :], X_AXIS, ALU.add))
            st.then(V.tensor_scalar(kv[:, 0, :], kv[:, 0, :], float(NE - 1), None, ALU.min))
            st.then(V.tensor_tensor(table[:, :, :], middle(iota[:, 0:NE], KOV),
                                    kv[:, 0, :].rearrange("p (k e) -> p k e", e=1).broadcast_to([P, KOV, NE]), ALU.is_equal))
            st.then(V.tensor_tensor(table[:, :, :], table[:, :, :], middle(base_e, KOV), ALU.mult))
            st.then(V.tensor_reduce(kv[:, 1, :], table[:, :, :], X_AXIS, ALU.add))
            st.then(V.scalar_tensor_tensor(kv[:, 2, :], iota[:, 0:KOV], -float(blk), kv[:, 1, :], ALU.mult, ALU.add))
            st.then(V.tensor_scalar(kv[:, 2, :], kv[:, 2, :], -float(blk), 0.0, ALU.add, ALU.max))
            st(V.tensor_copy(over_i[:, 0, :], kv[:, 0, :]))
            V.tensor_copy(over_i[:, 1, :], kv[:, 2, :])

        def pe_part(pe):
            pe.wait_ge(s_c, 1)
            for tt in range(TT):
                o = PS[:, 7, tt * NE:(tt + 1) * NE]
                for t2 in range(tt):
                    nc.tensor.matmul(o, ones, both[:, t2, :], start=(t2 == 0), stop=False)
                nc.tensor.matmul(o, const["lt"], both[:, tt, :], start=(tt == 0), stop=True)
            for tt in range(TT):
                last = nc.tensor.matmul(PS[:, 6, 0:NE], ones, both[:, tt, :], start=(tt == 0), stop=(tt == TT - 1))
            last.then_inc(s_p, 1)
        add_stage(pool=pool_part, act=act_part, dve=dve_part, pe=pe_part)
    route()

    tok_hi = at("tok_hi", o_a, [P, TT, D], F32R)
    tok_lo = at("tok_lo", o_a + 16 * KB, [P, TT, D], F32R)
    sel = at("sel", o_w + 16 * KB, [P, TT, SLOTS], F32R)
    sel_t = at("sel_t", o_b, [P, 2, SLOTS])
    sorted_h = at("sorted_h", o_b, [P, KT, SLOTS + blk])

    def select():
        s_h = local("sl_h")

        def act_part(act, st):
            for tt in range(TT):
                nc.scalar.activation(tok_hi[:, tt, :], xn2[:, tt, :], ACT.Copy).then_inc(s_h, 1)

        def dve_part(dve, st):
            for tt in range(TT):
                st.then(nc.vector.tensor_scalar(sel_t[:, tt % 2, :], iota[:, :], dest[:, 0, tt:tt + 1], None, ALU.is_equal))
                st(nc.vector.scalar_tensor_tensor(sel[:, tt, :], iota[:, :], dest[:, 1, tt:tt + 1], sel_t[:, tt % 2, :],
                                                  ALU.is_equal, ALU.add))
            for tt in range(TT):
                dve.wait_ge(s_h, tt + 1)
                nc.vector.tensor_tensor(tok_lo[:, tt, :], xn2[:, tt, :], tok_hi[:, tt, :].bitcast(F32), ALU.subtract)
        add_stage(act=act_part, dve=dve_part)
    select()

    def sort_tokens():
        s_b, s_e = local("so_b"), local("so_e")

        def pool_part(pool, st):
            nc.gpsimd.memset(sorted_h[:, :, SLOTS:SLOTS + blk], 0.0)

        def pe_part(pe):
            for u in range(2 * KT):
                c, half = divmod(u, 2)
                if u >= 8:
                    pe.wait_ge(s_e, u - 7)
                for tt in range(TT):
                    for k, src in enumerate((tok_hi, tok_lo)):
                        last = nc.tensor.matmul(PS[:, u % 8, :], src[:, tt, c:D:KT], sel[:, tt, half * 512:(half + 1) * 512],
                                                start=(tt == 0 and k == 0), stop=(tt == TT - 1 and k == 1))
                last.then_inc(s_b, 1)

        def act_part(act, st):
            for u in range(2 * KT):
                c, half = divmod(u, 2)
                act.wait_ge(s_b, u + 1)
                nc.scalar.activation(sorted_h[:, c, half * 512:(half + 1) * 512], PS[:, u % 8, :], ACT.Copy,
                                     scale=col("ln2_i", c)).then_inc(s_e, 1)
        add_stage(pool=pool_part, pe=pe_part, act=act_part)
    sort_tokens()

    st_hi = at("st_hi", o_a, [P, 2, KT, P], F32R)
    st_lo = at("st_lo", o_a + 8 * KB, [P, 2, KT, P], F32R)
    y_sb = at("y_sb", o_a + 16 * KB, [P, 4, D])
    g_sb = at("g_sb", o_w, [P, 2, DE])
    hid = at("hid", o_w + 2 * KB, [P, 2, DE])
    hT_hi = at("hT_hi", o_w + 4 * KB, [P, 2, 2, P], F32R)
    hT_lo = at("hT_lo", o_w + 6 * KB, [P, 2, 2, P], F32R)
    y_sorted = nc.dram_tensor("y_sorted", [SLOTS + blk, D], F32).ap()
    y_store = [sem(f"y_store{i}") for i in range(4)]
    s_y2 = sem("y_over")
    BODY = 4

    def experts():
        u0 = Stream.n
        Stream.n += 3 * NE
        s_z, s_stat, s_silu, s_hid, s_tr, s_hh, s_hl = (local("ex_" + n) for n in ("z", "stat", "silu", "hid", "tr", "hh", "hl"))
        s_ya, s_yd = sem("ex_ya"), sem("ex_yd")
        s_cp = local("ex_cp")

        class At:

            def __init__(self, q, p):
                self.p, self.q = p, q
                self.e = q * BODY + p
                self.first = isinstance(q, int)

            def unit(self, k):
                if self.first:
                    u = u0 + 3 * self.e - 1 + k if self.e else u0 + k
                    u = min(u, u0 + 3 * NE - 1)
                    return u, u, u // RAW + 1
                s = u0 + 3 * self.p - 1 + k
                return s, self.q * (3 * BODY) + s, self.q * 3 + s // RAW + 1

            def ahead(self, k):
                if self.first:
                    u = self.unit(k)[0] + 2
                    return u, u, u // RAW + 1
                s = u0 + 3 * self.p - 1 + k + 2
                return s, self.q * (3 * BODY) + s, self.q * 3 + s // RAW + 1

            def had(self, n):
                return not self.first or self.e >= n

        def each(eng, body):
            for e in range(2 * BODY):
                body(At(e // BODY, e % BODY))
            with eng.Fori(2, NE // BODY) as q:
                for p in range(BODY):
                    body(At(q, p))

        last = At(NE // BODY, 0)

        def sp_part(sp):
            def store(e, slot, before, filled):
                sp.wait_ge(s_ya, e + 1)
                sp.wait_ge(s_yd, e + 1)
                pass_wait(sp, "sp")
                if filled is not None:
                    sp.wait_ge(y_store[before], filled)
                    pass_wait(sp, "sp")
                n = sp.value_load(start_i[0:1, bass.ds(e, 1)], min_val=0, max_val=SLOTS)
                sp.dma_start(y_sorted[bass.ds(n, blk), :], y_sb[0:blk, slot, :]).then_inc(y_store[slot], 16)

            def body(a):
                for k, w in enumerate((w_gate, w_up)):
                    s, u, _ = a.unit(k)
                    load_unit(sp, s, u, None, w[a.e].rearrange("(p c) n -> p (c n)", c=KT) if a.first
                              else w[bass.ds(a.e, 1)].rearrange("o (p c) n -> p (o c n)", c=KT))
                if a.had(1):
                    s, u, _ = a.unit(2)
                    load_unit(sp, s, u, ("p (j n) -> p j n", dict(j=2)), w_down[a.e - 1].rearrange("(j p) n -> p j n", p=P) if a.first
                              else w_down[bass.ds(a.e - 1, 1)].rearrange("o (j p) n -> p (o j) n", p=P))
                if a.had(4):
                    filled = (a.q if a.p else a.q - 1) * 16
                    store(a.e - 4, a.p, (a.p - 1) % 4, None if a.first and a.e == 4 else filled)
            each(sp, body)
            s, u, _ = last.unit(2)
            load_unit(sp, s, u, ("p (j n) -> p j n", dict(j=2)), w_down[NE - 1].rearrange("(j p) n -> p j n", p=P))
            nxt = iter(slabs(w_in2, 0, RAW))
            for e in range(NE - 4, NE):
                store(e, e % 4, (e - 1) % 4, (e - 1) // 4 * 16 + 16)
                for _ in range({0: 2, 2: 2}.get(e % 4, 0)):
                    s += 1
                    load_unit(sp, s, s, ("p (c n) -> p c n", dict(c=KT)), next(nxt).rearrange("(c p) n -> p c n", p=P))

        def pool_part(pool, st):
            nc.gpsimd.memset(st_hi[:, :, :, blk:P].bitcast(F32), 0.0)
            nc.gpsimd.memset(st_lo[:, :, :, blk:P].bitcast(F32), 0.0).then_inc(s_z, 1)

            def body(a):
                if a.had(2):
                    pool.wait_ge(pe_unit, a.e * 3 + (u0 - 5) if not a.first or a.e > 2 else u0 + 2)
                b = a.p % 2
                n = pool.value_load(start_i[0:1, bass.ds(a.e, 1)], min_val=0, max_val=SLOTS)
                src = sorted_h[:, :, bass.ds(n, blk)]
                nc.gpsimd.tensor_copy(st_hi[:, b, :, 0:blk], src).then_inc(s_cp, 1)
                pool.wait_ge(s_cp, a.e + 1)
                pass_wait(pool, "pool")
                nc.gpsimd.tensor_tensor(st_lo[:, b, :, 0:blk], src, st_hi[:, b, :, 0:blk].bitcast(F32), ALU.subtract).then_inc(s_stat, 1)
            each(pool, body)

        def turn(pe, e, b, had_one):
            pe.wait_ge(s_hid, e + 1)
            if had_one:
                pe.wait_ge(s_hl, e)
            for j in range(2):
                i = nc.tensor.transpose(PS[:, 2, j * P:(j + 1) * P], hid[:, b, j * P:(j + 1) * P], ident)
            i.then_inc(s_tr, 1)

        def down(pe, e, b, s, u, had_two):
            pe.wait_ge(lo_ready, u + 1)
            pe.wait_ge(s_hl, e + 1)
            if had_two:
                pe.wait_ge(s_ya, e - 1)
                pe.wait_ge(s_yd, e - 1)
            h = whi[:, s % SPLIT, :].rearrange("p (j n) -> p j n", j=2)
            l = wlo[:, s % SPLIT, :].rearrange("p (j n) -> p j n", j=2)
            for half in range(2):
                c = slice(half * 512, (half + 1) * 512)
                for j in range(2):
                    for k, (x_, w_) in enumerate(((hT_hi, h), (hT_hi, l), (hT_lo, h))):
                        i = nc.tensor.matmul(PS[:, 3 + 2 * b + half, :], x_[:, b, j, :], w_[:, j, c],
                                             start=(j == 0 and k == 0), stop=(j == 1 and k == 2))
            i.then_inc(pe_unit, 1)

        def pe_part(pe):
            pe.wait_ge(s_z, 1)

            def product(a, k):
                s, u, _ = a.unit(k)
                b = a.p % 2
                pe.wait_ge(lo_ready, u + 1)
                h = whi[:, s % SPLIT, :].rearrange("p (c n) -> p c n", c=KT)
                l = wlo[:, s % SPLIT, :].rearrange("p (c n) -> p c n", c=KT)
                for c in range(KT):
                    for m, (x_, w_) in enumerate(((st_hi, h), (st_hi, l), (st_lo, h))):
                        i = nc.tensor.matmul(PS[:, b, k * DE:(k + 1) * DE], x_[:, b, c, :], w_[:, c, :],
                                             start=(c == 0 and m == 0), stop=(c == KT - 1 and m == 2))
                i.then_inc(pe_unit, 1)

            def body(a):
                pe.wait_ge(s_stat, a.e + 1)
                if a.had(2):
                    pe.wait_ge(s_hid, a.e - 1)
                product(a, 0)
                if a.had(1):
                    turn(pe, a.e - 1, (a.p - 1) % 2, a.had(2))
                product(a, 1)
                if a.had(1):
                    s, u, _ = a.unit(2)
                    down(pe, a.e - 1, (a.p - 1) % 2, s, u, a.had(3))
            each(pe, body)
            turn(pe, NE - 1, 1, True)
            s, u, _ = last.unit(2)
            down(pe, NE - 1, 1, s, u, True)

        def act_hid(act, a):
            b = (a.p - 1) % 2
            act.wait_ge(s_tr, a.e)
            if a.had(3):
                act.wait_ge(pe_unit, a.e * 3 + (u0 - 4))
            nc.scalar.activation(hT_hi[:, b, :, :].rearrange("p j n -> p (j n)"), PS[:, 2, 0:DE], ACT.Copy).then_inc(s_hh, 1)

        def y_out(eng, a, half, s_y):
            b, slot = (a.p - 1) % 2, (a.p - 1) % 4
            eng.wait_ge(pe_unit, a.unit(2)[1] + 1)
            if a.had(5):
                eng.wait_ge(y_store[slot], (a.q - (1 if a.p == 0 else 0)) * 16)
            c = slice(half * 512, (half + 1) * 512)
            src, dst = PS[0:blk, 3 + 2 * b + half, :], y_sb[0:blk, slot, c]
            (nc.scalar.activation(dst, src, ACT.Copy) if half == 0 else nc.vector.tensor_copy(dst, src)).then_inc(s_y, 1)

        def act_part(act, st):
            def body(a):
                if a.had(1):
                    act_hid(act, a)
                split_hi(act, *a.ahead(0))
                act.wait_ge(pe_unit, a.unit(1)[1] + 1)
                if a.had(2):
                    act.wait_ge(s_hid, a.e - 1)
                b = a.p % 2
                nc.scalar.activation(g_sb[:, b, :], PS[:, b, 0:DE], ACT.Silu).then_inc(s_silu, 1)
                split_hi(act, *a.ahead(1))
                if a.had(1):
                    y_out(act, a, 0, s_ya)
                    split_hi(act, *a.ahead(2))
            each(act, body)
            act_hid(act, last)
            y_out(act, last, 0, s_ya)
            split_hi(act, *last.ahead(2))

        def dve_hid(dve, a):
            b = (a.p - 1) % 2
            dve.wait_ge(s_hh, a.e)
            nc.vector.tensor_tensor(hT_lo[:, b, :, :].rearrange("p j n -> p (j n)"), PS[:, 2, 0:DE],
                                    hT_hi[:, b, :, :].rearrange("p j n -> p (j n)").bitcast(F32), ALU.subtract).then_inc(s_hl, 1)

        def dve_part(dve, st):
            def body(a):
                if a.had(1):
                    dve_hid(dve, a)
                split_lo(dve, *a.ahead(0)[:2])
                dve.wait_ge(s_silu, a.e + 1)
                dve.wait_ge(pe_unit, a.unit(1)[1] + 1)
                if a.had(2):
                    dve.wait_ge(s_tr, a.e - 1)
                b = a.p % 2
                nc.vector.tensor_tensor(hid[:, b, :], g_sb[:, b, :], PS[:, b, DE:2 * DE], ALU.mult).then_inc(s_hid, 1)
                split_lo(dve, *a.ahead(1)[:2])
                if a.had(1):
                    y_out(dve, a, 1, s_yd)
                    split_lo(dve, *a.ahead(2)[:2])
            each(dve, body)
            dve_hid(dve, last)
            y_out(dve, last, 1, s_yd)
            split_lo(dve, *last.ahead(2)[:2])
        add_stage(sp=sp_part, pool=pool_part, pe=pe_part, act=act_part, dve=dve_part)
    experts()

    ov_w = at("ov_w", o_w + 8 * KB, [P, 3, UNIT])
    ov_st = at("ov_st", o_a, [P, KT, blk])
    ov_g = at("ov_g", o_w, [P, DE])
    ov_h = at("ov_h", o_w + KB, [P, DE])
    ov_hT = at("ov_hT", o_w + 2 * KB, [P, 2, P])
    ov_y = at("ov_y", o_a + 16 * KB, [P, D])

    def extra_blocks():
        s_w, s_st, s_gu, s_si, s_hi2, s_tr, s_ht, s_dn, s_y, s_yo = (
            sem("ov_" + n) for n in ("w", "st", "gu", "si", "hid", "tr", "ht", "dn", "y", "yo"))

        def each(eng, body):
            n = eng.value_load(n_over[0:1, 0:1], min_val=0, max_val=KOV)
            with eng.If(n > 0):
                with eng.Fori(0, n) as k:
                    body(k)
                eng.drain()
            eng.drain()

        def sp_part(sp):
            for i in range(4):
                sp.wait_ge(y_store[i], NE // 4 * 16)
            for name in ("pe", "act", "dve", "pool"):
                sp.wait_ge(done[name], stage_no)

            def body(k):
                e = sp.value_load(over_i[0:1, 0, bass.ds(k, 1)], min_val=0, max_val=NE - 1)
                sp.wait_ge(s_dn, k + 1)
                pass_wait(sp, "sp")
                for i, w in enumerate((w_gate, w_up)):
                    sp.dma_start(ov_w[:, i, :], w[bass.ds(e, 1)].rearrange("o (p c) n -> p (o c n)", c=KT)).then_inc(s_w, 16)
                sp.dma_start(ov_w[:, 2, :].rearrange("p (j n) -> p j n", j=2),
                             w_down[bass.ds(e, 1)].rearrange("o (j p) n -> p (o j) n", p=P)).then_inc(s_w, 16)
                sp.wait_ge(s_y, k + 1)
                pass_wait(sp, "sp")
                n = sp.value_load(over_i[0:1, 1, bass.ds(k, 1)], min_val=0, max_val=SLOTS)
                sp.dma_start(y_sorted[bass.ds(n, blk), :], ov_y[0:blk, :]).then_inc(s_y2, 16)
                sp.wait_ge(s_y2, k * 16 + 16)
                sp.sem_inc(s_yo, 1)
            sp.sem_inc(s_yo, 1)
            each(sp, body)

        def pool_part(pool, st):
            def body(k):
                pool.wait_ge(s_gu, k + 1)
                n = pool.value_load(over_i[0:1, 1, bass.ds(k, 1)], min_val=0, max_val=SLOTS)
                nc.gpsimd.tensor_copy(ov_st[:, :, :], sorted_h[:, :, bass.ds(n, blk)]).then_inc(s_st, 1)
            each(pool, body)

        def pe_part(pe):
            def body(k):
                pe.wait_ge(s_w, k * 48 + 48)
                pe.wait_ge(s_st, k + 1)
                for i in range(2):
                    w = ov_w[:, i, :].rearrange("p (c n) -> p c n", c=KT)
                    for c in range(KT):
                        last = nc.tensor.matmul(PS[0:blk, 0, i * DE:(i + 1) * DE], ov_st[:, c, :], w[:, c, :], start=(c == 0), stop=(c == KT - 1))
                last.then_inc(s_gu, 1)
                pe.wait_ge(s_hi2, k + 1)
                pass_wait(pe, "pe")
                for j in range(2):
                    last = nc.tensor.transpose(PS[:, 2, j * blk:(j + 1) * blk], ov_h[0:blk, j * P:(j + 1) * P], ident[0:blk, 0:blk])
                last.then_inc(s_tr, 1)
                pe.wait_ge(s_ht, k + 1)
                w = ov_w[:, 2, :].rearrange("p (j n) -> p j n", j=2)
                for half in range(2):
                    for j in range(2):
                        last = nc.tensor.matmul(PS[0:blk, 3 + half, :], ov_hT[:, j, 0:blk], w[:, j, half * 512:(half + 1) * 512], start=(j == 0), stop=(j == 1))
                last.then_inc(s_dn, 1)
            pe.sem_inc(s_gu, 1)
            pe.sem_inc(s_dn, 1)
            each(pe, body)

        def act_part(act, st):
            def body(k):
                act.wait_ge(s_gu, k + 2)
                nc.scalar.activation(ov_g[0:blk, :], PS[0:blk, 0, 0:DE], ACT.Silu).then_inc(s_si, 1)
                act.wait_ge(s_tr, k + 1)
                nc.scalar.activation(ov_hT[:, :, 0:blk], PS[:, 2, 0:2 * blk].rearrange("p (j n) -> p j n", j=2), ACT.Copy).then_inc(s_ht, 1)
            each(act, body)

        def dve_part(dve, st):
            def body(k):
                dve.wait_ge(s_si, k + 1)
                nc.vector.tensor_tensor(ov_h[0:blk, :], ov_g[0:blk, :], PS[0:blk, 0, DE:2 * DE], ALU.mult).then_inc(s_hi2, 1)
                dve.wait_ge(s_dn, k + 2)
                dve.wait_ge(s_yo, k + 1)
                nc.vector.tensor_copy(ov_y[0:blk, :].rearrange("p (a b) -> p a b", a=2), PS[0:blk, 3:5, :]).then_inc(s_y, 1)
            each(dve, body)
        stage_no = len(stages)
        add_stage(sp=sp_part, pool=pool_part, pe=pe_part, act=act_part, dve=dve_part)
        return s_yo
    s_yo = extra_blocks()

    y_rows = at("y_rows", o_b, [P, 2, TT, D])

    def combine():
        s_gather, s_go = sem("cb_g"), sem("cb_go")

        def sp_part(sp):
            sp.drain().then_inc(s_go, 1)

        def pool_part(pool, st):
            for i in range(4):
                pool.wait_ge(y_store[i], NE // 4 * 16)
            pool.wait_ge(s_go, 1)
            for tt in range(TT):
                for k in range(2):
                    pool.indirect_dma_start(y_rows[:, k, tt, :], None, y_sorted[0:SLOTS, :],
                                            bass.IndirectOffsetOnAxis(ap=dest_u[:, k, tt:tt + 1], axis=0)).then_inc(s_gather, 16)
            pool.wait_ge(s_gather, 2 * TT * 16)
            pool.sem_inc(s_gd, 1)

        def dve_part(dve, st):
            dve.wait_ge(s_gather, 2 * TT * 16)
            dve.wait_ge(s_gd, 1)
            for tt in range(TT):
                for k in range(2):
                    st.then(nc.vector.scalar_tensor_tensor(x[:, tt, :], y_rows[:, k, tt, :], gates[:, k, tt:tt + 1], x[:, tt, :],
                                                           ALU.mult, ALU.add))
        s_gd = sem("cb_gd")
        add_stage(sp=sp_part, pool=pool_part, dve=dve_part)
    combine()

    C_Q, C_K, C_V, C_O = 0, 1024, 2048, 3072
    C_SCB = 4 * D + 2 * HM
    C_SCC, C_SCU, C_SBQ, C_SBK, C_SBV, C_GML, C_GSC, C_GSB = (C_SCB + D * i for i in range(1, 9))
    xn3 = at("xn3", o_w, [P, TT, D])
    sq3 = at("sq3", o_w + 16 * KB, [P, TT * D])
    stat3 = at("stat3", o_w + 40 * KB + 1400 // 32 * 32, [P, 2, TT])

    def hidden(tag, gain):
        normalise(tag + "n", x[:, :, :], xn3[:, :, :], stat3[:, 0, :], stat3[:, 1, :], D, sq3[:, :])
        transposes(tag + "t", lambda tt, c: xn3[:, tt, c * P:(c + 1) * P], lambda c: col(gain, c))
    hidden("h2a", "mix2")

    mq = at("mq", o_b, [P, KT, T])
    mk = at("mk", o_b + 16 * KB, [P, KT, T])
    kw = at("kw", o_m, [P, TT, D])
    VA = DM + 1
    v_aug = at("v_aug", o_w, [P, TT, HM, VA])
    o_so = o_w + (TT * HM * VA * 4 + 31) // 32 * 32
    so = at("so", o_so, [P, TT, D])
    Rb = at("Rb", o_so + 16 * KB, [P, HM, T])
    o_ms = o_so + 24 * KB
    gt = at("gt", o_ms, [P, TT, 8])
    lf = at("lf", o_ms + 128, [P, TT, HM])
    lt = at("lt", o_ms + 192, [P, TT, HM])
    ucol = at("ucol", o_ms + 256, [P, TT, HM])
    emcol = at("emcol", o_ms + 320, [P, TT, HM])
    rlast = at("rlast", o_ms + 384, [P, TT, HM])
    wst = at("wst", o_ms + 448, [P, TT, HM])
    stat_y = at("stat_y", o_ms + 512, [P, 2, 16])
    den_s = at("den_s", o_ms + 640, [P, 4])
    g2w = at("g2w", o_so + 16 * KB, [P, KT, 8])
    g2h = at("g2h", o_so + 17 * KB, [P, KT, 8], F32R)
    g2l = at("g2l", o_so + 18 * KB, [P, KT, 8], F32R)
    small_product("g2", w_gates2, g2w, g2h, g2l, 8, gt[:, :, :])

    def ml_out(eng, st, j, ps):
        k, j = divmod(j, 4)
        if k < 2:
            return nc.scalar.activation((mq, mk)[k][:, 2 * j:2 * j + 2, :], ps, ACT.Copy)
        if k == 2:
            return nc.scalar.activation(v_aug[:, :, j, 0:DM], ps, ACT.Copy)
        return nc.scalar.activation(so[:, :, j * DM:(j + 1) * DM], ps, ACT.Sigmoid)
    dense("ml", slabs(w_in2, C_Q, 16), ["feature"] * 8 + ["token"] * 8, ml_out, "act", loaded=RAW)

    ri = at("ri", o_a, [P, T])
    rlf = at("rlf", o_a + 2 * KB, [P, T])
    rz = at("rz", o_a + 4 * KB, [P, T])
    rcum = at("rcum", o_a + 6 * KB, [P, T])
    rR = at("rR", o_a + 8 * KB, [P, T])
    rm = at("rm", o_a + 10 * KB, [P, T])
    sel4 = at("sel4", o_a + 12 * KB, [P, HM, P])

    def ml_rows():
        s_a, s_e, s_l, s_t, s_r, s_b, s_f, s_on = (local("mr_" + n) for n in ("a", "e", "l", "t", "r", "b", "f", "on"))

        def pool_part(pool, st):
            nc.gpsimd.memset(v_aug[:, :, :, DM:VA], 1.0).then_inc(s_on, 1)

        def dve_part(dve, st):
            V = nc.vector
            st.then(V.tensor_tensor(gt[:, :, :], gt[:, :, :], middle(row("b_if", 8), TT), ALU.add))
            V.scalar_tensor_tensor(lt[:, :, :], gt[:, :, HM:2 * HM], -1.0, gt[:, :, HM:2 * HM], ALU.mult, ALU.max).then_inc(s_a, 1)
            st(V.memset(rz[0:HM, :], 0.0))
            st(V.tensor_copy(sel4[0:HM, :, :], ident[0:HM, 0:HM].rearrange("p (h m) -> p h m", m=1).broadcast_to([HM, HM, P])))
            dve.wait_ge(s_e, 2)
            V.scalar_tensor_tensor(lf[:, :, :], gt[:, :, HM:2 * HM], 0.0, lt[:, :, :], ALU.min, ALU.subtract).then_inc(s_l, 1)
            dve.wait_ge(s_t, 1)
            st(V.tensor_copy(ri[0:HM, :], PS[0:HM, 0, :]))
            st.then(V.tensor_copy(rlf[0:HM, :], PS[0:HM, 1, :]))
            st.then(V.tensor_tensor_scan(rcum[0:HM, :], rlf[0:HM, :], rz[0:HM, :], 0.0, ALU.add, ALU.add))
            st.then(V.tensor_tensor(ri[0:HM, :], ri[0:HM, :], rcum[0:HM, :], ALU.subtract))
            st.then(V.tensor_tensor_scan(rR[0:HM, :], ri[0:HM, :], ri[0:HM, :], 0.0, ALU.max, ALU.max))
            V.tensor_tensor(rm[0:HM, :], rcum[0:HM, :], rR[0:HM, :], ALU.add).then_inc(s_r, 1)
            dve.wait_ge(s_b, 1)
            uc = PS[:, 6, 0:16].rearrange("p (t h) -> p t h", h=HM)
            mc = PS[:, 6, 16:32].rearrange("p (t h) -> p t h", h=HM)
            st(V.tensor_copy(ucol[:, :, :], uc))
            st(V.tensor_copy(emcol[:, :, :], mc))
            dve.wait_ge(s_f, 4)
            st.then(V.tensor_copy(rlast[:, :, :], Rb[:, :, P - 1:T:P].rearrange("p h t -> p t h")))
            V.tensor_tensor(wst[:, :, :], ucol[:, :, :], rlast[:, :, :], ALU.subtract).then_inc(s_r, 1)

        def act_part(act, st):
            act.wait_ge(s_a, 1)
            nc.scalar.activation(lt[:, :, :], lt[:, :, :], ACT.Exp, scale=-1.0).then_inc(s_e, 1)
            act.wait_ge(s_e, 1)
            nc.scalar.activation(lt[:, :, :], lt[:, :, :], ACT.Ln, bias=1.0).then_inc(s_e, 1)
            act.wait_ge(s_b, 2)
            for h in range(HM):
                nc.scalar.activation(Rb[:, h, :], PS[:, 2 + h, :], ACT.Copy).then_inc(s_f, 1)
            act.wait_ge(s_r, 2)
            nc.scalar.activation(wst[:, :, :], wst[:, :, :], ACT.Exp)
            nc.scalar.activation(emcol[:, :, :], emcol[:, :, :], ACT.Exp, scale=-1.0)

        def pe_part(pe):
            pe.wait_ge(s_l, 1)
            for b, src in enumerate((gt, lf)):
                for tt in range(TT):
                    last = nc.tensor.transpose(PS[0:HM, b, tt * P:(tt + 1) * P], src[:, tt, 0:HM], ident)
            last.then_inc(s_t, 1)
            pe.wait_ge(s_r, 1)
            for b, src in enumerate((ri, rm)):
                for tt in range(TT):
                    last = nc.tensor.transpose(PS[:, 6, b * 16 + tt * HM:b * 16 + (tt + 1) * HM], src[0:HM, tt * P:(tt + 1) * P], ident[0:HM, 0:HM])
            last.then_inc(s_b, 1)
            for h in range(HM):
                last = nc.tensor.matmul(PS[:, 2 + h, :], sel4[0:HM, h, :], rR[0:HM, :], start=True, stop=True)
            last.then_inc(s_b, 1)
        add_stage(pool=pool_part, dve=dve_part, act=act_part, pe=pe_part)
    ml_rows()

    def ml_keys():
        s_t, s_c = local("mk_t"), local("mk_c")

        def pe_part(pe):
            for u in range(TT * HM):
                tt, h = divmod(u, HM)
                if u >= 8:
                    pe.wait_ge(s_c, u - 7)
                for k in range(2):
                    last = nc.tensor.transpose(PS[:, u % 8, k * P:(k + 1) * P], mk[:, 2 * h + k, tt * P:(tt + 1) * P], ident)
                last.then_inc(s_t, 1)

        def act_part(act, st):
            for u in range(TT * HM):
                tt, h = divmod(u, HM)
                act.wait_ge(s_t, u + 1)
                nc.scalar.activation(kw[:, tt, h * DM:(h + 1) * DM], PS[:, u % 8, 0:DM], ACT.Copy, scale=wst[:, tt, h:h + 1]).then_inc(s_c, 1)
        add_stage(pe=pe_part, act=act_part)
    ml_keys()

    y_tok = at("y_tok", o_a, [P, TT, D])
    cst = at("cst", o_a + 16 * KB, [P, 2, 2, VA])
    sT = at("sT", o_a + 24 * KB, [P, 2, TT, P])
    abc = at("abc", o_a + 28 * KB, [P, 2, TT - 1, P])
    SC = DM ** -0.5

    def ml_pair(pair):
        tag = f"m{pair}_"
        s_sc, s_wi, s_ex, s_sT, s_q, s_num, s_cu, s_cs, s_y = (local(tag + n) for n in ("sc", "wi", "ex", "sT", "q", "num", "cu", "cs", "y"))
        heads = (2 * pair, 2 * pair + 1)

        def pe_part(pe):
            for hb, h in enumerate(heads):
                for i in range(TT):
                    s = slice(i * P, (i + 1) * P)
                    for k in range(2):
                        last = nc.tensor.matmul(PS[:, hb, s], mk[:, 2 * h + k, s], mq[:, 2 * h + k, s], start=(k == 0), stop=(k == 1))
                last.then_inc(s_sc, 1)
            for c in range(TT):
                for hb, h in enumerate(heads):
                    pe.wait_ge(s_sT, hb + 1)
                    if c:
                        pe.wait_ge(s_q, hb + 1)
                        pe.wait_ge(s_cs, 2 * (c - 1) + hb + 1)
                        pe.wait_ge(s_y, 2 * (c - 1) + hb + 1)
                    o = PS[:, 2 + hb, 0:VA]
                    last = nc.tensor.matmul(o, sT[:, hb, c, :], v_aug[:, c, h, :], start=True, stop=(c == 0))
                    if c:
                        for k in range(2):
                            last = nc.tensor.matmul(o, mq[:, 2 * h + k, c * P:(c + 1) * P], cst[:, hb, k, :], start=False, stop=(k == 1))
                    last.then_inc(s_num, 1)
                if c < TT - 1:
                    for hb, h in enumerate(heads):
                        for k in range(2):
                            last = nc.tensor.matmul(PS[:, 4 + 2 * hb + k, 0:VA], kw[:, c, h * DM + k * P:h * DM + (k + 1) * P],
                                                    v_aug[:, c, h, :], start=True, stop=True)
                        last.then_inc(s_cu, 1)

        def act_part(act, st):
            for hb, h in enumerate(heads):
                for c in range(1, TT):
                    i = nc.scalar.activation(abc[:, hb, c - 1, :], Rb[:, h, c * P:(c + 1) * P], ACT.Exp, scale=-1.0, bias=rlast[:, c - 1, h:h + 1])
                i.then_inc(s_ex, 1)
                act.wait_ge(s_wi, hb + 1)
                nc.scalar.activation(flat(sT, hb), flat(sT, hb), ACT.Exp, scale=-1.0).then_inc(s_ex, 1)

        def dve_part(dve, st):
            V = nc.vector
            for hb, h in enumerate(heads):
                for i in range(TT):
                    last = V.tensor_scalar(sT[:, hb, i, :], Rb[:, h, i * P:(i + 1) * P], ucol[:, i, h:h + 1], 0.0, ALU.subtract, ALU.max)
                last.then_inc(s_wi, 1)
            for hb, h in enumerate(heads):
                dve.wait_ge(s_ex, 2 * hb + 2)
                st.then(V.tensor_tensor(sT[:, hb, :, :], sT[:, hb, :, :], middle(const["le"], TT), ALU.mult))
                dve.wait_ge(s_sc, hb + 1)
                V.scalar_tensor_tensor(flat(sT, hb), PS[:, hb, :], SC, flat(sT, hb), ALU.mult, ALU.mult).then_inc(s_sT, 1)
                a = abc[:, hb, :, :].rearrange("p c n -> p (c n)")
                V.scalar_tensor_tensor(mq[:, 2 * h:2 * h + 2, P:T], mq[:, 2 * h:2 * h + 2, P:T], SC, middle(a, 2),
                                       ALU.mult, ALU.mult).then_inc(s_q, 1)
            for c in range(TT):
                if c < TT - 1:
                    for hb, h in enumerate(heads):
                        dve.wait_ge(s_cu, 2 * c + hb + 1)
                        if c:
                            dve.wait_ge(s_num, 2 * c + hb + 1)
                        for k in range(2):
                            ps = PS[:, 4 + 2 * hb + k, 0:VA]
                            if c:
                                i = V.scalar_tensor_tensor(cst[:, hb, k, :], cst[:, hb, k, :], abc[:, hb, c - 1, P - 1:P], ps, ALU.mult, ALU.add)
                            else:
                                i = V.tensor_copy(cst[:, hb, k, :], ps)
                        i.then_inc(s_cs, 1)
                for hb, h in enumerate(heads):
                    dve.wait_ge(s_num, 2 * c + hb + 1)
                    d = den_s[:, hb:hb + 1]
                    st.then(V.tensor_scalar(d, PS[:, 2 + hb, DM:VA], emcol[:, c, h:h + 1], None, ALU.max))
                    st.then(V.scalar_tensor_tensor(d, PS[:, 2 + hb, DM:VA], -1.0, d, ALU.mult, ALU.max))
                    st.then(V.reciprocal(d, d))
                    s = slice(h * DM, (h + 1) * DM)
                    V.scalar_tensor_tensor(y_tok[:, c, s], PS[:, 2 + hb, 0:DM], d, so[:, c, s], ALU.mult, ALU.mult).then_inc(s_y, 1)
        add_stage(pe=pe_part, act=act_part, dve=dve_part)
    ml_pair(0)
    ml_pair(1)

    y_hi = at("y_hi", o_b, [P, KT, T], F32R)
    y_lo = at("y_lo", o_b + 16 * KB, [P, KT, T], F32R)
    merged = at("merged", o_m, [P, KT, T])
    sig_w = at("sig_w", o_w, [P, KT, T])
    sq_y = at("sq_y", o_b, [P, TT * D])
    yh = y_tok[:, :, :].rearrange("p t (h e) -> p (t h) e", e=DM)
    normalise("ny", yh, yh, stat_y[:, 0, :], stat_y[:, 1, :], DM, sq_y[:, :])
    transposes("ty", lambda tt, c: y_tok[:, tt, c * P:(c + 1) * P], lambda c: col("ml", c), dst_hi=y_hi, dst_lo=y_lo)
    hidden("h2b", "mix2")

    def sigmoid_to(dst):
        return lambda eng, st, j, ps: nc.scalar.activation(dst[:, 2 * j:2 * j + 2, :], ps, ACT.Sigmoid)

    def merge_with(sig, first):
        def out_fn(dve, st, j, ps):
            s = slice(2 * j, 2 * j + 2)
            if first:
                return nc.vector.tensor_tensor(merged[:, s, :], sig[:, s, :], ps, ALU.mult)
            st.then(nc.vector.tensor_tensor(sig[:, s, :], sig[:, s, :], ps, ALU.mult))
            return nc.vector.tensor_tensor(merged[:, s, :], merged[:, s, :], sig[:, s, :], ALU.add)
        return out_fn
    dense("gml", slabs(w_in2, C_GML, 4), "feature", sigmoid_to(sig_w), "act")
    dense("pml", slabs(w_ml, 0, 4), "feature", merge_with(sig_w, True), "dve", y_hi, y_lo)

    sc_c = at("sc_c", o_w, [P, KT, T])
    sc_z = at("sc_z", o_w + 16 * KB, [P, KT, T + 2])
    dense("scc", slabs(w_in2, C_SCC, 4), "feature",
          lambda eng, st, j, ps: nc.scalar.activation(sc_c[:, 2 * j:2 * j + 2, :], ps, ACT.Copy), "act")
    dense("scu", slabs(w_in2, C_SCU, 4), "feature",
          lambda eng, st, j, ps: nc.vector.tensor_tensor(sc_z[:, 2 * j:2 * j + 2, 2:2 + T], sc_c[:, 2 * j:2 * j + 2, :], ps, ALU.mult), "dve")
    add_stage(pool=lambda pool, st: nc.gpsimd.memset(sc_z[:, :, 0:2], 0.0))

    def scb_out(dve, st, j, ps):
        V = nc.vector
        for c in (2 * j, 2 * j + 1):
            st.then(V.tensor_scalar(sc_c[:, c, :], sc_z[:, c, 0:T], col("conv2", 3 * c), None, ALU.mult))
            for w in (1, 2):
                st.then(V.scalar_tensor_tensor(sc_c[:, c, :], sc_z[:, c, w:w + T], col("conv2", 3 * c + w), sc_c[:, c, :], ALU.mult, ALU.add))
        return V.tensor_tensor(sc_c[:, 2 * j:2 * j + 2, :], sc_c[:, 2 * j:2 * j + 2, :], ps, ALU.mult)
    dense("scb", slabs(w_in2, C_SCB, 4), "feature", scb_out, "dve")
    split_into("ssc", sc_c, y_hi, y_lo)
    dense("gsc", slabs(w_in2, C_GSC, 4), "feature", sigmoid_to(sig_w), "act")
    dense("psc", slabs(w_sc, 0, 4), "feature", merge_with(sig_w, False), "dve", y_hi, y_lo)

    bqT = at("bqT", o_w, [P, KT, T])
    bkT = at("bkT", o_w + 16 * KB, [P, KT, T])
    bv_tok = at("bv_tok", o_b, [P, TT, D])
    sig_b = at("sig_b", o_b + 16 * KB, [P, KT, T])

    def sb_out(eng, st, j, ps):
        k, j = divmod(j, 4)
        if k < 2:
            return nc.scalar.activation((bqT, bkT)[k][:, 2 * j:2 * j + 2, :], ps, ACT.Copy)
        return nc.scalar.activation(bv_tok[:, :, j * UC:(j + 1) * UC], ps, ACT.Copy)
    dense("sb", slabs(w_in2, C_SBQ, 12), ["feature"] * 8 + ["token"] * 4, sb_out, "act")
    dense("gsb", slabs(w_in2, C_GSB, 4), "feature", sigmoid_to(sig_b), "act")
    by_tok = at("by_tok", o_a, [P, TT, D])
    NZ = 1280
    zs = at("zs", o_a + 16 * KB, [P, 2, NZ])
    zl = at("zl", o_a + 16 * KB + 2 * NZ * 4, [P, NZ])
    zp = at("zp", o_w + 32 * KB, [P, NZ])
    OFF = {0: 512, 1: 1024, 2: 896}

    def later(j):
        return slice(OFF[j], OFF[j] + T - (j + 1) * P)

    def block_of(j, tt):
        a = j * P if tt == j else OFF[j] + (tt - j - 1) * P
        return slice(a, a + P)

    def stick():
        s_z, s_zc, s_zd, s_ab, s_ln, s_sp, s_suf, s_arg, s_A, s_av, s_y = (
            local("sb_" + n) for n in ("z", "zc", "zd", "ab", "ln", "sp", "suf", "arg", "A", "av", "y"))
        s_e = local("sb_e")
        zps = PS[:, 0:3, :].rearrange("p b n -> p (b n)")
        sps = PS[:, 3:6, :].rearrange("p b n -> p (b n)")

        def pe_part(pe):
            def scores(h):
                if h:
                    pe.wait_ge(s_zc, h)
                    pe.wait_ge(s_zd, h)
                r = slice((h % 2) * DS, (h % 2) * DS + DS)
                for j in range(TT):
                    k = bkT[r, h // 2, j * P:(j + 1) * P]
                    last = nc.tensor.matmul(zps[:, block_of(j, j)], k, bqT[r, h // 2, j * P:(j + 1) * P], start=True, stop=True)
                    if j < TT - 1:
                        last = nc.tensor.matmul(zps[:, later(j)], k, bqT[r, h // 2, (j + 1) * P:T], start=True, stop=True)
                last.then_inc(s_z, 1)

            def sums(h):
                pe.wait_ge(s_sp, h + 1)
                if h:
                    pe.wait_ge(s_arg, h)
                for i in range(TT):
                    for j in range(i, TT):
                        tri = const["neg_ge"] if j == i else const["neg_ones"]
                        last = nc.tensor.matmul(sps[:, block_of(i, j)], tri, zp[:, block_of(j, j)], start=(j == i), stop=(j in (i, TT - 1)))
                        if j < TT - 1:
                            a = block_of(i, j + 1).start
                            last = nc.tensor.matmul(sps[:, a:a + T - (j + 1) * P], tri, zp[:, later(j)], start=(j == i), stop=False)
                last.then_inc(s_suf, 1)

            def values(h):
                pe.wait_ge(s_A, h + 1)
                if h >= 2:
                    pe.wait_ge(s_y, h - 1)
                for tt in range(TT):
                    for j in range(tt + 1):
                        last = nc.tensor.matmul(PS[:, 6 + h % 2, tt * DS:(tt + 1) * DS], zs[:, h % 2, block_of(j, tt)],
                                                bv_tok[:, j, h * DS:(h + 1) * DS], start=(j == 0), stop=(j == tt))
                last.then_inc(s_av, 1)
            scores(0)
            for h in range(HS):
                if h + 1 < HS:
                    scores(h + 1)
                sums(h)
                if h:
                    values(h - 1)
            values(HS - 1)

        def act_part(act, st):
            def weights(h):
                act.wait_ge(s_arg, h + 1)
                nc.scalar.activation(zs[:, h % 2, :], zs[:, h % 2, :], ACT.Exp).then_inc(s_A, 1)

            def out_y(h):
                act.wait_ge(s_av, h + 1)
                nc.scalar.activation(by_tok[:, :, h * DS:(h + 1) * DS], PS[:, 6 + h % 2, 0:TT * DS].rearrange("p (t e) -> p t e", e=DS),
                                     ACT.Copy).then_inc(s_y, 1)
            for h in range(HS):
                act.wait_ge(s_z, h + 1)
                if h >= 2:
                    act.wait_ge(s_av, h - 1)
                nc.scalar.activation(zs[:, h % 2, T:NZ], zps[:, T:NZ], ACT.Copy, scale=DS ** -0.5).then_inc(s_zc, 1)
                act.wait_ge(s_ab, h + 1)
                nc.scalar.activation(zl[:, :], zl[:, :], ACT.Exp, scale=-1.0).then_inc(s_e, 1)
                act.wait_ge(s_e, h + 1)
                nc.scalar.activation(zl[:, :], zl[:, :], ACT.Ln, bias=1.0).then_inc(s_ln, 1)
                if h:
                    weights(h - 1)
                if h >= 2:
                    out_y(h - 2)
            weights(HS - 1)
            out_y(HS - 2)
            out_y(HS - 1)

        def dve_part(dve, st):
            V = nc.vector

            def arg(h):
                dve.wait_ge(s_suf, h + 1)
                V.tensor_tensor(zs[:, h % 2, :], zs[:, h % 2, :], sps[:, 0:NZ], ALU.add).then_inc(s_arg, 1)
            for h in range(HS):
                dve.wait_ge(s_z, h + 1)
                if h >= 2:
                    dve.wait_ge(s_av, h - 1)
                V.scalar_tensor_tensor(zs[:, h % 2, 0:T].rearrange("p (a b) -> p a b", b=P), zps[:, 0:T].rearrange("p (a b) -> p a b", b=P),
                                       DS ** -0.5, middle(const["neg_mask"], TT), ALU.mult, ALU.add).then_inc(s_zd, 1)
                dve.wait_ge(s_zc, h + 1)
                dve.wait_ge(s_zd, h + 1)
                if h:
                    dve.wait_ge(s_sp, h)
                V.scalar_tensor_tensor(zl[:, :], zs[:, h % 2, :], -1.0, zs[:, h % 2, :], ALU.mult, ALU.max).then_inc(s_ab, 1)
                if h:
                    arg(h - 1)
                dve.wait_ge(s_ln, h + 1)
                V.scalar_tensor_tensor(zp[:, :], zs[:, h % 2, :], 0.0, zl[:, :], ALU.max, ALU.add).then_inc(s_sp, 1)
            arg(HS - 1)
        add_stage(pe=pe_part, act=act_part, dve=dve_part)
    stick()
    b_hi = at("b_hi", o_w, [P, KT, T], F32R)
    b_lo = at("b_lo", o_w + 16 * KB, [P, KT, T], F32R)
    transposes("tby", lambda tt, c: by_tok[:, tt, c * P:(c + 1) * P], None, dst_hi=b_hi, dst_lo=b_lo)
    dense("psb", slabs(w_sb, 0, 4), "feature", merge_with(sig_b, False), "dve", b_hi, b_lo)
    split_into("smg", merged, act_hi, act_lo)
    dense("wout2", slabs(w_out2, 0, 4), "token", residual_out, "dve")

    hidden("h3", "mlp2")

    def mlp():
        u0 = Stream.n
        NCH = DFF // D
        Stream.n += 8 * NCH
        s_relu, s_sq, s_bh, s_bl, s_add = (local("mlp_" + n) for n in ("relu", "sq", "bh", "bl", "add"))
        rl = at("rl", o_w, [P, 2, 2, T])

        def each(eng, body):
            body(0)
            with eng.Fori(1, NCH - 1) as c:
                body(c)
            body(NCH - 1)

        def num(c, j):
            s = u0 + j
            if isinstance(c, int):
                s += 8 * c
                return s, s, s // RAW + 1
            return s, c * 8 + s, c * 2 + s // RAW + 1

        def sp_part(sp):
            def body(c):
                for j in range(8):
                    s, u, _ = num(c, j)
                    if j < 4:
                        src = w_up2[:, bass.ds(c * D + j * UC, UC)].rearrange("(c p) n -> p c n", p=P)
                    else:
                        src = w_down2[bass.ds(c * D, D), (j - 4) * UC:(j - 3) * UC].rearrange("(c p) n -> p c n", p=P)
                    load_unit(sp, s, u, ("p (c n) -> p c n", dict(c=KT)), src)
            each(sp, body)

        def pe_part(pe):
            def body(c):
                for j in range(8):
                    s, u, _ = num(c, j)
                    pe.wait_ge(lo_ready, u + 1)
                    if j >= 6:
                        pe.wait_ge(s_add, c * 4 + (j - 5))
                    elif j >= 2:
                        pe.wait_ge(s_relu, c * 4 + (j - 1))
                    elif not isinstance(c, int) or c:
                        pe.wait_ge(s_add, c * 4 + (j - 1))
                    if j == 4:
                        pe.wait_ge(s_bl, c * 4 + 4)
                    h = whi[:, s % SPLIT, :].rearrange("p (c n) -> p c n", c=KT)
                    l = wlo[:, s % SPLIT, :].rearrange("p (c n) -> p c n", c=KT)
                    b = PS[:, 2 * (j % 2):2 * (j % 2) + 2, :]
                    bt = b.rearrange("p b (t c) -> p (b t) c", c=UC)
                    for m in range(2 if j < 4 else TT):
                        f = slice(m * P, m * P + P)
                        for k in range(KT):
                            if j < 4:
                                three = ((h[:, k, f], act_hi[:, k, :]), (h[:, k, f], act_lo[:, k, :]), (l[:, k, f], act_hi[:, k, :]))
                            else:
                                three = ((y_hi[:, k, f], h[:, k, :]), (y_hi[:, k, f], l[:, k, :]), (y_lo[:, k, f], h[:, k, :]))
                            for n, (a_, b_) in enumerate(three):
                                i = nc.tensor.matmul((b if j < 4 else bt)[:, m, :], a_, b_, start=(k == 0 and n == 0), stop=(k == KT - 1 and n == 2))
                    i.then_inc(pe_unit, 1)
            each(pe, body)

        def ahead(c, j):
            s, u, _ = num(c, j)
            if isinstance(c, int):
                return s + 2, u + 2, (s + 2) // RAW + 1
            return s + 2, u + 2, c * 2 + (s + 2) // RAW + 1

        def act_part(act, st):
            def body(c):
                for j in range(8):
                    s, u, _ = num(c, j)
                    b = PS[:, 2 * (j % 2):2 * (j % 2) + 2, :]
                    if j < 4:
                        act.wait_ge(pe_unit, u + 1)
                        if not isinstance(c, int) or c or j >= 2:
                            act.wait_ge(s_bl, c * 4 + (j - 1))
                        nc.scalar.activation(rl[:, j % 2, :, :], b, ACT.Relu).then_inc(s_relu, 1)
                    split_hi(act, *ahead(c, j))
                    if j < 4:
                        act.wait_ge(s_sq, c * 4 + (j + 1))
                        nc.scalar.activation(y_hi[:, 2 * j:2 * j + 2, :], rl[:, j % 2, :, :], ACT.Copy).then_inc(s_bh, 1)
            each(act, body)

        def dve_part(dve, st):
            def body(c):
                for j in range(8):
                    s, u, _ = num(c, j)
                    if j < 4:
                        dve.wait_ge(s_relu, c * 4 + (j + 1))
                        nc.vector.tensor_tensor(rl[:, j % 2, :, :], rl[:, j % 2, :, :], rl[:, j % 2, :, :], ALU.mult).then_inc(s_sq, 1)
                    else:
                        dve.wait_ge(pe_unit, u + 1)
                        f = slice((j - 4) * UC, (j - 3) * UC)
                        ps = PS[:, 2 * (j % 2):2 * (j % 2) + 2, :].rearrange("p b (t c) -> p (b t) c", c=UC)
                        if not isinstance(c, int) or c:
                            dve.wait_ge(s_add, c * 4 + (j - 7))
                        nc.vector.tensor_tensor(x[:, :, f], x[:, :, f], ps, ALU.add).then_inc(s_add, 1)
                    split_lo(dve, *ahead(c, j)[:2])
                    if j < 4:
                        dve.wait_ge(s_bh, c * 4 + (j + 1))
                        nc.vector.tensor_tensor(y_lo[:, 2 * j:2 * j + 2, :], rl[:, j % 2, :, :], y_hi[:, 2 * j:2 * j + 2, :].bitcast(F32),
                                                ALU.subtract).then_inc(s_bl, 1)
            each(dve, body)
        add_stage(sp=sp_part, pe=pe_part, act=act_part, dve=dve_part)
    mlp()
    TOTAL["n"] = Stream.n

    gfin = at("gfin", o_b, [P, D])
    s_gf = sem("gfin")
    normalise("nf", x[:, :, :], xn3[:, :, :], stat3[:, 0, :], stat3[:, 1, :], D, sq3[:, :])
    add_stage(pool=lambda pool, st: pool.dma_start(gfin[:, :], gfin_in).then_inc(s_gf, 16))
    s_fin = sem("fin")
    out_v = out.rearrange("o (t p) d -> p (o t) d", p=P)

    def final_dve(dve, st):
        dve.wait_ge(s_gf, 16)
        for tt in range(TT):
            nc.vector.tensor_tensor(xn3[:, tt, :], xn3[:, tt, :], gfin[:, :], ALU.mult).then_inc(s_fin, 1)

    def final_sp(sp):
        for tt in range(TT):
            sp.wait_ge(s_fin, tt + 1)
            sp.dma_start(out_v[:, tt, :], xn3[:, tt, :]).then_inc(s_out, 16)
        sp.wait_ge(s_out, 16 * TT)
    add_stage(dve=final_dve, sp=final_sp)
    return_stages = stages if upto is None else stages[:upto]

    def close(eng, name, k):
        eng.drain().then_inc(done[name], 1)
        for other in done:
            if other != name:
                eng.wait_ge(done[other], k + 1)

    with nc.Block() as block:
        @block.sync
        def _(sp):
            for stage in return_stages:
                if "sp" in stage:
                    stage["sp"](sp)

        @block.tensor
        def _(pe):
            for k, stage in enumerate(return_stages):
                if "pe" in stage:
                    stage["pe"](pe)
                close(pe, "pe", k)

        @block.scalar
        def _(act):
            st = Steps(act, "act")
            for k, stage in enumerate(return_stages):
                if "act" in stage:
                    stage["act"](act, st)
                close(act, "act", k)

        @block.vector
        def _(dve):
            st = Steps(dve, "dve")
            for k, stage in enumerate(return_stages):
                if "dve" in stage:
                    stage["dve"](dve, st)
                close(dve, "dve", k)

        @block.gpsimd
        def _(pool):
            st = Steps(pool, "pool")
            for k, stage in enumerate(return_stages):
                if used.get(k - 1):
                    b = banks[(k - 1) % 3]
                    nc.gpsimd.sem_clear(range(b[0], b[0] + used[k - 1]))
                if "pool" in stage:
                    stage["pool"](pool, st)
                close(pool, "pool", k)
    return stages


def lay_out(a):
    f = np.float32

    def by_partition(v, n):
        return np.asarray(v, f).reshape(n, P).T

    c = np.zeros((P, NCOLS), f)

    def put(name, block):
        c[:, COLS[name]:COLS[name] + block.shape[1]] = block
    put("ln1", by_partition(a["ln1_g"][0], KT))
    put("qg", np.concatenate([a["attn_q_norm_g"][0]] * 2)[:, None])
    put("kg", np.concatenate([a["attn_k_norm_g"][0]] * 2)[:, None])
    put("attn_out", by_partition(a["attn_out_norm_g"][0], 4))
    put("dn_out", np.asarray(a["dn_out_norm_g"][0])[:, None])
    put("ln2", by_partition(a["ln2_g"][0], KT))
    put("ln2_i", np.asarray(a["ln2_g"][0]).reshape(P, KT))
    put("mix2", by_partition(a["norm_mix_g_2"][0], KT))
    put("ml", by_partition(a["ml_norm_g_2"][0], KT))
    put("mlp2", by_partition(a["norm_mlp_g_2"][0], KT))
    put("conv", np.asarray(a["dn_conv_w"][0]).reshape(CONV, 12, P).transpose(2, 1, 0).reshape(P, 12 * CONV))
    put("conv2", np.asarray(a["conv_w_2"][0]).reshape(3, KT, P).transpose(2, 1, 0).reshape(P, 3 * KT))
    r = np.concatenate([np.asarray(a["dn_a_log"]).reshape(-1), np.asarray(a["dn_dt_bias"]).reshape(-1),
                        np.asarray(a["router_group_b"]).reshape(-1), np.asarray(a["router_expert_b"]).reshape(-1),
                        np.asarray(a["b_if_2"]).reshape(-1)]).astype(f)
    rpb = np.asarray(a["attn_rpb"][0])
    r2, qc = np.divmod(np.arange(P), GW)
    kk, kc = np.arange(KROWS), np.arange(GW)
    first = np.clip(qc - WIN // 2, 0, GW - WIN)
    inside = (kc[None] >= first[:, None]) & (kc[None] < first[:, None] + WIN)
    ro = kk[None] + 1 - r2[:, None]
    co = np.clip(kc[None] - qc[:, None] + WIN - 1, 0, 2 * WIN - 2)
    table = rpb[:, ro[:, :, None], co[:, None, :]].transpose(1, 0, 2, 3)
    bias = np.where(inside[:, None, None, :], table, f(-BIG)).astype(f)
    w_in, w_in2 = np.asarray(a["w_in"][0]), np.asarray(a["w_in_2"][0])
    g0 = 4 * D
    return {
        "x": np.asarray(a["x"]), "cols": c, "rows": np.broadcast_to(r, (P, NROWS)).copy(), "consts": constant_matrices(),
        "bias": bias, "w_in": w_in, "w_ab": w_in[:, -16:].copy(), "w_out": np.asarray(a["w_out"][0]),
        "w_router": np.concatenate([np.asarray(a["router_group_w"][0]), np.asarray(a["router_expert_w"][0])], axis=1),
        "w_gate": np.asarray(a["expert_w_gate"][0]), "w_up": np.asarray(a["expert_w_up"][0]), "w_down": np.asarray(a["expert_w_down"][0]),
        "w_in2": w_in2, "w_gates2": w_in2[:, g0:g0 + 2 * HM].copy(),
        "w_ml": np.asarray(a["w_ml_proj_2"][0]), "w_sc": np.asarray(a["w_sc_proj_2"][0]), "w_sb": np.asarray(a["w_sb_proj_2"][0]),
        "w_out2": np.asarray(a["w_out_2"][0]), "w_up2": np.asarray(a["w_up_2"][0]), "w_down2": np.asarray(a["w_down_2"][0]),
        "gfin": np.broadcast_to(np.asarray(a["norm_final_g_2"]), (P, D)).copy(),
    }


def kernel(**inputs):
    import concourse.bacc as bacc
    from concourse.bass_utils import run_bass_kernel_spmd

    arrays = lay_out(inputs)
    nc = bacc.Bacc("TRN2", target_bir_lowering=False, num_devices=1)
    args = [nc.dram_tensor(f"in_{n}", v.shape, F32, kind="ExternalInput").ap() for n, v in arrays.items()]
    args.append(nc.dram_tensor("out_y", (1, T, D), F32, kind="ExternalOutput").ap())
    build(nc, *args)
    r = run_bass_kernel_spmd(nc, [{f"in_{n}": np.ascontiguousarray(v) for n, v in arrays.items()}], core_ids=[0])
    return np.asarray(r.results[0]["out_y"])
```

```python
from contextlib import contextmanager

import numpy as np

import concourse.bass as bass
from concourse import mybir

F32 = mybir.dt.float32
F32R = mybir.dt.float32r
I32 = mybir.dt.int32
U32 = mybir.dt.uint32
ALU = mybir.AluOpType
ACT = mybir.ActivationFunctionType
X_AXIS = mybir.AxisListType.X

P = 128
T = 512
TT = T // P
D = 1024
KT = D // P
EPS = 1e-6
HA, DA = 8, 64
GW, GH = 64, T // 64
WIN = 16
KROWS = 2 * GH - 2
HD, DD = 4, 128
CONV = 5
NG, EG = 8, 8
NE = NG * EG
DE = 256
SLOTS = 2 * T
BLK = 64
HM, DM = 4, 256
HS, DS = 16, 64
DFF = 4 * D
UNIT = 2048
UC = UNIT // KT
RAW = 4
SPLIT = 2
BIG = 1e30

COLS = {}
_n = 0
for _name, _w in (("ln1", KT), ("qg", 1), ("kg", 1), ("attn_out", 4), ("dn_out", 1), ("ln2", KT), ("ln2_i", KT),
                  ("mix2", KT), ("ml", KT), ("mlp2", KT), ("conv", 12 * CONV), ("conv2", KT * 3)):
    COLS[_name] = _n
    _n += _w
NCOLS = _n
ROWS = {}
_n = 0
for _name, _w in (("a_log", 8), ("dt_bias", 8), ("rb", NG + NE), ("b_if", 8)):
    ROWS[_name] = _n
    _n += _w
NROWS = _n
CONSTS = ("ident", "le", "ge", "lt", "gt", "diag16", "ones")


def constant_matrices():
    p, f = np.arange(P)[:, None], np.arange(P)[None, :]
    m = {"ident": p == f, "le": p <= f, "ge": p >= f, "lt": p < f, "gt": p > f, "diag16": p // 16 == f // 16,
         "ones": p >= 0 * f}
    return np.stack([m[k].astype(np.float32) for k in CONSTS], axis=1)


def build(nc, x_in, cols_in, rows_in, consts_in, bias_in, w_in, w_ab, w_out, w_router, w_gate, w_up, w_down,
          w_in2, w_gates2, w_ml, w_sc, w_sb, w_out2, w_up2, w_down2, gfin_in, out, upto=None, blk=BLK):
    stages = []
    BANK = 14
    holders = {}
    for i in range(3 * BANK):
        h = nc.alloc_semaphore(f"local{i}")
        holders[h.num] = h
    first_sem = min(holders)
    banks = [list(range(first_sem + b * BANK, first_sem + (b + 1) * BANK)) for b in range(3)]
    used = {}

    def local(name):
        k = len(stages)
        i = used.get(k, 0)
        used[k] = i + 1
        num = banks[k % 3][i]
        if num in holders:
            nc.release_semaphore(holders[num])
        holders[num] = nc.alloc_semaphore(name, num=num)
        return holders[num]

    def sem(name):
        return nc.alloc_semaphore(name)

    base = 16512
    o_raw = base
    o_hi = o_raw + RAW * UNIT * 4
    o_lo = o_hi + SPLIT * UNIT * 4
    o_x = o_lo + SPLIT * UNIT * 4
    o_a = o_x + TT * D * 4
    o_b = o_a + 2 * KT * T * 4
    o_m = o_b + 2 * KT * T * 4
    o_p = o_m + KT * T * 4
    o_w = o_p + 4608
    end = 229344
    KB = 1024

    def at(name, offset, shape, dt=F32):
        size = int(np.prod(shape[1:])) * 4
        assert offset % 32 == 0 and offset + size <= end, (name, offset, size, end)
        return nc.alloc_sbuf_tensor_at(name, shape, dt, offset=offset)

    raw = at("raw", o_raw, [P, RAW, UNIT])
    whi = at("whi", o_hi, [P, SPLIT, UNIT], F32R)
    wlo = at("wlo", o_lo, [P, SPLIT, UNIT], F32R)
    x = at("x", o_x, [P, TT, D])
    consts = at("consts", o_p, [P, len(CONSTS), P])
    o_cols = o_p + 4 * len(CONSTS) * P
    o_rows = o_cols + 4 * ((NCOLS + 7) // 8 * 8)
    cols = at("cols", o_cols, [P, NCOLS])
    rows = at("rows", o_rows, [P, NROWS])
    assert o_rows + 4 * NROWS <= o_w
    act_hi = at("act_hi", o_a, [P, KT, T], F32R)
    act_lo = at("act_lo", o_a + 16 * KB, [P, KT, T], F32R)
    PS = nc.alloc_psum_tensor("PS", [P, 8, 512], F32)
    const = {n: consts[:, i, :] for i, n in enumerate(CONSTS)}
    ident, ones = const["ident"], const["ones"]

    def col(name, j=0):
        return cols[:, COLS[name] + j:COLS[name] + j + 1]

    def row(name, n):
        return rows[:, ROWS[name]:ROWS[name] + n]

    def middle(ap, n):
        return ap.rearrange("p (a f) -> p a f", a=1).broadcast_to([P, n, ap.shape[-1]])

    raw_full = [sem(f"raw_full{i}") for i in range(RAW)]
    hi_ready, lo_ready = sem("hi_ready"), sem("lo_ready")
    pe_unit = sem("pe_unit")
    evac = {n: sem(f"{n}_evac") for n in ("act", "dve")}
    done = {n: sem(f"{n}_stage") for n in ("pe", "act", "dve", "pool")}
    steps = {n: sem(f"{n}_steps") for n in ("act", "dve", "pool")}
    passed = {n: sem(f"{n}_passed") for n in ("sp", "pe", "pool")}

    def pass_wait(eng, name):
        eng.sem_inc(passed[name], 1)

    s_load = sem("s_load")
    s_small = sem("s_small")
    small_uses = []
    s_out = sem("s_out")

    class Steps:

        def __init__(self, eng, name):
            self.eng, self.sem, self.n = eng, steps[name], 0

        def __call__(self, ins):
            ins.then_inc(self.sem, 1)
            self.n += 1
            return self.n

        def wait(self, n=None):
            self.eng.wait_ge(self.sem, self.n if n is None else n)

        def then(self, ins):
            self(ins)
            self.wait()

    class Stream:
        n = 0
        left = {"act": 0, "dve": 0}

    def raw_slot(u):
        return u % RAW

    def load_unit(sp, u, u_reg, view, src):
        if isinstance(u_reg, int):
            if u_reg >= RAW:
                sp.wait_ge(lo_ready, u_reg - RAW + 1)
        else:
            sp.wait_ge(lo_ready, u_reg - (RAW - 1))
            pass_wait(sp, "sp")
        dst = raw[:, raw_slot(u), :]
        if view:
            dst = dst.rearrange(view[0], **view[1])
        sp.dma_start(dst, src).then_inc(raw_full[raw_slot(u)], 16)

    TOTAL = {}

    WIDE = 3
    whi_x = at("whi_x", o_w + 8 * KB, [P, UNIT], F32R)
    wlo_x = at("wlo_x", o_w + 16 * KB, [P, UNIT], F32R)
    wide_from = {}

    def parts(u, wide=False):
        i = (u - wide_from["u"]) % WIDE if wide else u % SPLIT
        return (whi_x[:, :], wlo_x[:, :]) if i == SPLIT else (whi[:, i, :], wlo[:, i, :])

    def split_hi(act, u, u_reg, uses, wide=False):
        slots = WIDE if wide else SPLIT
        if isinstance(u_reg, int):
            if u_reg >= TOTAL["n"]:
                return
            if u_reg >= slots:
                act.wait_ge(pe_unit, u_reg - slots + 1)
        else:
            act.wait_ge(pe_unit, u_reg - (slots - 1))
        act.wait_ge(raw_full[raw_slot(u)], uses * 16)
        nc.scalar.activation(parts(u, wide)[0], raw[:, raw_slot(u), :], ACT.Copy).then_inc(hi_ready, 1)

    def split_lo(dve, u, u_reg, wide=False):
        if isinstance(u_reg, int) and u_reg >= TOTAL["n"]:
            return
        dve.wait_ge(hi_ready, u_reg + 1)
        hi, lo = parts(u, wide)
        nc.vector.tensor_tensor(lo, raw[:, raw_slot(u), :], hi.bitcast(F32),
                                ALU.subtract).then_inc(lo_ready, 1)

    group = []

    def add_stage(**parts):
        if group:
            group[-1].append(parts)
        else:
            stages.append(parts)

    @contextmanager
    def together():
        group.append([])
        yield
        members = group.pop()

        def one_after_another(fns):
            return lambda *args: [fn(*args) for fn in fns]
        stages.append({e: one_after_another([m[e] for m in members if e in m])
                       for e in ("sp", "pe", "act", "dve", "pool") if any(e in m for m in members)})

    def dense(tag, sources, mode, out_fn, by, acc_hi=act_hi, acc_lo=act_lo, loaded=0, act_also=None, dve_also=None, pool_part=None):
        u0, n = Stream.n, len(sources)
        modes, bys, acc_his, acc_los = (v if isinstance(v, list) else [v] * n for v in (mode, by, acc_hi, acc_lo))
        Stream.n += n
        counts = []
        for by_j in bys:
            Stream.left[by_j] += 1
            counts.append(Stream.left[by_j])

        def bank(j):
            return 2 * (j % 2)

        def psum_of(j):
            b = PS[:, bank(j):bank(j) + 2, :]
            if modes[j] == "token":
                return b.rearrange("p b (t c) -> p (b t) c", c=UC)
            return b

        def sp_part(sp):
            for j, src in enumerate(sources):
                if j < loaded:
                    continue
                load_unit(sp, u0 + j, u0 + j, ("p (c n) -> p c n", dict(c=KT)), src.rearrange("(c p) n -> p c n", p=P))

        def pe_part(pe):
            for j in range(n):
                u = u0 + j
                pe.wait_ge(lo_ready, u + 1)
                if j >= 2:
                    pe.wait_ge(evac[bys[j - 2]], counts[j - 2])
                h = whi[:, u % SPLIT, :].rearrange("p (c n) -> p c n", c=KT)
                l = wlo[:, u % SPLIT, :].rearrange("p (c n) -> p c n", c=KT)
                ps = psum_of(j)
                a_hi, a_lo = acc_his[j], acc_los[j]
                for m in range(2 if modes[j] == "feature" else TT):
                    for c in range(KT):
                        if modes[j] == "feature":
                            s = slice(m * P, m * P + P)
                            three = ((h[:, c, s], a_hi[:, c, :]), (h[:, c, s], a_lo[:, c, :]), (l[:, c, s], a_hi[:, c, :]))
                        else:
                            s = slice(m * P, m * P + P)
                            three = ((a_hi[:, c, s], h[:, c, :]), (a_hi[:, c, s], l[:, c, :]), (a_lo[:, c, s], h[:, c, :]))
                        for k, (a, b) in enumerate(three):
                            last = nc.tensor.matmul(ps[:, m, :], a, b, start=(c == 0 and k == 0), stop=(c == KT - 1 and k == 2))
                last.then_inc(pe_unit, 1)

        def taker(eng, st, j):
            eng.wait_ge(pe_unit, u0 + j + 1)
            out_fn(eng, st, j, psum_of(j)).then_inc(evac[bys[j]], 1)

        def act_part(act, st):
            for j in range(n):
                u = u0 + j
                if bys[j] == "act":
                    taker(act, st, j)
                split_hi(act, u + 2, u + 2, (u + 2) // RAW + 1)
                if act_also:
                    act_also(act, st, j, counts[j])

        def dve_part(dve, st):
            for j in range(n):
                u = u0 + j
                if bys[j] == "dve":
                    taker(dve, st, j)
                split_lo(dve, u + 2, u + 2)
                if dve_also:
                    dve_also(dve, st, j, counts[j])

        add_stage(sp=sp_part, pe=pe_part, act=act_part, dve=dve_part, **({"pool": pool_part} if pool_part else {}))

    def slabs(w, c0, n):
        return [w[:, c0 + UC * j:c0 + UC * (j + 1)] for j in range(n)]

    def transposes(tag, src_tile, gain, n_c=KT, dst_hi=act_hi, dst_lo=act_lo, dst_f32=None, bank=0):
        s_t = local(f"{tag}_t")

        def pe_part(pe):
            for c in range(n_c):
                for tt in range(TT):
                    last = nc.tensor.transpose(PS[:, bank + c % 8, tt * P:(tt + 1) * P], src_tile(tt, c), ident)
                last.then_inc(s_t, 1)

        s_h = local(f"{tag}_h")

        def act_part(act, st):
            for c in range(n_c):
                act.wait_ge(s_t, c + 1)
                dst = dst_f32[:, c, :] if dst_f32 is not None else dst_hi[:, c, :]
                g = gain(c) if gain else 1.0
                nc.scalar.activation(dst, PS[:, bank + c % 8, :], ACT.Copy, scale=g).then_inc(s_h, 1)

        def dve_part(dve, st):
            if dst_f32 is not None:
                return
            for c in range(n_c):
                dve.wait_ge(s_h, c + 1)
                g = gain(c) if gain else 1.0
                nc.vector.scalar_tensor_tensor(dst_lo[:, c, :], PS[:, bank + c % 8, :], g, dst_hi[:, c, :].bitcast(F32),
                                               ALU.mult, ALU.subtract)
        add_stage(pe=pe_part, act=act_part, dve=dve_part)

    def normalise(tag, src, dst, ss, inv, width, scratch, eps_scale=None, extra=1.0):
        groups = src.shape[1]
        eps_scale = width if eps_scale is None else eps_scale
        s_sq, s_var, s_std = local(f"{tag}_sq"), local(f"{tag}_var"), local(f"{tag}_std")
        few = groups == TT and width == D
        chunks = 4
        gc = groups // chunks
        sc = scratch.rearrange("p (g w) -> p g w", w=width)

        def act_part(act, st):
            for i in range(chunks):
                if few:
                    if i < 2:
                        nc.scalar.activation(sc[:, i, :], src[:, i, :], ACT.Square, accum_out=ss[:, i:i + 1]).then_inc(s_sq, 1)
                else:
                    nc.scalar.activation(sc[:, i * gc:(i + 1) * gc, :], src[:, i * gc:(i + 1) * gc, :], ACT.Square).then_inc(s_sq, 1)
            act.wait_ge(s_var, 1)
            nc.scalar.activation(inv, ss, ACT.Sqrt).then_inc(s_std, 1)

        def dve_part(dve, st):
            if few:
                for i in (2, 3):
                    st(nc.vector.tensor_tensor_reduce(out=sc[:, i, :], in0=src[:, i, :], in1=src[:, i, :], scale=1.0, scalar=0.0,
                                                      op0=ALU.mult, op1=ALU.add, accum_out=ss[:, i:i + 1]))
                dve.wait_ge(s_sq, 2)
            else:
                for i in range(chunks):
                    dve.wait_ge(s_sq, i + 1)
                    st(nc.vector.tensor_reduce(ss[:, i * gc:(i + 1) * gc], sc[:, i * gc:(i + 1) * gc, :], X_AXIS, ALU.add))
            st.wait()
            nc.vector.tensor_scalar(ss, ss, 1.0 / eps_scale, EPS, ALU.mult, ALU.add).then_inc(s_var, 1)
            dve.wait_ge(s_std, 1)
            st.then(nc.vector.reciprocal(inv, inv))
            if extra != 1.0:
                st.then(nc.vector.tensor_scalar(inv, inv, extra, None, ALU.mult))
            if few:
                for i in range(groups):
                    nc.vector.tensor_scalar(dst[:, i, :], src[:, i, :], inv[:, i:i + 1], None, ALU.mult)
            else:
                nc.vector.tensor_tensor(dst, src, inv.rearrange("p (g w) -> p g w", w=1).broadcast_to([P, groups, width]), ALU.mult)
        add_stage(act=act_part, dve=dve_part)

    xv = x_in.rearrange("o (t p) d -> p (o t) d", p=P)
    attn_bias = at("attn_bias", o_w + 8 * KB, [P, HA, KROWS, GW])
    xn = at("xn", o_b, [P, TT, D])
    sq_b = at("sq_b", o_m, [P, TT * D])
    stat_a = at("stat_a", o_w, [P, 32])
    stat_b = at("stat_b", o_w + 128, [P, 32])

    def first_sp(sp):
        for tt in range(TT):
            sp.dma_start(x[:, tt, :], xv[:, tt, :]).then_inc(s_load, 16)
        sp.dma_start(consts[:, :, :], consts_in).then_inc(s_load, 16)
        sp.dma_start(cols[:, :], cols_in).then_inc(s_load, 16)
        sp.dma_start(rows[:, :], rows_in).then_inc(s_load, 16)

    s_bias = sem("s_bias")

    def first_pool(pool, st):
        pool.wait_ge(s_load, 7 * 16)

    def load_bias(pool, st):
        pool.dma_start(attn_bias[:, :, :, :], bias_in).then_inc(s_bias, 16)

    def first_act(act, st):
        act.wait_ge(s_load, 7 * 16)
        for u in range(SPLIT):
            split_hi(act, u, u, 1)

    def first_dve(dve, st):
        dve.wait_ge(s_load, 7 * 16)
        for u in range(SPLIT):
            split_lo(dve, u, u)

    add_stage(sp=first_sp, act=first_act, dve=first_dve, pe=lambda pe: pe.wait_ge(s_load, 7 * 16), pool=first_pool)
    normalise("n1", x[:, :, :], xn[:, :, :], stat_a[:, 0:TT], stat_b[:, 0:TT], D, sq_b[:, :])
    transposes("t1", lambda tt, c: xn[:, tt, c * P:(c + 1) * P], lambda c: col("ln1", c))

    q_tok = at("q_tok", o_b, [P, TT, 512])
    k_tok = at("k_tok", o_b + 8 * KB, [P, TT, 512])
    v_tok = at("v_tok", o_b + 16 * KB, [P, TT, 512])
    qT = at("qT", o_b + 24 * KB, [P, 4, T])
    kT = at("kT", o_w, [P, 4, T])
    mix = at("mix", o_m, [P, KT, T])
    sq_a = at("sq_a", o_m, [P, 2, TT * 512])
    stat_q = at("stat_q", o_w + 36 * KB, [P, 4, 32])
    qkv = [q_tok, k_tok, v_tok]

    def qkv_out(eng, st, j, ps):
        return nc.scalar.activation(qkv[j // 2][:, :, (j % 2) * UC:(j % 2 + 1) * UC], ps, ACT.Copy)
    dense("qkv", slabs(w_in, 0, 6), "token", qkv_out, "act", pool_part=load_bias)

    def heads64(t):
        return t[:, :, :].rearrange("p t (h e) -> p (t h) e", e=DA)
    with together():
        normalise("nq", heads64(q_tok), heads64(q_tok), stat_q[:, 0, :], stat_q[:, 1, :], DA, sq_a[:, 0, :], extra=DA ** -0.5)
        normalise("nk", heads64(k_tok), heads64(k_tok), stat_q[:, 2, :], stat_q[:, 3, :], DA, sq_a[:, 1, :])
    with together():
        transposes("tq", lambda tt, c: q_tok[:, tt, c * P:(c + 1) * P], lambda c: col("qg"), n_c=4, dst_f32=qT)
        transposes("tk", lambda tt, c: k_tok[:, tt, c * P:(c + 1) * P], lambda c: col("kg"), n_c=4, dst_f32=kT, bank=4)

    def attention():
        DEEP = 4
        logit = at("logit", o_m + 8 * KB, [P, DEEP, 512])
        prob = at("prob", o_b + 8 * KB, [P, DEEP, 512])
        probT = at("probT", o_m, [P, DEEP, TT, P])
        o_tok = at("o_tok", o_b, [P, TT, 512])
        mx = at("mx", o_w + 40 * KB, [P, 32])
        nmx = at("nmx", o_w + 40 * KB + 128, [P, 32])
        rsum = at("rsum", o_w + 40 * KB + 256, [P, 32])
        rinv = at("rinv", o_w + 40 * KB + 384, [P, 32])
        s_logit, s_max, s_exp = local("a_logit"), local("a_max"), local("a_exp")
        s_pt, s_pts, s_av, s_o = local("a_pt"), local("a_pts"), local("a_av"), local("a_o")
        N = HA * TT

        def pe_part(pe):
            def logits(u):
                h, i = divmod(u, TT)
                if u >= DEEP:
                    pe.wait_ge(s_max, u - DEEP + 1)
                r = slice((h % 2) * DA, (h % 2) * DA + DA)
                nc.tensor.matmul(PS[:, u % DEEP, :], qT[r, h // 2, i * P:(i + 1) * P], kT[r, h // 2, :],
                                 start=True, stop=True).then_inc(s_logit, 1)

            def turn(u):
                pe.wait_ge(s_exp, u + 1)
                if u >= 2:
                    pe.wait_ge(s_pts, u - 1)
                for kt in range(TT):
                    last = nc.tensor.transpose(PS[:, 4 + u % 2, kt * P:(kt + 1) * P], prob[:, u % DEEP, kt * P:(kt + 1) * P], ident)
                last.then_inc(s_pt, 1)

            def values(u):
                h, i = divmod(u, TT)
                pe.wait_ge(s_pts, u + 1)
                if i == 0 and h >= 2:
                    pe.wait_ge(s_o, h - 1)
                for kt in range(TT):
                    last = nc.tensor.matmul(PS[:, 6 + h % 2, i * DA:(i + 1) * DA], probT[:, u % DEEP, kt, :],
                                            v_tok[:, kt, h * DA:(h + 1) * DA], start=(kt == 0), stop=(kt == TT - 1))
                last.then_inc(s_av, 1)
            logits(0)
            logits(1)
            for u in range(0, N, 2):
                if u + 2 < N:
                    logits(u + 2)
                    logits(u + 3)
                turn(u)
                turn(u + 1)
                if u:
                    values(u - 2)
                    values(u - 1)
            values(N - 2)
            values(N - 1)

        def act_part(act, st):
            def copy(u):
                act.wait_ge(s_pt, u + 1)
                if u >= DEEP:
                    act.wait_ge(s_av, u - DEEP + 1)
                nc.scalar.activation(probT[:, u % DEEP, :, :].rearrange("p a b -> p (a b)"), PS[:, 4 + u % 2, :], ACT.Copy).then_inc(s_pts, 1)

            def exponentials(u):
                act.wait_ge(s_max, u + 1)
                if u >= DEEP:
                    act.wait_ge(s_pt, u - DEEP + 1)
                nc.scalar.activation(prob[:, u % DEEP, :], logit[:, u % DEEP, :], ACT.Exp, bias=nmx[:, u:u + 1],
                                     accum_out=rsum[:, u:u + 1]).then_inc(s_exp, 1)
            for u in range(0, N, 2):
                exponentials(u)
                exponentials(u + 1)
                if u:
                    copy(u - 2)
                    copy(u - 1)
            copy(N - 2)
            copy(N - 1)

        def dve_part(dve, st):
            def head_out(h):
                dve.wait_ge(s_exp, TT * (h + 1))
                st.then(nc.vector.reciprocal(rinv[:, TT * h:TT * (h + 1)], rsum[:, TT * h:TT * (h + 1)]))
                dve.wait_ge(s_av, TT * (h + 1))
                nc.vector.tensor_tensor(o_tok[:, :, h * DA:(h + 1) * DA],
                                        PS[:, 6 + h % 2, 0:TT * DA].rearrange("p (t e) -> p t e", e=DA),
                                        rinv[:, TT * h:TT * (h + 1)].rearrange("p (t e) -> p t e", e=1).broadcast_to([P, TT, DA]),
                                        ALU.mult).then_inc(s_o, 1)
            dve.wait_ge(s_bias, 16)
            for u in range(N):
                h, i = divmod(u, TT)
                dve.wait_ge(s_logit, u + 1)
                if u >= DEEP:
                    dve.wait_ge(s_exp, u - DEEP + 1)
                k0 = KROWS // 2 - 1 - 2 * i
                st.then(nc.vector.tensor_tensor_reduce(
                    out=logit[:, u % DEEP, :], in0=PS[:, u % DEEP, :],
                    in1=attn_bias[:, h, k0:k0 + GH, :].rearrange("p r c -> p (r c)"),
                    scale=1.0, scalar=-3e38, op0=ALU.add, op1=ALU.max, accum_out=mx[:, u:u + 1]))
                nc.vector.tensor_scalar(nmx[:, u:u + 1], mx[:, u:u + 1], -1.0, None, ALU.mult).then_inc(s_max, 1)
                if u % TT == 3 and u >= 7:
                    head_out((u - 7) // TT)
            head_out(HA - 1)
        add_stage(pe=pe_part, act=act_part, dve=dve_part)
        return o_tok

    o_tok = attention()
    attn_n = at("attn_n", o_b + 8 * KB, [P, TT, 512])
    sq_o = at("sq_o", o_b + 16 * KB, [P, TT * 512])
    ab_w = at("ab_w", o_b + 25 * KB, [P, KT, 16])

    def load_small(tag, w_dram, w_f32):
        small_uses.append(tag)
        add_stage(pool=lambda pool, st: pool.dma_start(w_f32[:, :, :], w_dram).then_inc(s_small, 16))
    with together():
        load_small("ab", w_ab, ab_w)
        normalise("nao", o_tok[:, :, :], attn_n[:, :, :], stat_q[:, 0, 0:TT], stat_q[:, 1, 0:TT], 512, sq_o[:, :])
    transposes("tao", lambda tt, c: attn_n[:, tt, c * P:(c + 1) * P], lambda c: col("attn_out", c), n_c=4, dst_f32=mix)

    conv_in = at("conv_in", o_b, [P, 12, T + CONV - 1])
    z_tok = at("z_tok", o_w, [P, TT, 512])
    ab_wh = at("ab_wh", o_b + 25 * KB + 512, [P, KT, 16], F32R)
    ab_wl = at("ab_wl", o_b + 26 * KB, [P, KT, 16], F32R)
    o_s = o_w + 36 * KB
    ab = at("ab", o_s, [P, TT, 16])

    def small_product(tag, w_f32, w_hi, w_lo, w_rows, n, dst):
        landed = (small_uses.index(tag) + 1) * 16
        s_wh, s_wl, s_p, s_r = local(f"{tag}_wh"), local(f"{tag}_wl"), local(f"{tag}_p"), local(f"{tag}_r")

        def act_part(act, st):
            act.wait_ge(s_small, landed)
            nc.scalar.activation(w_hi[:, :, :], w_f32[:, :, :], ACT.Copy).then_inc(s_wh, 1)

        def dve_part(dve, st):
            dve.wait_ge(s_wh, 1)
            nc.vector.tensor_tensor(w_lo[:, :, :], w_f32[:, :, :], w_hi[:, :, :].bitcast(F32), ALU.subtract).then_inc(s_wl, 1)
            dve.wait_ge(s_p, 1)
            nc.vector.tensor_copy(w_rows[0:n, :], PS[0:n, 7, :]).then_inc(s_r, 1)
            dve.wait_ge(s_p, 2)
            nc.vector.tensor_copy(dst, PS[:, 6, 0:TT * n].rearrange("p (t n) -> p t n", n=n))

        def pe_part(pe):
            pe.wait_ge(s_wl, 1)
            for c in range(KT):
                for k, (a, b) in enumerate(((act_hi, w_hi), (act_hi, w_lo), (act_lo, w_hi))):
                    last = nc.tensor.matmul(PS[0:n, 7, :], b[:, c, :], a[:, c, :], start=(c == 0 and k == 0), stop=(c == KT - 1 and k == 2))
            last.then_inc(s_p, 1)
            pe.wait_ge(s_r, 1)
            for tt in range(TT):
                last = nc.tensor.transpose(PS[:, 6, tt * n:(tt + 1) * n], w_rows[0:n, tt * P:(tt + 1) * P], ident[0:n, 0:n])
            last.then_inc(s_p, 1)
        add_stage(act=act_part, dve=dve_part, pe=pe_part)

    ab_rows = at("ab_rows", o_b + 27 * KB, [P, T])
    small_product("ab", ab_w, ab_wh, ab_wl, ab_rows, 16, ab[:, :, :])

    def dn_out_fn(eng, st, j, ps):
        if j < 6:
            return nc.scalar.activation(conv_in[:, 2 * j:2 * j + 2, 2:2 + T], ps, ACT.Copy)
        return nc.scalar.activation(z_tok[:, :, (j - 6) * UC:(j - 5) * UC], ps, ACT.Copy)

    g = at("g", o_s + 256, [P, TT, 8])
    beta = at("beta", o_s + 384, [P, TT, 8])
    gc = at("gc", o_s + 512, [P, TT, 8])
    bexp = at("bexp", o_s + 640, [P, TT, 8])
    t_a = at("t_a", o_s + 768, [P, TT, 8])
    t_b = at("t_b", o_s + 896, [P, TT, 8])
    t_c = at("t_c", o_s + 1024, [P, TT, 8])
    glast = at("glast", o_s + 1152, [P, 8, TT])
    eglast = at("eglast", o_s + 1280, [P, 8, TT])
    kdsc = at("kdsc", o_s + 1408, [P, 8, TT])
    stat_d = at("stat_d", o_s + 1536, [P, 4, 16])
    rates = at("rates", o_s + 1792, [P, 8])
    conv_o = at("conv_o", o_w + 8 * KB, [P, 12, T])

    def conv_stage():
        s_pads, s_c, s_g0, s_g1 = local("pads"), local("cv_c"), local("cv_g0"), local("cv_g1")

        def pool_part(pool, st):
            nc.gpsimd.memset(conv_in[:, :, 0:2], 0.0)
            nc.gpsimd.memset(conv_in[:, :, T + 2:T + 4], 0.0).then_inc(s_pads, 1)

        def convolve(dve, st, j):
            tiles = (2 * j, 2 * j + 1)
            for i in tiles:
                st(nc.vector.tensor_scalar(conv_o[:, i, :], conv_in[:, i, 0:T], col("conv", i * CONV), None, ALU.mult))
            for w in range(1, CONV):
                for i in tiles:
                    st.wait(st.n - 1 if w < CONV - 1 or i == tiles[0] else st.n)
                    last = nc.vector.scalar_tensor_tensor(conv_o[:, i, :], conv_in[:, i, w:w + T], col("conv", i * CONV + w),
                                                          conv_o[:, i, :], ALU.mult, ALU.add)
                    if w < CONV - 1:
                        st(last)
                    else:
                        last.then_inc(s_c, 1)

        def dve_also(dve, st, j, left):
            if j == 0:
                st.then(nc.vector.tensor_tensor(t_a[:, :, :], ab[:, :, 0:8], middle(row("dt_bias", 8), TT), ALU.add))
                nc.vector.scalar_tensor_tensor(t_b[:, :, :], t_a[:, :, :], -1.0, t_a[:, :, :], ALU.mult, ALU.max).then_inc(s_g0, 1)
                dve.wait_ge(s_pads, 1)
            elif j <= 6:
                dve.wait_ge(evac["act"], left - 1)
                convolve(dve, st, j - 1)
            else:
                dve.wait_ge(s_g1, 4)
                st.then(nc.vector.scalar_tensor_tensor(t_c[:, :, :], t_a[:, :, :], 0.0, t_c[:, :, :], ALU.max, ALU.add))
                nc.vector.scalar_tensor_tensor(g[:, :, :], t_c[:, :, :], -1.0, middle(rates[:, :], TT), ALU.mult, ALU.mult)

        def act_also(act, st, j, left):
            if j == 0:
                act.wait_ge(s_g0, 1)
                nc.scalar.activation(rates[:, :], row("a_log", 8), ACT.Exp).then_inc(s_g1, 1)
                nc.scalar.activation(t_c[:, :, :], t_b[:, :, :], ACT.Exp, scale=-1.0).then_inc(s_g1, 1)
                act.wait_ge(s_g1, 2)
                nc.scalar.activation(t_c[:, :, :], t_c[:, :, :], ACT.Ln, bias=1.0).then_inc(s_g1, 1)
                nc.scalar.activation(beta[:, :, :], ab[:, :, 8:16], ACT.Sigmoid).then_inc(s_g1, 1)
            elif j >= 2:
                for i in (2 * (j - 2), 2 * (j - 2) + 1):
                    act.wait_ge(s_c, i + 1)
                    nc.scalar.activation(conv_o[:, i, :], conv_o[:, i, :], ACT.Silu)
        dense("dn", slabs(w_in, 3 * HA * DA, 8), ["feature"] * 6 + ["token"] * 2, dn_out_fn, "act",
              act_also=act_also, dve_also=dve_also, pool_part=pool_part)

    conv_stage()

    dq_tok = at("dq_tok", o_a, [P, TT, 512])
    dk_tok = at("dk_tok", o_a + 8 * KB, [P, TT, 512])
    dv_tok = at("dv_tok", o_a + 16 * KB, [P, TT, 512])

    def to_tokens():
        s_t, s_c = local("dt_t"), local("dt_c")

        def pe_part(pe):
            for kind in range(3):
                for tt in range(TT):
                    u = kind * TT + tt
                    if u >= 8:
                        pe.wait_ge(s_c, u - 7)
                    for h in range(HD):
                        last = nc.tensor.transpose(PS[:, u % 8, h * DD:(h + 1) * DD], conv_o[:, kind * HD + h, tt * P:(tt + 1) * P], ident)
                    last.then_inc(s_t, 1)

        def act_part(act, st):
            for u in range(3 * TT):
                act.wait_ge(s_t, u + 1)
                dst = (dq_tok, dk_tok, dv_tok)[u // TT]
                nc.scalar.activation(dst[:, u % TT, :], PS[:, u % 8, :], ACT.Copy).then_inc(s_c, 1)
        add_stage(pe=pe_part, act=act_part)
    to_tokens()

    def heads128(t):
        return t[:, :, :].rearrange("p t (h e) -> p (t h) e", e=DD)
    sq_d = at("sq_d", o_w + 8 * KB, [P, TT * 512])
    sq_e = at("sq_e", o_w + 16 * KB, [P, TT * 512])
    with together():
        normalise("ndq", heads128(dq_tok), heads128(dq_tok), stat_d[:, 0, :], stat_d[:, 1, :], DD, sq_d[:, :], eps_scale=1.0, extra=DD ** -0.5)
        normalise("ndk", heads128(dk_tok), heads128(dk_tok), stat_d[:, 2, :], stat_d[:, 3, :], DD, sq_e[:, :], eps_scale=1.0)
    dqT = at("dqT", o_b, [P, HD, T])
    dkT = at("dkT", o_b + 8 * KB, [P, HD, T])
    with together():
        transposes("tdq", lambda tt, c: dq_tok[:, tt, c * P:(c + 1) * P], None, n_c=4, dst_f32=dqT)
        transposes("tdk", lambda tt, c: dk_tok[:, tt, c * P:(c + 1) * P], None, n_c=4, dst_f32=dkT, bank=4)
    KK = at("KK", o_w + 8 * KB, [P, HD, T])
    KQ = at("KQ", o_w + 16 * KB, [P, HD, T])
    dn_o = at("dn_o", o_a, [P, TT, 512])

    def grams():
        s_g, s_gc = local("gr_g"), local("gr_gc")

        def pe_part(pe):
            for b, (rhs) in enumerate((dkT, dqT)):
                for h in range(HD):
                    for tt in range(TT):
                        s = slice(tt * P, (tt + 1) * P)
                        if b == 1 and h >= 2 and tt == 0:
                            pe.wait_ge(s_gc, 4 * b + h - 5)
                        bank = (4 * b + h) % 6
                        last = nc.tensor.matmul(PS[:, bank, s], dkT[:, h, s], rhs[:, h, s], start=True, stop=True)
                    last.then_inc(s_g, 1)
            for tt in range(TT):
                nc.tensor.matmul(PS[:, 6, tt * 8:tt * 8 + 4], const["le"], g[:, tt, 0:4], start=True, stop=True)
                last = nc.tensor.matmul(PS[:, 6, tt * 8 + 4:tt * 8 + 8], const["ge"], g[:, tt, 4:8], start=True, stop=True)
            last.then_inc(s_g, 1)

        def act_part(act, st):
            for b in range(8):
                act.wait_ge(s_g, b + 1)
                dst = (KK, KQ)[b // 4]
                nc.scalar.activation(dst[:, b % 4, :], PS[:, b % 6, :], ACT.Copy).then_inc(s_gc, 1)

        def dve_part(dve, st):
            dve.wait_ge(s_g, 9)
            nc.vector.tensor_copy(gc[:, :, :], PS[:, 6, 0:TT * 8].rearrange("p (t n) -> p t n", n=8))
        add_stage(pe=pe_part, act=act_part, dve=dve_part)
    grams()

    def batch_array(name, offset):
        return at(name, offset, [P, 2, TT, P])
    pw = batch_array("pw", o_a + 24 * KB)
    pwT = batch_array("pwT", o_a + 28 * KB)
    yT = batch_array("yT", o_b + 16 * KB)
    lo_m = batch_array("lo_m", o_b + 20 * KB)
    vT = batch_array("vT", o_b + 24 * KB)
    dec = batch_array("dec", o_b + 28 * KB)
    bv = batch_array("bv", o_w + 24 * KB)
    kbe = batch_array("kbe", o_w + 28 * KB)
    kd = batch_array("kd", o_w + 32 * KB)
    qeT = batch_array("qeT", o_m + 8 * KB)
    qkT = batch_array("qkT", o_m + 12 * KB)
    tinvT, y_m, u_m, wT_m = lo_m, dec, pw, pwT
    state = at("state", o_s + 2048, [P, 2, DD])
    vnew = at("vnew", o_s + 3072, [P, 2, DD])

    def flat(t, h):
        return t[:, h, :, :].rearrange("p a b -> p (a b)")

    def bc(ap, n=TT):
        return ap.rearrange("p (a b) -> p a b", b=1).broadcast_to([P, n, P])

    def delta_batch(d, pair):
        tag = f"d{d}{pair}_"
        heads = (2 * pair, 2 * pair + 1)
        incl, strict = (("le", "gt"), ("ge", "lt"))[d]
        s_tg, s_gr, s_raw, s_exp, s_prep, s_pool = (local(tag + n) for n in ("tg", "gr", "raw", "exp", "prep", "pool"))
        s_mm, s_ea, s_ev = local(tag + "mm"), local(tag + "ea"), local(tag + "ev")
        s_vn, s_pv, s_po, s_st, s_oo = (local(tag + n) for n in ("vn", "pv", "po", "st", "oo"))
        last_col = P - 1 if d == 0 else 0
        dh = [4 * d + h for h in heads]
        order = list(range(TT)) if d == 0 else list(range(TT))[::-1]
        STEPS = [
            ([("t", pw)], [("dve", yT, "eye-"), ("dve", pwT, "copy")], [0, 0]),
            ([(pwT, pw), (pw, pwT)], [("act", pw, "copy"), ("dve", pwT, "copy")], [0, 1]),
            ([(pw, yT), (pwT, pw), (pw, pwT)], [("dve", yT, "add"), ("act", pw, "copy"), ("dve", pwT, "copy")], [0, 1, 2]),
            ([(pw, yT), (pwT, pw)], [("dve", yT, "add"), ("act", pw, "copy")], [0, 1]),
            ([(pw, yT)], [("dve", yT, "add")], [0]),
            ([(yT, lo_m), (lo_m, yT), ("t", yT)],
             [("act", pw, "copy"), ("dve", pwT, "copy"), ("dve", vT, "eye-"), ("act", y_m, "copy")], [0, 1, 1, 2]),
            ([(pwT, pw), (pw, pwT)], [("act", pw, "copy"), ("dve", pwT, "copy")], [0, 1]),
            ([(pw, vT), (pwT, pw)], [("dve", vT, "add"), ("act", pw, "copy")], [0, 1]),
            ([(pw, vT)], [("dve", vT, "add")], [0]),
            ([(y_m, vT)], [("act", tinvT, "copy")], [0]),
            ([(tinvT, bv), (kbe, tinvT)], [("act", u_m, "copy"), ("dve", wT_m, "copy")], [0, 1]),
        ]
        n_act = [sum(k[0] == "act" for k in s[1]) for s in STEPS]
        n_dve = [sum(k[0] == "dve" for k in s[1]) for s in STEPS]

        def before(counts, s, hb):
            return 2 * sum(counts[:s]) + (hb + 1) * counts[s]

        def pe_part(pe):
            for hb in range(2):
                pe.wait_ge(s_tg, hb + 1)
                nc.tensor.matmul(PS[:, 6 + hb, :], ones, flat(vT, hb), start=True, stop=True).then_inc(s_gr, 1)
            for s, (products, _, _) in enumerate(STEPS):
                for hb in range(2):
                    if s == 0:
                        pe.wait_ge(s_prep, hb + 1)
                    else:
                        if before(n_act, s - 1, hb):
                            pe.wait_ge(s_ea, before(n_act, s - 1, hb))
                        pe.wait_ge(s_ev, before(n_dve, s - 1, hb))
                    if s == 10:
                        pe.wait_ge(s_pool, 1 + hb)
                    for b, (lhsT, rhs) in enumerate(products):
                        for tt in order:
                            o = PS[:, 3 * hb + b, tt * P:(tt + 1) * P]
                            if isinstance(lhsT, str):
                                last = nc.tensor.transpose(o, rhs[:, hb, tt, :], ident)
                            else:
                                last = nc.tensor.matmul(o, lhsT[:, hb, tt, :], rhs[:, hb, tt, :], start=True, stop=True)
                    last.then_inc(s_mm, 1)
            n_s = len(STEPS) - 1
            for n, tt in enumerate(order):
                for hb in range(2):
                    pe.wait_ge(s_ea, before(n_act, n_s, hb))
                    pe.wait_ge(s_ev, before(n_dve, n_s, hb))
                    if n:
                        pe.wait_ge(s_st, 2 * (n - 1) + hb + 1)
                        nc.tensor.matmul(PS[:, 3 * hb, 0:P], wT_m[:, hb, tt, :], state[:, hb, :], start=True, stop=True).then_inc(s_pv, 1)
                    if n >= 1:
                        pe.wait_ge(s_oo, 2 * (n - 1) + hb + 1)
                if n == 0:
                    pe.wait_ge(s_pool, 6)
                for hb in range(2):
                    pe.wait_ge(s_vn, 2 * n + hb + 1)
                    o = PS[:, 3 * hb + 1, 0:P]
                    if n:
                        nc.tensor.matmul(o, qeT[:, hb, tt, :], state[:, hb, :], start=True, stop=False)
                    nc.tensor.matmul(o, qkT[:, hb, tt, :], vnew[:, hb, :], start=(n == 0), stop=True)
                    nc.tensor.matmul(PS[:, 3 * hb + 2, 0:P], kd[:, hb, tt, :], vnew[:, hb, :], start=True, stop=True).then_inc(s_po, 1)

        def take(eng, st, who, s, hb):
            products, takers, banks = STEPS[s]
            eng.wait_ge(s_mm, 2 * s + hb + 1)
            for (by, dst, how), b in zip(takers, banks):
                if by != who:
                    continue
                ps = PS[:, 3 * hb + b, :]
                out = flat(dst, hb)
                if by == "act":
                    nc.scalar.activation(out, ps, ACT.Copy).then_inc(s_ea, 1)
                elif how == "copy":
                    nc.vector.tensor_copy(out, ps).then_inc(s_ev, 1)
                elif how == "add":
                    nc.vector.tensor_tensor(out, out, ps, ALU.add).then_inc(s_ev, 1)
                else:
                    nc.vector.scalar_tensor_tensor(dst[:, hb, :, :], ps.rearrange("p (a b) -> p a b", b=P), -1.0,
                                                   middle(ident, TT), ALU.mult, ALU.add).then_inc(s_ev, 1)

        def pool_part(pool, st):
            for hb, h in enumerate(heads):
                s = slice(h * DD, (h + 1) * DD)
                nc.gpsimd.tensor_tensor(bv[:, hb, :, :], dv_tok[:, :, s], bc(beta[:, :, dh[hb]]), ALU.mult)
                nc.gpsimd.tensor_tensor(kbe[:, hb, :, :], dk_tok[:, :, s], bc(bexp[:, :, dh[hb]]), ALU.mult).then_inc(s_pool, 1)
            for hb, h in enumerate(heads):
                pool.wait_ge(s_exp, 2 * hb + 4)
                st(nc.gpsimd.tensor_tensor(qkT[:, hb, :, :], qkT[:, hb, :, :], middle(const[incl], TT), ALU.mult))
                nc.gpsimd.tensor_tensor(flat(qeT, hb), flat(qeT, hb), dqT[:, h, :], ALU.mult)
                st.wait()
                nc.gpsimd.tensor_tensor(flat(qkT, hb), flat(qkT, hb), KQ[:, h, :], ALU.mult).then_inc(s_pool, 1)
            pool.wait_ge(s_exp, 8)
            for hb, h in enumerate(heads):
                s = slice(h * DD, (h + 1) * DD)
                nc.gpsimd.tensor_tensor(kd[:, hb, :, :], dk_tok[:, :, s], bc(kdsc[:, dh[hb], :]), ALU.mult).then_inc(s_pool, 1)

        def act_part(act, st):
            for hb in range(2):
                act.wait_ge(s_raw, hb + 1)
                nc.scalar.activation(flat(dec, hb), flat(dec, hb), ACT.Exp, scale=-1.0).then_inc(s_exp, 1)
            for hb in range(2):
                act.wait_ge(s_raw, 3 + hb)
                nc.scalar.activation(flat(qkT, hb), flat(qkT, hb), ACT.Exp).then_inc(s_exp, 1)
                nc.scalar.activation(flat(qeT, hb), PS[:, 6 + hb, :], ACT.Exp).then_inc(s_exp, 1)
            act.wait_ge(s_raw, 6)
            nc.scalar.activation(eglast[:, dh[0]:dh[1] + 1, :], glast[:, dh[0]:dh[1] + 1, :], ACT.Exp).then_inc(s_exp, 1)
            nc.scalar.activation(kdsc[:, dh[0]:dh[1] + 1, :], kdsc[:, dh[0]:dh[1] + 1, :], ACT.Exp).then_inc(s_exp, 1)
            for s in range(len(STEPS)):
                for hb in range(2):
                    if n_act[s]:
                        take(act, st, "act", s, hb)

        def dve_part(dve, st):
            nc_v = nc.vector
            for hb in range(2):
                nc_v.tensor_tensor(vT[:, hb, :, :], middle(const[incl], TT), bc(g[:, :, dh[hb]]), ALU.mult).then_inc(s_tg, 1)
            for hb in range(2):
                dve.wait_ge(s_gr, hb + 1)
                for tt in range(TT):
                    last = nc_v.tensor_scalar(dec[:, hb, tt, :], PS[:, 6 + hb, tt * P:(tt + 1) * P],
                                              gc[:, tt, dh[hb]:dh[hb] + 1], 0.0, ALU.subtract, ALU.max)
                last.then_inc(s_raw, 1)
            for hb in range(2):
                st(nc_v.tensor_copy(glast[:, dh[hb], :], PS[:, 6 + hb, last_col:last_col + (TT - 1) * P + 1:P]))
                for tt in range(TT):
                    last = nc_v.tensor_scalar(qkT[:, hb, tt, :], PS[:, 6 + hb, tt * P:(tt + 1) * P],
                                              gc[:, tt, dh[hb]:dh[hb] + 1], 0.0, ALU.subtract, ALU.min)
                last.then_inc(s_raw, 1)
            for hb in range(2):
                h = heads[hb]
                dve.wait_ge(s_exp, hb + 1)
                st.then(nc_v.tensor_tensor(dec[:, hb, :, :], dec[:, hb, :, :], middle(const[strict], TT), ALU.mult))
                for tt in range(TT):
                    st(nc_v.scalar_tensor_tensor(lo_m[:, hb, tt, :], KK[:, h, tt * P:(tt + 1) * P], beta[:, tt, dh[hb]:dh[hb] + 1],
                                                 dec[:, hb, tt, :], ALU.mult, ALU.mult))
                st.wait()
                st.then(nc_v.tensor_tensor(pw[:, hb, :, :], lo_m[:, hb, :, :], middle(const["diag16"], TT), ALU.mult))
                nc_v.tensor_tensor(flat(lo_m, hb), flat(lo_m, hb), flat(pw, hb), ALU.subtract).then_inc(s_prep, 1)
            for hb in range(2):
                nc_v.tensor_tensor(kdsc[:, dh[hb], :], glast[:, dh[hb], :], gc[:, :, dh[hb]], ALU.subtract).then_inc(s_raw, 1)
            for s in range(len(STEPS)):
                for hb in range(2):
                    if n_dve[s]:
                        take(dve, st, "dve", s, hb)
            dve.wait_ge(s_ea, before(n_act, len(STEPS) - 1, 1))
            for n, tt in enumerate(order):
                for hb in range(2):
                    if n:
                        dve.wait_ge(s_pv, 2 * (n - 1) + hb + 1)
                        nc_v.tensor_tensor(vnew[:, hb, :], u_m[:, hb, tt, :], PS[:, 3 * hb, 0:P], ALU.subtract).then_inc(s_vn, 1)
                    else:
                        nc_v.tensor_copy(vnew[:, hb, :], u_m[:, hb, tt, :]).then_inc(s_vn, 1)
                for hb in range(2):
                    h = heads[hb]
                    dve.wait_ge(s_po, 2 * n + hb + 1)
                    if n:
                        nc_v.scalar_tensor_tensor(state[:, hb, :], state[:, hb, :], eglast[:, dh[hb], tt:tt + 1],
                                                  PS[:, 3 * hb + 2, 0:P], ALU.mult, ALU.add).then_inc(s_st, 1)
                    else:
                        nc_v.tensor_copy(state[:, hb, :], PS[:, 3 * hb + 2, 0:P]).then_inc(s_st, 1)
                    dst = dn_o[:, tt, h * DD:(h + 1) * DD]
                    if d == 0:
                        nc_v.tensor_copy(dst, PS[:, 3 * hb + 1, 0:P]).then_inc(s_oo, 1)
                    else:
                        nc_v.tensor_tensor(dst, dst, PS[:, 3 * hb + 1, 0:P], ALU.add).then_inc(s_oo, 1)
        add_stage(pool=pool_part, pe=pe_part, act=act_part, dve=dve_part)

    def beta_exp():
        s_e = local("be_e")

        def act_part(act, st):
            nc.scalar.activation(t_a[:, :, :], gc[:, :, :], ACT.Exp).then_inc(s_e, 1)

        def dve_part(dve, st):
            dve.wait_ge(s_e, 1)
            nc.vector.tensor_tensor(bexp[:, :, :], t_a[:, :, :], beta[:, :, :], ALU.mult)
        add_stage(act=act_part, dve=dve_part)
    beta_exp()
    for d in range(2):
        for pair in range(2):
            delta_batch(d, pair)

    dn_sq = at("dn_sq", o_b, [P, TT * 512])
    dn_z = at("dn_z", o_b + 8 * KB, [P, TT, 512])
    dn_n = at("dn_n", o_b + 16 * KB, [P, TT, 512])
    normalise("ndo", heads128(dn_o), heads128(dn_n), stat_d[:, 0, :], stat_d[:, 1, :], DD, dn_sq[:, :])

    def gate_z():
        s_z = local("gz")

        def act_part(act, st):
            nc.scalar.activation(dn_z[:, :, :], z_tok[:, :, :], ACT.Silu).then_inc(s_z, 1)

        def dve_part(dve, st):
            dve.wait_ge(s_z, 1)
            nc.vector.tensor_tensor(dn_n[:, :, :], dn_n[:, :, :], dn_z[:, :, :], ALU.mult)
        add_stage(act=act_part, dve=dve_part)
    gate_z()
    mix_d = mix[:, 4:8, :]
    transposes("tdn", lambda tt, c: dn_n[:, tt, c * P:(c + 1) * P], lambda c: col("dn_out"), n_c=4, dst_f32=mix_d)

    def split_into(tag, src, hi, lo):
        s_h = local(f"{tag}_h")

        def act_part(act, st):
            for c in range(0, KT, 2):
                nc.scalar.activation(hi[:, c:c + 2, :], src[:, c:c + 2, :], ACT.Copy).then_inc(s_h, 1)

        def dve_part(dve, st):
            for c in range(0, KT, 2):
                dve.wait_ge(s_h, c // 2 + 1)
                nc.vector.tensor_tensor(lo[:, c:c + 2, :], src[:, c:c + 2, :], hi[:, c:c + 2, :].bitcast(F32), ALU.subtract)
        add_stage(act=act_part, dve=dve_part)
    split_into("smix", mix, act_hi, act_lo)

    def residual_out(eng, st, j, ps):
        s = slice((j % 4) * UC, (j % 4 + 1) * UC)
        return nc.vector.tensor_tensor(x[:, :, s], x[:, :, s], ps, ALU.add)
    dense("wout", slabs(w_out, 0, 4), "token", residual_out, "dve")

    xn2 = at("xn2", o_w, [P, TT, D])
    sq_m = at("sq_m", o_b, [P, TT * D])
    o_r = o_w + 36 * KB
    stat_m = at("stat_m", o_r, [P, 2, TT])
    normalise("n2", x[:, :, :], xn2[:, :, :], stat_m[:, 0, :], stat_m[:, 1, :], D, sq_m[:, :])
    NR = NG + NE
    r_w = at("r_w", o_b, [P, KT, NR])
    r_wh = at("r_wh", o_b + 3 * KB, [P, KT, NR], F32R)
    r_wl = at("r_wl", o_b + 6 * KB, [P, KT, NR], F32R)
    lg = at("lg", o_b + 9 * KB, [P, TT, NR])
    with together():
        load_small("router", w_router, r_w)
        transposes("t2", lambda tt, c: xn2[:, tt, c * P:(c + 1) * P], lambda c: col("ln2", c))
    r_rows = at("r_rows", o_b + 12 * KB, [P, T])
    small_product("router", r_w, r_wh, r_wl, r_rows, NR, lg[:, :, :])

    KOV = SLOTS // blk
    iota = at("iota", o_w + 32 * KB, [P, SLOTS])
    onehot = at("onehot", o_b + 11 * KB, [P, 2, TT, NE])
    both = at("both", o_b + 13 * KB, [P, TT, NE])
    tmp64 = at("tmp64", o_b + 14 * KB, [P, TT, NE])
    table = at("table", o_b + 15 * KB, [P, KOV, NE])
    pos = at("pos", o_b + 31 * KB, [P, TT, NE])
    r8 = at("r8", o_m, [P, 10, TT, 8])
    r1 = at("r1", o_m + 2 * KB, [P, 12, TT])
    ev = at("ev", o_m + 3 * KB, [P, 8, NE])
    kv = at("kv", o_m + 5 * KB, [P, 4, KOV])
    gates = at("gates", o_r + 64, [P, 2, TT])
    dest = at("dest", o_r + 128, [P, 2, TT])
    dest_u = at("dest_u", o_r + 192, [P, 2, TT], U32)
    start_i = at("start_i", o_r + 256, [P, NE], I32)
    over_i = at("over_i", o_r + 512, [P, 2, KOV], I32)
    n_over = at("n_over", o_r + 1024, [P, 1], I32)

    def route():
        s_i, s_e0, s_e1, s_c, s_p = local("rt_i"), local("rt_e0"), local("rt_e1"), local("rt_c"), local("rt_p")
        lgs, tmp8, cand, oh_g, ing, oh1, oh2, rest, eg = (r8[:, i, :, :] for i in range(9))
        gmax, gsel, gsum, v1, v2, i1, i2, e21, den, gp = (r1[:, i, :] for i in range(10))
        cnt, incl, start, nov, oc, ocx, base_e = (ev[:, i, :] for i in range(7))
        iota8 = iota[:, 0:8]

        def bc8(ap):
            return ap.rearrange("p (t e) -> p t e", e=1).broadcast_to([P, TT, 8])

        def pool_part(pool, st):
            nc.gpsimd.iota(iota[:, :], pattern=[[1, SLOTS]], base=0, channel_multiplier=0,
                           allow_small_or_imprecise_dtypes=True).then_inc(s_i, 1)

        def act_part(act, st):
            act.wait_ge(s_e0, 1)
            nc.scalar.activation(eg, tmp8, ACT.Exp).then_inc(s_e1, 1)
            act.wait_ge(s_e0, 2)
            nc.scalar.activation(e21, den, ACT.Exp).then_inc(s_e1, 1)

        def dve_part(dve, st):
            V = nc.vector

            def first_of(values, top, oh, idx):
                st.then(V.tensor_tensor(cand, values, bc8(top), ALU.is_equal))
                st.then(V.scalar_tensor_tensor(cand, cand, -99.0, middle(iota8, TT), ALU.mult, ALU.add))
                st.then(V.tensor_reduce(idx, cand, X_AXIS, ALU.min))
                st.then(V.tensor_scalar(idx, idx, 99.0, None, ALU.add))
                st.then(V.tensor_tensor(oh, middle(iota8, TT), bc8(idx), ALU.is_equal))

            dve.wait_ge(s_i, 1)
            st.then(V.tensor_tensor(lg[:, :, :], lg[:, :, :], middle(row("rb", NR), TT), ALU.add))
            G = lg[:, :, 0:NG]
            st.then(V.tensor_reduce(gmax, G, X_AXIS, ALU.max))
            V.tensor_tensor(tmp8, G, bc8(gmax), ALU.subtract).then_inc(s_e0, 1)
            first_of(G, gmax, oh_g, gsel)
            t4 = tmp64[:, :, :].rearrange("p t (g e) -> p t g e", e=EG)
            st.then(V.tensor_tensor(t4, lg[:, :, NG:NR].rearrange("p t (g e) -> p t g e", e=EG),
                                    oh_g.rearrange("p t (g e) -> p t g e", e=1).broadcast_to([P, TT, NG, EG]), ALU.mult))
            st.then(V.tensor_reduce(ing, t4.rearrange("p t g e -> p t e g"), X_AXIS, ALU.add))
            st.then(V.tensor_reduce(v1, ing, X_AXIS, ALU.max))
            first_of(ing, v1, oh1, i1)
            st.then(V.scalar_tensor_tensor(rest, oh1, -BIG, ing, ALU.mult, ALU.add))
            st.then(V.tensor_reduce(v2, rest, X_AXIS, ALU.max))
            first_of(rest, v2, oh2, i2)
            V.tensor_tensor(den, v2, v1, ALU.subtract).then_inc(s_e0, 1)
            dve.wait_ge(s_e1, 2)
            st.then(V.tensor_reduce(gsum, eg, X_AXIS, ALU.add))
            st.then(V.scalar_tensor_tensor(den, e21, 1.0, gsum, ALU.add, ALU.mult))
            st.then(V.reciprocal(gates[:, 0, :], den))
            st.then(V.tensor_tensor(gates[:, 1, :], gates[:, 0, :], e21, ALU.mult))
            for k, oh in enumerate((oh1, oh2)):
                st(V.tensor_tensor(onehot[:, k, :, :].rearrange("p t (g e) -> p t g e", e=EG),
                                   oh_g.rearrange("p t (g e) -> p t g e", e=1).broadcast_to([P, TT, NG, EG]),
                                   oh.rearrange("p t (g e) -> p t g e", g=1).broadcast_to([P, TT, NG, EG]), ALU.mult))
            st.wait()
            V.tensor_tensor(both[:, :, :], onehot[:, 0, :, :], onehot[:, 1, :, :], ALU.add).then_inc(s_c, 1)
            dve.wait_ge(s_p, 1)
            st.then(V.tensor_copy(cnt, PS[:, 6, 0:NE]))
            st.then(V.memset(base_e, 0.0))
            st.then(V.tensor_tensor_scan(incl, cnt, base_e, 0.0, ALU.add, ALU.add))
            st.then(V.tensor_tensor(start, incl, cnt, ALU.subtract))
            st(V.tensor_copy(start_i[:, :], start))
            st.then(V.tensor_tensor(pos[:, :, :], PS[:, 7, 0:TT * NE].rearrange("p (t e) -> p t e", e=NE), middle(start, TT), ALU.add))
            for k in range(2):
                st.then(V.tensor_tensor(tmp64[:, :, :], pos[:, :, :], onehot[:, k, :, :], ALU.mult))
                st.then(V.tensor_reduce(dest[:, k, :], tmp64[:, :, :], X_AXIS, ALU.add))
            st(V.tensor_copy(dest_u[:, :, :], dest[:, :, :]))
            st.then(V.tensor_scalar(nov, cnt, float(blk), None, ALU.is_gt))
            for m in range(2, T // blk):
                st.then(V.scalar_tensor_tensor(nov, cnt, float(m * blk), nov, ALU.is_gt, ALU.add))
            st.then(V.tensor_tensor_scan(oc, nov, base_e, 0.0, ALU.add, ALU.add))
            st(V.tensor_copy(n_over[:, :], oc[:, NE - 1:NE]))
            st.then(V.tensor_tensor(ocx, oc, nov, ALU.subtract))
            st.then(V.scalar_tensor_tensor(base_e, ocx, float(blk), incl, ALU.mult, ALU.add))
            kk = iota[:, 0:KOV].rearrange("p (k e) -> p k e", e=1).broadcast_to([P, KOV, NE])
            st.then(V.tensor_tensor(table[:, :, :], middle(oc, KOV), kk, ALU.is_le))
            st.then(V.tensor_reduce(kv[:, 0, :], table[:, :, :], X_AXIS, ALU.add))
            st.then(V.tensor_scalar(kv[:, 0, :], kv[:, 0, :], float(NE - 1), None, ALU.min))
            st.then(V.tensor_tensor(table[:, :, :], middle(iota[:, 0:NE], KOV),
                                    kv[:, 0, :].rearrange("p (k e) -> p k e", e=1).broadcast_to([P, KOV, NE]), ALU.is_equal))
            st.then(V.tensor_tensor(table[:, :, :], table[:, :, :], middle(base_e, KOV), ALU.mult))
            st.then(V.tensor_reduce(kv[:, 1, :], table[:, :, :], X_AXIS, ALU.add))
            st.then(V.scalar_tensor_tensor(kv[:, 2, :], iota[:, 0:KOV], -float(blk), kv[:, 1, :], ALU.mult, ALU.add))
            st.then(V.tensor_scalar(kv[:, 2, :], kv[:, 2, :], -float(blk), 0.0, ALU.add, ALU.max))
            st(V.tensor_copy(over_i[:, 0, :], kv[:, 0, :]))
            V.tensor_copy(over_i[:, 1, :], kv[:, 2, :])

        def pe_part(pe):
            pe.wait_ge(s_c, 1)
            for tt in range(TT):
                o = PS[:, 7, tt * NE:(tt + 1) * NE]
                for t2 in range(tt):
                    nc.tensor.matmul(o, ones, both[:, t2, :], start=(t2 == 0), stop=False)
                nc.tensor.matmul(o, const["lt"], both[:, tt, :], start=(tt == 0), stop=True)
            for tt in range(TT):
                last = nc.tensor.matmul(PS[:, 6, 0:NE], ones, both[:, tt, :], start=(tt == 0), stop=(tt == TT - 1))
            last.then_inc(s_p, 1)
        add_stage(pool=pool_part, act=act_part, dve=dve_part, pe=pe_part)
    route()

    tok_hi = at("tok_hi", o_a, [P, TT, D], F32R)
    tok_lo = at("tok_lo", o_a + 16 * KB, [P, TT, D], F32R)
    sel = at("sel", o_w + 16 * KB, [P, TT, SLOTS], F32R)
    sel_t = at("sel_t", o_b, [P, TT, SLOTS])
    sorted_h = at("sorted_h", o_b, [P, KT, SLOTS + blk])

    def select():
        s_h, s_first = local("sl_h"), local("sl_first")

        def act_part(act, st):
            for tt in range(TT):
                nc.scalar.activation(tok_hi[:, tt, :], xn2[:, tt, :], ACT.Copy).then_inc(s_h, 1)

        def dve_part(dve, st):
            for tt in range(TT):
                dve.wait_ge(s_h, tt + 1)
                nc.vector.tensor_tensor(tok_lo[:, tt, :], xn2[:, tt, :], tok_hi[:, tt, :].bitcast(F32), ALU.subtract)
            st.then(nc.vector.tensor_scalar(sel_t[:, TT - 1, :], iota[:, :], dest[:, 0, TT - 1:TT], None, ALU.is_equal))
            for tt in (TT - 1, *range(TT - 1)):
                if tt < TT - 1:
                    dve.wait_ge(s_first, tt + 1)
                nc.vector.scalar_tensor_tensor(sel[:, tt, :], iota[:, :], dest[:, 1, tt:tt + 1], sel_t[:, tt, :],
                                               ALU.is_equal, ALU.add)

        def pool_part(pool, st):
            for tt in range(TT - 1):
                nc.gpsimd.tensor_scalar(sel_t[:, tt, :], iota[:, :], dest[:, 0, tt:tt + 1], None, ALU.is_equal).then_inc(s_first, 1)
        add_stage(act=act_part, dve=dve_part, pool=pool_part)
    select()

    def sort_tokens():
        s_b, s_e = local("so_b"), local("so_e")

        def pool_part(pool, st):
            nc.gpsimd.memset(sorted_h[:, :, SLOTS:SLOTS + blk], 0.0)

        def pe_part(pe):
            for u in range(2 * KT):
                c, half = divmod(u, 2)
                if u >= 8:
                    pe.wait_ge(s_e, u - 7)
                for tt in range(TT):
                    for k, src in enumerate((tok_hi, tok_lo)):
                        last = nc.tensor.matmul(PS[:, u % 8, :], src[:, tt, c:D:KT], sel[:, tt, half * 512:(half + 1) * 512],
                                                start=(tt == 0 and k == 0), stop=(tt == TT - 1 and k == 1))
                last.then_inc(s_b, 1)

        def act_part(act, st):
            for u in range(2 * KT):
                c, half = divmod(u, 2)
                act.wait_ge(s_b, u + 1)
                nc.scalar.activation(sorted_h[:, c, half * 512:(half + 1) * 512], PS[:, u % 8, :], ACT.Copy,
                                     scale=col("ln2_i", c)).then_inc(s_e, 1)
        add_stage(pool=pool_part, pe=pe_part, act=act_part)
    sort_tokens()

    st_hi = at("st_hi", o_a, [P, 2, KT, P], F32R)
    st_lo = at("st_lo", o_a + 8 * KB, [P, 2, KT, P], F32R)
    y_sb = at("y_sb", o_a + 16 * KB, [P, 4, D])
    g_sb = at("g_sb", o_w, [P, 2, DE])
    hid = at("hid", o_w + 2 * KB, [P, 2, DE])
    hT_hi = at("hT_hi", o_w + 4 * KB, [P, 2, 2, P], F32R)
    hT_lo = at("hT_lo", o_w + 6 * KB, [P, 2, 2, P], F32R)
    y_sorted = nc.dram_tensor("y_sorted", [SLOTS + blk, D], F32).ap()
    y_store = [sem(f"y_store{i}") for i in range(4)]
    s_y2 = sem("y_over")
    BODY = 4

    def experts():
        u0 = wide_from["u"] = Stream.n
        Stream.n += 3 * NE
        assert u0 % SPLIT == 0 and 3 * NE % WIDE == 0
        s_z, s_stat, s_silu, s_hid, s_tr, s_hh, s_hl = (local("ex_" + n) for n in ("z", "stat", "silu", "hid", "tr", "hh", "hl"))
        s_ya, s_yd = sem("ex_ya"), sem("ex_yd")
        s_cp = local("ex_cp")

        class At:

            def __init__(self, q, p):
                self.p, self.q = p, q
                self.e = q * BODY + p
                self.first = isinstance(q, int)

            def unit(self, k):
                if self.first:
                    u = u0 + 3 * self.e - 1 + k if self.e else u0 + k
                    u = min(u, u0 + 3 * NE - 1)
                    return u, u, u // RAW + 1
                s = u0 + 3 * self.p - 1 + k
                return s, self.q * (3 * BODY) + s, self.q * 3 + s // RAW + 1

            def ahead(self, k):
                if self.first:
                    u = self.unit(k)[0] + WIDE
                    return u, u, u // RAW + 1
                s = u0 + 3 * self.p - 1 + k + WIDE
                return s, self.q * (3 * BODY) + s, self.q * 3 + s // RAW + 1

            def had(self, n):
                return not self.first or self.e >= n

        def each(eng, body):
            for e in range(2 * BODY):
                body(At(e // BODY, e % BODY))
            with eng.Fori(2, NE // BODY) as q:
                for p in range(BODY):
                    body(At(q, p))

        last = At(NE // BODY, 0)

        def sp_part(sp):
            def store(e, slot, before, filled):
                sp.wait_ge(s_ya, e + 1)
                sp.wait_ge(s_yd, e + 1)
                pass_wait(sp, "sp")
                if filled is not None:
                    sp.wait_ge(y_store[before], filled)
                    pass_wait(sp, "sp")
                n = sp.value_load(start_i[0:1, bass.ds(e, 1)], min_val=0, max_val=SLOTS)
                sp.dma_start(y_sorted[bass.ds(n, blk), :], y_sb[0:blk, slot, :]).then_inc(y_store[slot], 16)

            def body(a):
                for k, w in enumerate((w_gate, w_up)):
                    s, u, _ = a.unit(k)
                    load_unit(sp, s, u, None, w[a.e].rearrange("(p c) n -> p (c n)", c=KT) if a.first
                              else w[bass.ds(a.e, 1)].rearrange("o (p c) n -> p (o c n)", c=KT))
                if a.had(1):
                    s, u, _ = a.unit(2)
                    load_unit(sp, s, u, ("p (j n) -> p j n", dict(j=2)), w_down[a.e - 1].rearrange("(j p) n -> p j n", p=P) if a.first
                              else w_down[bass.ds(a.e - 1, 1)].rearrange("o (j p) n -> p (o j) n", p=P))
                if a.had(4):
                    filled = (a.q if a.p else a.q - 1) * 16
                    store(a.e - 4, a.p, (a.p - 1) % 4, None if a.first and a.e == 4 else filled)
            each(sp, body)
            s, u, _ = last.unit(2)
            load_unit(sp, s, u, ("p (j n) -> p j n", dict(j=2)), w_down[NE - 1].rearrange("(j p) n -> p j n", p=P))
            nxt = iter(slabs(w_in2, 0, RAW))
            for e in range(NE - 4, NE):
                store(e, e % 4, (e - 1) % 4, (e - 1) // 4 * 16 + 16)
                for _ in range({0: 2, 2: 2}.get(e % 4, 0)):
                    s += 1
                    load_unit(sp, s, s, ("p (c n) -> p c n", dict(c=KT)), next(nxt).rearrange("(c p) n -> p c n", p=P))

        def pool_part(pool, st):
            nc.gpsimd.memset(st_hi[:, :, :, blk:P].bitcast(F32), 0.0)
            nc.gpsimd.memset(st_lo[:, :, :, blk:P].bitcast(F32), 0.0).then_inc(s_z, 1)

            def body(a):
                if a.had(2):
                    pool.wait_ge(pe_unit, a.e * 3 + (u0 - 5) if not a.first or a.e > 2 else u0 + 2)
                b = a.p % 2
                n = pool.value_load(start_i[0:1, bass.ds(a.e, 1)], min_val=0, max_val=SLOTS)
                src = sorted_h[:, :, bass.ds(n, blk)]
                nc.gpsimd.tensor_copy(st_hi[:, b, :, 0:blk], src).then_inc(s_cp, 1)
                pool.wait_ge(s_cp, a.e + 1)
                pass_wait(pool, "pool")
                nc.gpsimd.tensor_tensor(st_lo[:, b, :, 0:blk], src, st_hi[:, b, :, 0:blk].bitcast(F32), ALU.subtract).then_inc(s_stat, 1)
            each(pool, body)

        def turn(pe, e, b, had_one):
            pe.wait_ge(s_hid, e + 1)
            if had_one:
                pe.wait_ge(s_hl, e)
            for j in range(2):
                i = nc.tensor.transpose(PS[:, 2, j * P:(j + 1) * P], hid[:, b, j * P:(j + 1) * P], ident)
            i.then_inc(s_tr, 1)

        def down(pe, e, b, s, u, had_two):
            pe.wait_ge(lo_ready, u + 1)
            pe.wait_ge(s_hl, e + 1)
            if had_two:
                pe.wait_ge(s_ya, e - 1)
                pe.wait_ge(s_yd, e - 1)
            h, l = (w.rearrange("p (j n) -> p j n", j=2) for w in parts(s, True))
            for half in range(2):
                c = slice(half * 512, (half + 1) * 512)
                for j in range(2):
                    for k, (x_, w_) in enumerate(((hT_hi, h), (hT_hi, l), (hT_lo, h))):
                        i = nc.tensor.matmul(PS[:, 3 + 2 * b + half, :], x_[:, b, j, :], w_[:, j, c],
                                             start=(j == 0 and k == 0), stop=(j == 1 and k == 2))
            i.then_inc(pe_unit, 1)

        def pe_part(pe):
            pe.wait_ge(s_z, 1)

            def product(a, k):
                s, u, _ = a.unit(k)
                b = a.p % 2
                pe.wait_ge(lo_ready, u + 1)
                h, l = (w.rearrange("p (c n) -> p c n", c=KT) for w in parts(s, True))
                for c in range(KT):
                    for m, (x_, w_) in enumerate(((st_hi, h), (st_hi, l), (st_lo, h))):
                        i = nc.tensor.matmul(PS[:, b, k * DE:(k + 1) * DE], x_[:, b, c, :], w_[:, c, :],
                                             start=(c == 0 and m == 0), stop=(c == KT - 1 and m == 2))
                i.then_inc(pe_unit, 1)

            def body(a):
                pe.wait_ge(s_stat, a.e + 1)
                if a.had(2):
                    pe.wait_ge(s_hid, a.e - 1)
                product(a, 0)
                if a.had(1):
                    turn(pe, a.e - 1, (a.p - 1) % 2, a.had(2))
                product(a, 1)
                if a.had(1):
                    s, u, _ = a.unit(2)
                    down(pe, a.e - 1, (a.p - 1) % 2, s, u, a.had(3))
            each(pe, body)
            turn(pe, NE - 1, 1, True)
            s, u, _ = last.unit(2)
            down(pe, NE - 1, 1, s, u, True)

        def act_hid(act, a):
            b = (a.p - 1) % 2
            act.wait_ge(s_tr, a.e)
            if a.had(3):
                act.wait_ge(pe_unit, a.e * 3 + (u0 - 4))
            nc.scalar.activation(hT_hi[:, b, :, :].rearrange("p j n -> p (j n)"), PS[:, 2, 0:DE], ACT.Copy).then_inc(s_hh, 1)

        def y_out(eng, a, half, s_y):
            b, slot = (a.p - 1) % 2, (a.p - 1) % 4
            eng.wait_ge(pe_unit, a.unit(2)[1] + 1)
            if a.had(5):
                eng.wait_ge(y_store[slot], (a.q - (1 if a.p == 0 else 0)) * 16)
            c = slice(half * 512, (half + 1) * 512)
            src, dst = PS[0:blk, 3 + 2 * b + half, :], y_sb[0:blk, slot, c]
            (nc.scalar.activation(dst, src, ACT.Copy) if half == 0 else nc.vector.tensor_copy(dst, src)).then_inc(s_y, 1)

        def act_part(act, st):
            def body(a):
                if a.had(1):
                    act_hid(act, a)
                split_hi(act, *a.ahead(0), wide=True)
                act.wait_ge(pe_unit, a.unit(1)[1] + 1)
                if a.had(2):
                    act.wait_ge(s_hid, a.e - 1)
                b = a.p % 2
                nc.scalar.activation(g_sb[:, b, :], PS[:, b, 0:DE], ACT.Silu).then_inc(s_silu, 1)
                split_hi(act, *a.ahead(1), wide=True)
                if a.had(1):
                    split_hi(act, *a.ahead(2), wide=True)
                    y_out(act, a, 0, s_ya)
            split_hi(act, u0 + SPLIT, u0 + SPLIT, (u0 + SPLIT) // RAW + 1, wide=True)
            each(act, body)
            act_hid(act, last)
            y_out(act, last, 0, s_ya)

        def dve_hid(dve, a):
            b = (a.p - 1) % 2
            dve.wait_ge(s_hh, a.e)
            nc.vector.tensor_tensor(hT_lo[:, b, :, :].rearrange("p j n -> p (j n)"), PS[:, 2, 0:DE],
                                    hT_hi[:, b, :, :].rearrange("p j n -> p (j n)").bitcast(F32), ALU.subtract).then_inc(s_hl, 1)

        def dve_part(dve, st):
            def body(a):
                if a.had(1):
                    dve_hid(dve, a)
                split_lo(dve, *a.ahead(0)[:2], wide=True)
                dve.wait_ge(s_silu, a.e + 1)
                dve.wait_ge(pe_unit, a.unit(1)[1] + 1)
                if a.had(2):
                    dve.wait_ge(s_tr, a.e - 1)
                b = a.p % 2
                nc.vector.tensor_tensor(hid[:, b, :], g_sb[:, b, :], PS[:, b, DE:2 * DE], ALU.mult).then_inc(s_hid, 1)
                split_lo(dve, *a.ahead(1)[:2], wide=True)
                if a.had(1):
                    split_lo(dve, *a.ahead(2)[:2], wide=True)
                    y_out(dve, a, 1, s_yd)
            split_lo(dve, u0 + SPLIT, u0 + SPLIT, wide=True)
            each(dve, body)
            dve_hid(dve, last)
            y_out(dve, last, 1, s_yd)
        add_stage(sp=sp_part, pool=pool_part, pe=pe_part, act=act_part, dve=dve_part)
    experts()

    ov_w = at("ov_w", o_w + 8 * KB, [P, 3, UNIT])
    ov_st = at("ov_st", o_a, [P, KT, blk])
    ov_g = at("ov_g", o_w, [P, DE])
    ov_h = at("ov_h", o_w + KB, [P, DE])
    ov_hT = at("ov_hT", o_w + 2 * KB, [P, 2, P])
    ov_y = at("ov_y", o_a + 16 * KB, [P, D])

    def extra_blocks():
        s_w, s_st, s_gu, s_si, s_hi2, s_tr, s_ht, s_dn, s_y, s_yo = (
            sem("ov_" + n) for n in ("w", "st", "gu", "si", "hid", "tr", "ht", "dn", "y", "yo"))

        def each(eng, body):
            n = eng.value_load(n_over[0:1, 0:1], min_val=0, max_val=KOV)
            with eng.If(n > 0):
                with eng.Fori(0, n) as k:
                    body(k)
                eng.drain()
            eng.drain()

        def sp_part(sp):
            for i in range(4):
                sp.wait_ge(y_store[i], NE // 4 * 16)
            for name in ("pe", "act", "dve", "pool"):
                sp.wait_ge(done[name], stage_no)

            def body(k):
                e = sp.value_load(over_i[0:1, 0, bass.ds(k, 1)], min_val=0, max_val=NE - 1)
                sp.wait_ge(s_dn, k + 1)
                pass_wait(sp, "sp")
                for i, w in enumerate((w_gate, w_up)):
                    sp.dma_start(ov_w[:, i, :], w[bass.ds(e, 1)].rearrange("o (p c) n -> p (o c n)", c=KT)).then_inc(s_w, 16)
                sp.dma_start(ov_w[:, 2, :].rearrange("p (j n) -> p j n", j=2),
                             w_down[bass.ds(e, 1)].rearrange("o (j p) n -> p (o j) n", p=P)).then_inc(s_w, 16)
                sp.wait_ge(s_y, k + 1)
                pass_wait(sp, "sp")
                n = sp.value_load(over_i[0:1, 1, bass.ds(k, 1)], min_val=0, max_val=SLOTS)
                sp.dma_start(y_sorted[bass.ds(n, blk), :], ov_y[0:blk, :]).then_inc(s_y2, 16)
                sp.wait_ge(s_y2, k * 16 + 16)
                sp.sem_inc(s_yo, 1)
            sp.sem_inc(s_yo, 1)
            each(sp, body)

        def pool_part(pool, st):
            def body(k):
                pool.wait_ge(s_gu, k + 1)
                n = pool.value_load(over_i[0:1, 1, bass.ds(k, 1)], min_val=0, max_val=SLOTS)
                nc.gpsimd.tensor_copy(ov_st[:, :, :], sorted_h[:, :, bass.ds(n, blk)]).then_inc(s_st, 1)
            each(pool, body)

        def pe_part(pe):
            def body(k):
                pe.wait_ge(s_w, k * 48 + 48)
                pe.wait_ge(s_st, k + 1)
                for i in range(2):
                    w = ov_w[:, i, :].rearrange("p (c n) -> p c n", c=KT)
                    for c in range(KT):
                        last = nc.tensor.matmul(PS[0:blk, 0, i * DE:(i + 1) * DE], ov_st[:, c, :], w[:, c, :], start=(c == 0), stop=(c == KT - 1))
                last.then_inc(s_gu, 1)
                pe.wait_ge(s_hi2, k + 1)
                pass_wait(pe, "pe")
                for j in range(2):
                    last = nc.tensor.transpose(PS[:, 2, j * blk:(j + 1) * blk], ov_h[0:blk, j * P:(j + 1) * P], ident[0:blk, 0:blk])
                last.then_inc(s_tr, 1)
                pe.wait_ge(s_ht, k + 1)
                w = ov_w[:, 2, :].rearrange("p (j n) -> p j n", j=2)
                for half in range(2):
                    for j in range(2):
                        last = nc.tensor.matmul(PS[0:blk, 3 + half, :], ov_hT[:, j, 0:blk], w[:, j, half * 512:(half + 1) * 512], start=(j == 0), stop=(j == 1))
                last.then_inc(s_dn, 1)
            pe.sem_inc(s_gu, 1)
            pe.sem_inc(s_dn, 1)
            each(pe, body)

        def act_part(act, st):
            def body(k):
                act.wait_ge(s_gu, k + 2)
                nc.scalar.activation(ov_g[0:blk, :], PS[0:blk, 0, 0:DE], ACT.Silu).then_inc(s_si, 1)
                act.wait_ge(s_tr, k + 1)
                nc.scalar.activation(ov_hT[:, :, 0:blk], PS[:, 2, 0:2 * blk].rearrange("p (j n) -> p j n", j=2), ACT.Copy).then_inc(s_ht, 1)
            each(act, body)

        def dve_part(dve, st):
            def body(k):
                dve.wait_ge(s_si, k + 1)
                nc.vector.tensor_tensor(ov_h[0:blk, :], ov_g[0:blk, :], PS[0:blk, 0, DE:2 * DE], ALU.mult).then_inc(s_hi2, 1)
                dve.wait_ge(s_dn, k + 2)
                dve.wait_ge(s_yo, k + 1)
                nc.vector.tensor_copy(ov_y[0:blk, :].rearrange("p (a b) -> p a b", a=2), PS[0:blk, 3:5, :]).then_inc(s_y, 1)
            each(dve, body)
        stage_no = len(stages)
        add_stage(sp=sp_part, pool=pool_part, pe=pe_part, act=act_part, dve=dve_part)
        return s_yo
    s_yo = extra_blocks()

    y_rows = at("y_rows", o_b, [P, 2, TT, D])

    def combine():
        s_gather, s_go = [sem(f"cb_g{tt}") for tt in range(TT)], sem("cb_go")

        def sp_part(sp):
            sp.drain().then_inc(s_go, 1)

        def pool_part(pool, st):
            for i in range(4):
                pool.wait_ge(y_store[i], NE // 4 * 16)
            pool.wait_ge(s_go, 1)
            for tt in range(TT):
                for k in range(2):
                    pool.indirect_dma_start(y_rows[:, k, tt, :], None, y_sorted[0:SLOTS, :],
                                            bass.IndirectOffsetOnAxis(ap=dest_u[:, k, tt:tt + 1], axis=0)).then_inc(s_gather[tt], 16)

        def dve_part(dve, st):
            for tt in range(TT):
                dve.wait_ge(s_gather[tt], 32)
                for k in range(2):
                    st.then(nc.vector.scalar_tensor_tensor(x[:, tt, :], y_rows[:, k, tt, :], gates[:, k, tt:tt + 1], x[:, tt, :],
                                                           ALU.mult, ALU.add))
        add_stage(sp=sp_part, pool=pool_part, dve=dve_part)
    combine()

    C_Q, C_K, C_V, C_O = 0, 1024, 2048, 3072
    C_SCB = 4 * D + 2 * HM
    C_SCC, C_SCU, C_SBQ, C_SBK, C_SBV, C_GML, C_GSC, C_GSB = (C_SCB + D * i for i in range(1, 9))
    xn3 = at("xn3", o_w, [P, TT, D])
    sq3 = at("sq3", o_w + 16 * KB, [P, TT * D])
    stat3 = at("stat3", o_w + 40 * KB + 1400 // 32 * 32, [P, 2, TT])

    def hidden(tag, gain, also=lambda: None):
        with together():
            also()
            normalise(tag + "n", x[:, :, :], xn3[:, :, :], stat3[:, 0, :], stat3[:, 1, :], D, sq3[:, :])
        transposes(tag + "t", lambda tt, c: xn3[:, tt, c * P:(c + 1) * P], lambda c: col(gain, c))

    mq = at("mq", o_b, [P, KT, T])
    mk = at("mk", o_b + 16 * KB, [P, KT, T])
    kw = at("kw", o_m, [P, TT, D])
    VA = DM + 1
    v_aug = at("v_aug", o_w, [P, TT, HM, VA])
    o_so = o_w + (TT * HM * VA * 4 + 31) // 32 * 32
    so = at("so", o_so, [P, TT, D])
    Rb = at("Rb", o_so + 16 * KB, [P, HM, T])
    o_ms = o_so + 24 * KB
    gt = at("gt", o_ms, [P, TT, 8])
    lf = at("lf", o_ms + 128, [P, TT, HM])
    lt = at("lt", o_ms + 192, [P, TT, HM])
    ucol = at("ucol", o_ms + 256, [P, TT, HM])
    emcol = at("emcol", o_ms + 320, [P, TT, HM])
    rlast = at("rlast", o_ms + 384, [P, TT, HM])
    wst = at("wst", o_ms + 448, [P, TT, HM])
    stat_y = at("stat_y", o_ms + 512, [P, 2, 16])
    den_s = at("den_s", o_ms + 640, [P, 4])
    g2w = at("g2w", o_so + 16 * KB, [P, KT, 8])
    g2h = at("g2h", o_so + 17 * KB, [P, KT, 8], F32R)
    g2l = at("g2l", o_so + 18 * KB, [P, KT, 8], F32R)
    g2r = at("g2r", o_so + 19 * KB, [P, T])
    hidden("h2a", "mix2", lambda: load_small("g2", w_gates2, g2w))
    small_product("g2", g2w, g2h, g2l, g2r, 8, gt[:, :, :])

    def ml_out(eng, st, j, ps):
        k, j = divmod(j, 4)
        if k < 2:
            return nc.scalar.activation((mq, mk)[k][:, 2 * j:2 * j + 2, :], ps, ACT.Copy)
        if k == 2:
            return nc.scalar.activation(v_aug[:, :, j, 0:DM], ps, ACT.Copy)
        return nc.scalar.activation(so[:, :, j * DM:(j + 1) * DM], ps, ACT.Sigmoid)
    dense("ml", slabs(w_in2, C_Q, 16), ["feature"] * 8 + ["token"] * 8, ml_out, "act", loaded=RAW)

    ri = at("ri", o_a, [P, T])
    rlf = at("rlf", o_a + 2 * KB, [P, T])
    rz = at("rz", o_a + 4 * KB, [P, T])
    rcum = at("rcum", o_a + 6 * KB, [P, T])
    rR = at("rR", o_a + 8 * KB, [P, T])
    rm = at("rm", o_a + 10 * KB, [P, T])
    sel4 = at("sel4", o_a + 12 * KB, [P, HM, P])

    def ml_rows():
        s_a, s_e, s_l, s_t, s_r, s_b, s_f = (local("mr_" + n) for n in ("a", "e", "l", "t", "r", "b", "f"))

        def pool_part(pool, st):
            nc.gpsimd.memset(v_aug[:, :, :, DM:VA], 1.0)

        def dve_part(dve, st):
            V = nc.vector
            st.then(V.tensor_tensor(gt[:, :, :], gt[:, :, :], middle(row("b_if", 8), TT), ALU.add))
            V.scalar_tensor_tensor(lt[:, :, :], gt[:, :, HM:2 * HM], -1.0, gt[:, :, HM:2 * HM], ALU.mult, ALU.max).then_inc(s_a, 1)
            st(V.memset(rz[0:HM, :], 0.0))
            st(V.tensor_copy(sel4[0:HM, :, :], ident[0:HM, 0:HM].rearrange("p (h m) -> p h m", m=1).broadcast_to([HM, HM, P])))
            dve.wait_ge(s_e, 2)
            V.scalar_tensor_tensor(lf[:, :, :], gt[:, :, HM:2 * HM], 0.0, lt[:, :, :], ALU.min, ALU.subtract).then_inc(s_l, 1)
            dve.wait_ge(s_t, 1)
            st(V.tensor_copy(ri[0:HM, :], PS[0:HM, 0, :]))
            st.then(V.tensor_copy(rlf[0:HM, :], PS[0:HM, 1, :]))
            st.then(V.tensor_tensor_scan(rcum[0:HM, :], rlf[0:HM, :], rz[0:HM, :], 0.0, ALU.add, ALU.add))
            st.then(V.tensor_tensor(ri[0:HM, :], ri[0:HM, :], rcum[0:HM, :], ALU.subtract))
            st.then(V.tensor_tensor_scan(rR[0:HM, :], ri[0:HM, :], ri[0:HM, :], 0.0, ALU.max, ALU.max))
            V.tensor_tensor(rm[0:HM, :], rcum[0:HM, :], rR[0:HM, :], ALU.add).then_inc(s_r, 1)
            dve.wait_ge(s_b, 1)
            uc = PS[:, 6, 0:16].rearrange("p (t h) -> p t h", h=HM)
            mc = PS[:, 6, 16:32].rearrange("p (t h) -> p t h", h=HM)
            st(V.tensor_copy(ucol[:, :, :], uc))
            st(V.tensor_copy(emcol[:, :, :], mc))
            dve.wait_ge(s_f, 4)
            st.then(V.tensor_copy(rlast[:, :, :], Rb[:, :, P - 1:T:P].rearrange("p h t -> p t h")))
            V.tensor_tensor(wst[:, :, :], ucol[:, :, :], rlast[:, :, :], ALU.subtract).then_inc(s_r, 1)

        def act_part(act, st):
            act.wait_ge(s_a, 1)
            nc.scalar.activation(lt[:, :, :], lt[:, :, :], ACT.Exp, scale=-1.0).then_inc(s_e, 1)
            act.wait_ge(s_e, 1)
            nc.scalar.activation(lt[:, :, :], lt[:, :, :], ACT.Ln, bias=1.0).then_inc(s_e, 1)
            act.wait_ge(s_b, 2)
            for h in range(HM):
                nc.scalar.activation(Rb[:, h, :], PS[:, 2 + h, :], ACT.Copy).then_inc(s_f, 1)
            act.wait_ge(s_r, 2)
            nc.scalar.activation(wst[:, :, :], wst[:, :, :], ACT.Exp)
            nc.scalar.activation(emcol[:, :, :], emcol[:, :, :], ACT.Exp, scale=-1.0)

        def pe_part(pe):
            pe.wait_ge(s_l, 1)
            for b, src in enumerate((gt, lf)):
                for tt in range(TT):
                    last = nc.tensor.transpose(PS[0:HM, b, tt * P:(tt + 1) * P], src[:, tt, 0:HM], ident)
            last.then_inc(s_t, 1)
            pe.wait_ge(s_r, 1)
            for b, src in enumerate((ri, rm)):
                for tt in range(TT):
                    last = nc.tensor.transpose(PS[:, 6, b * 16 + tt * HM:b * 16 + (tt + 1) * HM], src[0:HM, tt * P:(tt + 1) * P], ident[0:HM, 0:HM])
            last.then_inc(s_b, 1)
            for h in range(HM):
                last = nc.tensor.matmul(PS[:, 2 + h, :], sel4[0:HM, h, :], rR[0:HM, :], start=True, stop=True)
            last.then_inc(s_b, 1)
        add_stage(pool=pool_part, dve=dve_part, act=act_part, pe=pe_part)
    ml_rows()

    def ml_keys():
        s_t, s_c = local("mk_t"), local("mk_c")

        def pe_part(pe):
            for u in range(TT * HM):
                tt, h = divmod(u, HM)
                if u >= 7:
                    pe.wait_ge(s_c, u - 6)
                for k in range(2):
                    last = nc.tensor.transpose(PS[:, u % 7, k * P:(k + 1) * P], mk[:, 2 * h + k, tt * P:(tt + 1) * P], ident)
                last.then_inc(s_t, 1)

        def act_part(act, st):
            for u in range(TT * HM):
                tt, h = divmod(u, HM)
                act.wait_ge(s_t, u + 1)
                nc.scalar.activation(kw[:, tt, h * DM:(h + 1) * DM], PS[:, u % 7, 0:DM], ACT.Copy, scale=wst[:, tt, h:h + 1]).then_inc(s_c, 1)
        add_stage(pe=pe_part, act=act_part)
    ml_keys()

    y_tok = at("y_tok", o_a, [P, TT, D])
    cst = at("cst", o_a + 16 * KB, [P, 2, 2, VA])
    sT = at("sT", o_a + 24 * KB, [P, 2, TT, P])
    abc = at("abc", o_a + 28 * KB, [P, 2, TT - 1, P])
    SC = DM ** -0.5

    def ml_pair(pair):
        tag = f"m{pair}_"
        s_sc, s_wi, s_ex, s_sT, s_q, s_num, s_cu, s_cs, s_y = (local(tag + n) for n in ("sc", "wi", "ex", "sT", "q", "num", "cu", "cs", "y"))
        heads = (2 * pair, 2 * pair + 1)

        def pe_part(pe):
            for hb, h in enumerate(heads):
                for i in range(TT):
                    s = slice(i * P, (i + 1) * P)
                    for k in range(2):
                        last = nc.tensor.matmul(PS[:, hb, s], mk[:, 2 * h + k, s], mq[:, 2 * h + k, s], start=(k == 0), stop=(k == 1))
                last.then_inc(s_sc, 1)
            for c in range(TT):
                for hb, h in enumerate(heads):
                    pe.wait_ge(s_sT, hb + 1)
                    if c:
                        pe.wait_ge(s_q, hb + 1)
                        pe.wait_ge(s_cs, 2 * (c - 1) + hb + 1)
                        pe.wait_ge(s_y, 2 * (c - 1) + hb + 1)
                    o = PS[:, 2 + hb, 0:VA]
                    last = nc.tensor.matmul(o, sT[:, hb, c, :], v_aug[:, c, h, :], start=True, stop=(c == 0))
                    if c:
                        for k in range(2):
                            last = nc.tensor.matmul(o, mq[:, 2 * h + k, c * P:(c + 1) * P], cst[:, hb, k, :], start=False, stop=(k == 1))
                    last.then_inc(s_num, 1)
                if c < TT - 1:
                    for hb, h in enumerate(heads):
                        for k in range(2):
                            last = nc.tensor.matmul(PS[:, 4 + 2 * hb + k, 0:VA], kw[:, c, h * DM + k * P:h * DM + (k + 1) * P],
                                                    v_aug[:, c, h, :], start=True, stop=True)
                        last.then_inc(s_cu, 1)

        def act_part(act, st):
            for hb, h in enumerate(heads):
                for c in range(1, TT):
                    i = nc.scalar.activation(abc[:, hb, c - 1, :], Rb[:, h, c * P:(c + 1) * P], ACT.Exp, scale=-1.0, bias=rlast[:, c - 1, h:h + 1])
                i.then_inc(s_ex, 1)
                act.wait_ge(s_wi, hb + 1)
                nc.scalar.activation(flat(sT, hb), flat(sT, hb), ACT.Exp, scale=-1.0).then_inc(s_ex, 1)

        def dve_part(dve, st):
            V = nc.vector
            for hb, h in enumerate(heads):
                for i in range(TT):
                    last = V.tensor_scalar(sT[:, hb, i, :], Rb[:, h, i * P:(i + 1) * P], ucol[:, i, h:h + 1], 0.0, ALU.subtract, ALU.max)
                last.then_inc(s_wi, 1)
            for hb, h in enumerate(heads):
                dve.wait_ge(s_ex, 2 * hb + 2)
                st.then(V.tensor_tensor(sT[:, hb, :, :], sT[:, hb, :, :], middle(const["le"], TT), ALU.mult))
                dve.wait_ge(s_sc, hb + 1)
                V.scalar_tensor_tensor(flat(sT, hb), PS[:, hb, :], SC, flat(sT, hb), ALU.mult, ALU.mult).then_inc(s_sT, 1)
                a = abc[:, hb, :, :].rearrange("p c n -> p (c n)")
                V.scalar_tensor_tensor(mq[:, 2 * h:2 * h + 2, P:T], mq[:, 2 * h:2 * h + 2, P:T], SC, middle(a, 2),
                                       ALU.mult, ALU.mult).then_inc(s_q, 1)
            for c in range(TT):
                if c < TT - 1:
                    for hb, h in enumerate(heads):
                        dve.wait_ge(s_cu, 2 * c + hb + 1)
                        if c:
                            dve.wait_ge(s_num, 2 * c + hb + 1)
                        for k in range(2):
                            ps = PS[:, 4 + 2 * hb + k, 0:VA]
                            if c:
                                i = V.scalar_tensor_tensor(cst[:, hb, k, :], cst[:, hb, k, :], abc[:, hb, c - 1, P - 1:P], ps, ALU.mult, ALU.add)
                            else:
                                i = V.tensor_copy(cst[:, hb, k, :], ps)
                        i.then_inc(s_cs, 1)
                for hb, h in enumerate(heads):
                    dve.wait_ge(s_num, 2 * c + hb + 1)
                    d = den_s[:, hb:hb + 1]
                    st.then(V.tensor_scalar(d, PS[:, 2 + hb, DM:VA], emcol[:, c, h:h + 1], None, ALU.max))
                    st.then(V.scalar_tensor_tensor(d, PS[:, 2 + hb, DM:VA], -1.0, d, ALU.mult, ALU.max))
                    st.then(V.reciprocal(d, d))
                    s = slice(h * DM, (h + 1) * DM)
                    V.scalar_tensor_tensor(y_tok[:, c, s], PS[:, 2 + hb, 0:DM], d, so[:, c, s], ALU.mult, ALU.mult).then_inc(s_y, 1)
        add_stage(pe=pe_part, act=act_part, dve=dve_part)
    ml_pair(0)
    ml_pair(1)

    y_hi = at("y_hi", o_b, [P, KT, T], F32R)
    y_lo = at("y_lo", o_b + 16 * KB, [P, KT, T], F32R)
    merged = at("merged", o_m, [P, KT, T])
    sig_w = at("sig_w", o_w, [P, KT, T])
    sq_y = at("sq_y", o_b, [P, TT * D])
    yh = y_tok[:, :, :].rearrange("p t (h e) -> p (t h) e", e=DM)
    with together():
        normalise("ny", yh, yh, stat_y[:, 0, :], stat_y[:, 1, :], DM, sq_y[:, :])
        normalise("h2bn", x[:, :, :], xn3[:, :, :], stat3[:, 0, :], stat3[:, 1, :], D, sq3[:, :])
    transposes("ty", lambda tt, c: y_tok[:, tt, c * P:(c + 1) * P], lambda c: col("ml", c), dst_hi=y_hi, dst_lo=y_lo)
    transposes("h2bt", lambda tt, c: xn3[:, tt, c * P:(c + 1) * P], lambda c: col("mix2", c))

    def sigmoid_to(dst):
        return lambda eng, st, j, ps: nc.scalar.activation(dst[:, 2 * j:2 * j + 2, :], ps, ACT.Sigmoid)

    def merge_with(sig, first, split=False):
        def out_fn(dve, st, j, ps):
            s = slice(2 * j, 2 * j + 2)
            if first:
                return nc.vector.tensor_tensor(merged[:, s, :], sig[:, s, :], ps, ALU.mult)
            st.then(nc.vector.tensor_tensor(sig[:, s, :], sig[:, s, :], ps, ALU.mult))
            total = nc.vector.tensor_tensor(merged[:, s, :], merged[:, s, :], sig[:, s, :], ALU.add)
            if not split:
                return total
            st.then(total)
            st.then(nc.vector.tensor_copy(act_hi[:, s, :], merged[:, s, :]))
            return nc.vector.tensor_tensor(act_lo[:, s, :], merged[:, s, :], act_hi[:, s, :].bitcast(F32), ALU.subtract)
        return out_fn

    sc_c = at("sc_c", o_w, [P, KT, T])
    sc_z = at("sc_z", o_w + 16 * KB, [P, KT, T + 2])
    sig_sc = at("sig_sc", o_w + 16 * KB, [P, KT, T])
    bqT = at("bqT", o_w, [P, KT, T])
    bkT = at("bkT", o_w + 16 * KB, [P, KT, T])
    bv_tok = at("bv_tok", o_b, [P, TT, D])
    sig_b = at("sig_b", o_b + 16 * KB, [P, KT, T])

    def branches():
        s_pad = local("br_pad")
        parts_of = []

        def part(w, c0, n, mode, by, fn, hi=act_hi, lo=act_lo):
            parts_of.extend((src, mode, by, hi, lo, fn, j) for j, src in enumerate(slabs(w, c0, n)))

        def two(j):
            return slice(2 * j, 2 * j + 2)

        def scb_out(dve, st, j, ps):
            V = nc.vector
            tiles = (2 * j, 2 * j + 1)
            if j == 0:
                dve.wait_ge(s_pad, 1)
            for c in tiles:
                st(V.tensor_scalar(sc_c[:, c, :], sc_z[:, c, 0:T], col("conv2", 3 * c), None, ALU.mult))
            for w in (1, 2):
                for c in tiles:
                    st.wait(st.n - 1)
                    st(V.scalar_tensor_tensor(sc_c[:, c, :], sc_z[:, c, w:w + T], col("conv2", 3 * c + w), sc_c[:, c, :], ALU.mult, ALU.add))
            st.wait()
            st.then(V.tensor_tensor(sc_c[:, two(j), :], sc_c[:, two(j), :], ps, ALU.mult))
            st.then(V.tensor_copy(y_hi[:, two(j), :], sc_c[:, two(j), :]))
            return V.tensor_tensor(y_lo[:, two(j), :], sc_c[:, two(j), :], y_hi[:, two(j), :].bitcast(F32), ALU.subtract)

        def copy_to(dst, scale=1.0):
            return lambda eng, st, j, ps: nc.scalar.activation(dst[:, two(j), :], ps, ACT.Copy, scale=scale)
        part(w_in2, C_GML, 4, "feature", "act", sigmoid_to(sig_w))
        part(w_ml, 0, 4, "feature", "dve", merge_with(sig_w, True), y_hi, y_lo)
        part(w_in2, C_SCC, 4, "feature", "act", copy_to(sc_c))
        part(w_in2, C_SCU, 4, "feature", "dve",
             lambda eng, st, j, ps: nc.vector.tensor_tensor(sc_z[:, two(j), 2:2 + T], sc_c[:, two(j), :], ps, ALU.mult))
        part(w_in2, C_SCB, 4, "feature", "dve", scb_out)
        part(w_in2, C_GSC, 4, "feature", "act", sigmoid_to(sig_sc))
        part(w_sc, 0, 4, "feature", "dve", merge_with(sig_sc, False), y_hi, y_lo)
        part(w_in2, C_SBQ, 4, "feature", "act", copy_to(bqT, DS ** -0.5))
        part(w_in2, C_SBK, 4, "feature", "act", copy_to(bkT))
        part(w_in2, C_SBV, 4, "token", "act",
             lambda eng, st, j, ps: nc.scalar.activation(bv_tok[:, :, j * UC:(j + 1) * UC], ps, ACT.Copy))
        part(w_in2, C_GSB, 4, "feature", "act", sigmoid_to(sig_b))
        sources, modes, bys, his, los, fns, js = (list(v) for v in zip(*parts_of))
        dense("branches", sources, modes, lambda eng, st, j, ps: fns[j](eng, st, js[j], ps), bys, his, los,
              pool_part=lambda pool, st: nc.gpsimd.memset(sc_z[:, :, 0:2], 0.0).then_inc(s_pad, 1))
    branches()
    by_tok = at("by_tok", o_a, [P, TT, D])
    NZ = 1280
    zs = at("zs", o_a + 16 * KB, [P, 3, NZ])
    zl = at("zl", o_w + 32 * KB, [P, 2, NZ])
    OFF = {0: 512, 1: 1024, 2: 896}

    def later(j):
        return slice(OFF[j], OFF[j] + T - (j + 1) * P)

    def block_of(j, tt):
        a = j * P if tt == j else OFF[j] + (tt - j - 1) * P
        return slice(a, a + P)

    def stick():
        s_z, s_zc, s_zd, s_ab, s_e, s_ln, s_sp, s_suf, s_arg, s_A, s_av, s_y = (
            local("sb_" + n) for n in ("z", "zc", "zd", "ab", "e", "ln", "sp", "suf", "arg", "A", "av", "y"))
        zps = PS[:, 0:3, :].rearrange("p b n -> p (b n)")
        sps = PS[:, 3:6, :].rearrange("p b n -> p (b n)")

        def z_of(h):
            return zs[:, h % 3, :]

        def l_of(h):
            return zl[:, h % 2, :]

        def pe_part(pe):
            def scores(h):
                if h:
                    pe.wait_ge(s_zc, h)
                    pe.wait_ge(s_zd, h)
                r = slice((h % 2) * DS, (h % 2) * DS + DS)
                for j in range(TT):
                    k = bkT[r, h // 2, j * P:(j + 1) * P]
                    last = nc.tensor.matmul(zps[:, block_of(j, j)], k, bqT[r, h // 2, j * P:(j + 1) * P], start=True, stop=True)
                    if j < TT - 1:
                        last = nc.tensor.matmul(zps[:, later(j)], k, bqT[r, h // 2, (j + 1) * P:T], start=True, stop=True)
                last.then_inc(s_z, 1)

            def sums(h):
                pe.wait_ge(s_sp, h + 1)
                if h:
                    pe.wait_ge(s_arg, h)
                for i in range(TT):
                    for j in range(i, TT):
                        tri = const["ge"] if j == i else ones
                        last = nc.tensor.matmul(sps[:, block_of(i, j)], tri, l_of(h)[:, block_of(j, j)], start=(j == i), stop=(j in (i, TT - 1)))
                        if j < TT - 1:
                            a = block_of(i, j + 1).start
                            last = nc.tensor.matmul(sps[:, a:a + T - (j + 1) * P], tri, l_of(h)[:, later(j)], start=(j == i), stop=False)
                last.then_inc(s_suf, 1)

            def values(h):
                pe.wait_ge(s_A, h + 1)
                if h >= 2:
                    pe.wait_ge(s_y, h - 1)
                for tt in range(TT):
                    for j in range(tt + 1):
                        last = nc.tensor.matmul(PS[:, 6 + h % 2, tt * DS:(tt + 1) * DS], z_of(h)[:, block_of(j, tt)],
                                                bv_tok[:, j, h * DS:(h + 1) * DS], start=(j == 0), stop=(j == tt))
                last.then_inc(s_av, 1)
            scores(0)
            scores(1)
            for h in range(HS):
                sums(h)
                if h:
                    values(h - 1)
                if h + 2 < HS:
                    scores(h + 2)
            values(HS - 1)

        def act_part(act, st):
            def copy(h):
                act.wait_ge(s_z, h + 1)
                if h >= 3:
                    act.wait_ge(s_av, h - 2)
                nc.scalar.activation(z_of(h)[:, T:NZ], zps[:, T:NZ], ACT.Copy).then_inc(s_zc, 1)

            def logs(h):
                act.wait_ge(s_ab, h + 1)
                nc.scalar.activation(l_of(h), l_of(h), ACT.Exp, scale=-1.0).then_inc(s_e, 1)
                act.wait_ge(s_e, h + 1)
                nc.scalar.activation(l_of(h), l_of(h), ACT.Ln, bias=1.0).then_inc(s_ln, 1)

            def weights(h):
                act.wait_ge(s_arg, h + 1)
                nc.scalar.activation(z_of(h), z_of(h), ACT.Exp).then_inc(s_A, 1)

            def out_y(h):
                act.wait_ge(s_av, h + 1)
                nc.scalar.activation(by_tok[:, :, h * DS:(h + 1) * DS], PS[:, 6 + h % 2, 0:TT * DS].rearrange("p (t e) -> p t e", e=DS),
                                     ACT.Copy).then_inc(s_y, 1)
            nc.scalar.preload_act_table_set("natural_log_exp_and_others")
            copy(0)
            logs(0)
            for h in range(HS):
                if h + 1 < HS:
                    copy(h + 1)
                if h:
                    weights(h - 1)
                if h + 1 < HS:
                    logs(h + 1)
                if h >= 2:
                    out_y(h - 2)
            weights(HS - 1)
            out_y(HS - 2)
            out_y(HS - 1)

        def dve_part(dve, st):
            V = nc.vector

            def mask_and_abs(h):
                dve.wait_ge(s_z, h + 1)
                if h >= 3:
                    dve.wait_ge(s_av, h - 2)
                V.scalar_tensor_tensor(z_of(h)[:, 0:T].rearrange("p (a b) -> p a b", b=P), middle(const["ge"], TT), -1e5,
                                       zps[:, 0:T].rearrange("p (a b) -> p a b", b=P), ALU.mult, ALU.add).then_inc(s_zd, 1)
                dve.wait_ge(s_zc, h + 1)
                dve.wait_ge(s_zd, h + 1)
                if h >= 2:
                    dve.wait_ge(s_suf, h - 1)
                V.scalar_tensor_tensor(l_of(h), z_of(h), -1.0, z_of(h), ALU.mult, ALU.max).then_inc(s_ab, 1)

            def softplus(h):
                dve.wait_ge(s_ln, h + 1)
                V.scalar_tensor_tensor(l_of(h), z_of(h), 0.0, l_of(h), ALU.max, ALU.add).then_inc(s_sp, 1)

            def arg(h):
                dve.wait_ge(s_suf, h + 1)
                V.tensor_tensor(z_of(h), z_of(h), sps[:, 0:NZ], ALU.subtract).then_inc(s_arg, 1)
            mask_and_abs(0)
            softplus(0)
            for h in range(HS):
                if h:
                    arg(h - 1)
                if h + 1 < HS:
                    mask_and_abs(h + 1)
                    softplus(h + 1)
            arg(HS - 1)
        add_stage(pe=pe_part, act=act_part, dve=dve_part)
    stick()
    b_hi = at("b_hi", o_w, [P, KT, T], F32R)
    b_lo = at("b_lo", o_w + 16 * KB, [P, KT, T], F32R)
    transposes("tby", lambda tt, c: by_tok[:, tt, c * P:(c + 1) * P], None, dst_hi=b_hi, dst_lo=b_lo)
    dense("psb", slabs(w_sb, 0, 4), "feature", merge_with(sig_b, False, split=True), "dve", b_hi, b_lo)
    dense("wout2", slabs(w_out2, 0, 4), "token", residual_out, "dve")

    hidden("h3", "mlp2")

    def mlp():
        u0 = Stream.n
        NCH = DFF // D
        Stream.n += 8 * NCH
        s_relu, s_sq, s_bh, s_bl, s_add = (local("mlp_" + n) for n in ("relu", "sq", "bh", "bl", "add"))
        rl = at("rl", o_w, [P, 2, 2, T])
        sq = at("sq", o_w + 8 * KB, [P, 2, 2, T])

        def each(eng, body):
            body(0)
            with eng.Fori(1, NCH - 1) as c:
                body(c)
            body(NCH - 1)

        def num(c, j):
            s = u0 + j
            if isinstance(c, int):
                s += 8 * c
                return s, s, s // RAW + 1
            return s, c * 8 + s, c * 2 + s // RAW + 1

        def sp_part(sp):
            def body(c):
                for j in range(8):
                    s, u, _ = num(c, j)
                    if j < 4:
                        src = w_up2[:, bass.ds(c * D + j * UC, UC)].rearrange("(c p) n -> p c n", p=P)
                    else:
                        src = w_down2[bass.ds(c * D, D), (j - 4) * UC:(j - 3) * UC].rearrange("(c p) n -> p c n", p=P)
                    load_unit(sp, s, u, ("p (c n) -> p c n", dict(c=KT)), src)
            each(sp, body)

        def pe_part(pe):
            def body(c):
                for j in range(8):
                    s, u, _ = num(c, j)
                    pe.wait_ge(lo_ready, u + 1)
                    if j >= 6:
                        pe.wait_ge(s_add, c * 4 + (j - 5))
                    elif j >= 2:
                        pe.wait_ge(s_relu, c * 4 + (j - 1))
                    elif not isinstance(c, int) or c:
                        pe.wait_ge(s_add, c * 4 + (j - 1))
                    h = whi[:, s % SPLIT, :].rearrange("p (c n) -> p c n", c=KT)
                    l = wlo[:, s % SPLIT, :].rearrange("p (c n) -> p c n", c=KT)
                    b = PS[:, 2 * (j % 2):2 * (j % 2) + 2, :]
                    bt = b.rearrange("p b (t c) -> p (b t) c", c=UC)
                    for m in range(2 if j < 4 else TT):
                        f = slice(m * P, m * P + P)
                        for k in range(KT):
                            if j == 4 and m == 0 and k % 2 == 0:
                                pe.wait_ge(s_bl, c * 4 + (k // 2 + 1))
                            if j < 4:
                                three = ((h[:, k, f], act_hi[:, k, :]), (h[:, k, f], act_lo[:, k, :]), (l[:, k, f], act_hi[:, k, :]))
                            else:
                                three = ((y_hi[:, k, f], h[:, k, :]), (y_hi[:, k, f], l[:, k, :]), (y_lo[:, k, f], h[:, k, :]))
                            for n, (a_, b_) in enumerate(three):
                                i = nc.tensor.matmul((b if j < 4 else bt)[:, m, :], a_, b_, start=(k == 0 and n == 0), stop=(k == KT - 1 and n == 2))
                    i.then_inc(pe_unit, 1)
            each(pe, body)

        def ahead(c, j):
            s, u, _ = num(c, j)
            if isinstance(c, int):
                return s + 2, u + 2, (s + 2) // RAW + 1
            return s + 2, u + 2, c * 2 + (s + 2) // RAW + 1

        def act_part(act, st):
            def body(c):
                for j in range(8):
                    s, u, _ = num(c, j)
                    b = PS[:, 2 * (j % 2):2 * (j % 2) + 2, :]
                    if j < 4:
                        act.wait_ge(pe_unit, u + 1)
                        if not isinstance(c, int) or c or j >= 2:
                            act.wait_ge(s_bl, c * 4 + (j - 1))
                        nc.scalar.activation(rl[:, j % 2, :, :], b, ACT.Relu).then_inc(s_relu, 1)
                    if j < 4:
                        act.wait_ge(s_relu, c * 4 + (j + 1))
                        nc.scalar.activation(y_hi[:, 2 * j:2 * j + 2, :], rl[:, j % 2, :, :], ACT.Square).then_inc(s_bh, 1)
                    split_hi(act, *ahead(c, j))
            each(act, body)

        def dve_part(dve, st):
            def body(c):
                for j in range(8):
                    s, u, _ = num(c, j)
                    if j < 4:
                        dve.wait_ge(s_relu, c * 4 + (j + 1))
                        nc.vector.tensor_tensor(sq[:, j % 2, :, :], rl[:, j % 2, :, :], rl[:, j % 2, :, :], ALU.mult).then_inc(s_sq, 1)
                    else:
                        dve.wait_ge(pe_unit, u + 1)
                        f = slice((j - 4) * UC, (j - 3) * UC)
                        ps = PS[:, 2 * (j % 2):2 * (j % 2) + 2, :].rearrange("p b (t c) -> p (b t) c", c=UC)
                        if not isinstance(c, int) or c:
                            dve.wait_ge(s_add, c * 4 + (j - 7))
                        nc.vector.tensor_tensor(x[:, :, f], x[:, :, f], ps, ALU.add).then_inc(s_add, 1)
                    if j < 4:
                        dve.wait_ge(s_sq, c * 4 + (j + 1))
                        dve.wait_ge(s_bh, c * 4 + (j + 1))
                        nc.vector.tensor_tensor(y_lo[:, 2 * j:2 * j + 2, :], sq[:, j % 2, :, :], y_hi[:, 2 * j:2 * j + 2, :].bitcast(F32),
                                                ALU.subtract).then_inc(s_bl, 1)
                    split_lo(dve, *ahead(c, j)[:2])
            each(dve, body)
        add_stage(sp=sp_part, pe=pe_part, act=act_part, dve=dve_part)
    mlp()
    TOTAL["n"] = Stream.n

    gfin = at("gfin", o_b, [P, D])
    s_gf = sem("gfin")
    normalise("nf", x[:, :, :], xn3[:, :, :], stat3[:, 0, :], stat3[:, 1, :], D, sq3[:, :])
    add_stage(pool=lambda pool, st: pool.dma_start(gfin[:, :], gfin_in).then_inc(s_gf, 16))
    s_fin = sem("fin")
    out_v = out.rearrange("o (t p) d -> p (o t) d", p=P)

    def final_dve(dve, st):
        dve.wait_ge(s_gf, 16)
        for tt in range(TT):
            nc.vector.tensor_tensor(xn3[:, tt, :], xn3[:, tt, :], gfin[:, :], ALU.mult).then_inc(s_fin, 1)

    def final_sp(sp):
        for tt in range(TT):
            sp.wait_ge(s_fin, tt + 1)
            sp.dma_start(out_v[:, tt, :], xn3[:, tt, :]).then_inc(s_out, 16)
        sp.wait_ge(s_out, 16 * TT)
    add_stage(dve=final_dve, sp=final_sp)
    return_stages = stages if upto is None else stages[:upto]

    def close(eng, name, k):
        eng.drain().then_inc(done[name], 1)
        for other in done:
            if other != name:
                eng.wait_ge(done[other], k + 1)

    with nc.Block() as block:
        @block.sync
        def _(sp):
            for stage in return_stages:
                if "sp" in stage:
                    stage["sp"](sp)

        @block.tensor
        def _(pe):
            for k, stage in enumerate(return_stages):
                if "pe" in stage:
                    stage["pe"](pe)
                close(pe, "pe", k)

        @block.scalar
        def _(act):
            st = Steps(act, "act")
            for k, stage in enumerate(return_stages):
                if "act" in stage:
                    stage["act"](act, st)
                close(act, "act", k)

        @block.vector
        def _(dve):
            st = Steps(dve, "dve")
            for k, stage in enumerate(return_stages):
                if "dve" in stage:
                    stage["dve"](dve, st)
                close(dve, "dve", k)

        @block.gpsimd
        def _(pool):
            st = Steps(pool, "pool")
            for k, stage in enumerate(return_stages):
                if used.get(k - 1):
                    b = banks[(k - 1) % 3]
                    nc.gpsimd.sem_clear(range(b[0], b[0] + used[k - 1]))
                if "pool" in stage:
                    stage["pool"](pool, st)
                close(pool, "pool", k)
    return stages


def lay_out(a):
    f = np.float32

    def by_partition(v, n):
        return np.asarray(v, f).reshape(n, P).T

    def by_rows(w):
        return w.reshape(KT, P, -1).transpose(1, 0, 2).copy()

    c = np.zeros((P, NCOLS), f)

    def put(name, block):
        c[:, COLS[name]:COLS[name] + block.shape[1]] = block
    put("ln1", by_partition(a["ln1_g"][0], KT))
    put("qg", np.concatenate([a["attn_q_norm_g"][0]] * 2)[:, None])
    put("kg", np.concatenate([a["attn_k_norm_g"][0]] * 2)[:, None])
    put("attn_out", by_partition(a["attn_out_norm_g"][0], 4))
    put("dn_out", np.asarray(a["dn_out_norm_g"][0])[:, None])
    put("ln2", by_partition(a["ln2_g"][0], KT))
    put("ln2_i", np.asarray(a["ln2_g"][0]).reshape(P, KT))
    put("mix2", by_partition(a["norm_mix_g_2"][0], KT))
    put("ml", by_partition(a["ml_norm_g_2"][0], KT))
    put("mlp2", by_partition(a["norm_mlp_g_2"][0], KT))
    put("conv", np.asarray(a["dn_conv_w"][0]).reshape(CONV, 12, P).transpose(2, 1, 0).reshape(P, 12 * CONV))
    put("conv2", np.asarray(a["conv_w_2"][0]).reshape(3, KT, P).transpose(2, 1, 0).reshape(P, 3 * KT))
    r = np.concatenate([np.asarray(a["dn_a_log"]).reshape(-1), np.asarray(a["dn_dt_bias"]).reshape(-1),
                        np.asarray(a["router_group_b"]).reshape(-1), np.asarray(a["router_expert_b"]).reshape(-1),
                        np.asarray(a["b_if_2"]).reshape(-1)]).astype(f)
    rpb = np.asarray(a["attn_rpb"][0])
    r2, qc = np.divmod(np.arange(P), GW)
    kk, kc = np.arange(KROWS), np.arange(GW)
    first = np.clip(qc - WIN // 2, 0, GW - WIN)
    inside = (kc[None] >= first[:, None]) & (kc[None] < first[:, None] + WIN)
    ro = kk[None] + 1 - r2[:, None]
    co = np.clip(kc[None] - qc[:, None] + WIN - 1, 0, 2 * WIN - 2)
    table = rpb[:, ro[:, :, None], co[:, None, :]].transpose(1, 0, 2, 3)
    bias = np.where(inside[:, None, None, :], table, f(-BIG)).astype(f)
    w_in, w_in2 = np.asarray(a["w_in"][0]), np.asarray(a["w_in_2"][0])
    g0 = 4 * D
    return {
        "x": np.asarray(a["x"]), "cols": c, "rows": np.broadcast_to(r, (P, NROWS)).copy(), "consts": constant_matrices(),
        "bias": bias, "w_in": w_in, "w_ab": by_rows(w_in[:, -16:]), "w_out": np.asarray(a["w_out"][0]),
        "w_router": by_rows(np.concatenate([np.asarray(a["router_group_w"][0]), np.asarray(a["router_expert_w"][0])], axis=1)),
        "w_gate": np.asarray(a["expert_w_gate"][0]), "w_up": np.asarray(a["expert_w_up"][0]), "w_down": np.asarray(a["expert_w_down"][0]),
        "w_in2": w_in2, "w_gates2": by_rows(w_in2[:, g0:g0 + 2 * HM]),
        "w_ml": np.asarray(a["w_ml_proj_2"][0]), "w_sc": np.asarray(a["w_sc_proj_2"][0]), "w_sb": np.asarray(a["w_sb_proj_2"][0]),
        "w_out2": np.asarray(a["w_out_2"][0]), "w_up2": np.asarray(a["w_up_2"][0]), "w_down2": np.asarray(a["w_down_2"][0]),
        "gfin": np.broadcast_to(np.asarray(a["norm_final_g_2"]), (P, D)).copy(),
    }


def kernel(**inputs):
    import concourse.bacc as bacc
    from concourse.bass_utils import run_bass_kernel_spmd

    arrays = lay_out(inputs)
    nc = bacc.Bacc("TRN2", target_bir_lowering=False, num_devices=1)
    args = [nc.dram_tensor(f"in_{n}", v.shape, F32, kind="ExternalInput").ap() for n, v in arrays.items()]
    args.append(nc.dram_tensor("out_y", (1, T, D), F32, kind="ExternalOutput").ap())
    build(nc, *args)
    r = run_bass_kernel_spmd(nc, [{f"in_{n}": np.ascontiguousarray(v) for n, v in arrays.items()}], core_ids=[0])
    return np.asarray(r.results[0]["out_y"])
```
